# Optimizing a Trainium2 kernel written in Bass

```python
import math
import jax, jax.numpy as jnp
from jax import lax
import numpy as np

D_MODEL = 1024
BATCH = 1
SEQ = 1024
DEPTH = 2

BLOCK = 128
ROPE_THETA = 500000.0
ROPE_FRACTION = 4
EPS = 1e-6
CONV_CH = 512
CONV_K = 3
DIFF_HEADS = 4
DIFF_DK = 64
DIFF_DV = 128
SWA_Q_HEADS = 16
SWA_KV_HEADS = 4
SWA_HEAD_DIM = 64
SWA_WINDOW = 128
MEM_LEN = 256
XATTN_HEADS = 4
XATTN_HEAD_DIM = 128
N_GROUPS = 4
EXPERTS_PER_GROUP = 8
N_EXPERTS = N_GROUPS * EXPERTS_PER_GROUP
TOP_K = 2
EXPERT_HIDDEN = 512

A_IN = 3 * CONV_CH
DIFF_QK = DIFF_HEADS * 2 * DIFF_DK
B_IN = 2 * DIFF_QK + DIFF_HEADS * DIFF_DV
HYB_IN = A_IN + B_IN
HYB_OUT = CONV_CH + DIFF_HEADS * DIFF_DV
SWA_QW = SWA_Q_HEADS * SWA_HEAD_DIM
SWA_KVW = SWA_KV_HEADS * SWA_HEAD_DIM
SWA_IN = SWA_QW + 2 * SWA_KVW
XATTN_W = XATTN_HEADS * XATTN_HEAD_DIM

kernel_name = "hybrid_conv_diffattn_swa_sink_xmem_hmoe"

def rmsnorm(x, g):
    xf = x.astype(jnp.float32)
    y = xf * lax.rsqrt(jnp.mean(xf * xf, axis=-1, keepdims=True) + EPS)
    return (y * g.astype(jnp.float32)).astype(x.dtype)

def rotary_tables(seq, head_dim):
    rot = head_dim // ROPE_FRACTION
    pos = jnp.arange(seq, dtype=jnp.float32)
    inv = ROPE_THETA ** (-jnp.arange(0, rot, 2, dtype=jnp.float32) / rot)
    ang = pos[:, None] * inv[None, :]
    return jnp.cos(ang), jnp.sin(ang)

def rope_partial(x, cos, sin):
    half = cos.shape[-1]
    extra = x.ndim - 3
    c = cos.reshape((cos.shape[0],) + (1,) * extra + (half,)).astype(x.dtype)
    s = sin.reshape((sin.shape[0],) + (1,) * extra + (half,)).astype(x.dtype)
    x1, x2, rest = x[..., :half], x[..., half:2 * half], x[..., 2 * half:]
    return jnp.concatenate([x1 * c - x2 * s, x2 * c + x1 * s, rest], axis=-1)

def short_conv(u, w):
    C = u.shape[-1]
    return lax.conv_general_dilated(
        u, w.astype(u.dtype)[:, None, :], window_strides=(1,), padding=[(CONV_K - 1, 0)],
        dimension_numbers=('NWC', 'WIO', 'NWC'), feature_group_count=C)

def diff_attention(q, k, v, lam):
    B, S, H, _, D = q.shape
    nb = S // BLOCK
    scale = D ** -0.5
    qb = q.reshape(B, nb, BLOCK, H, 2, D).swapaxes(0, 1)
    kpos = jnp.arange(S)

    def block(args):
        qblk, n = args
        qpos = n * BLOCK + jnp.arange(BLOCK)
        s = jnp.einsum('bqhmd,bkhmd->bhmqk', qblk, k).astype(jnp.float32) * scale
        s = jnp.where(kpos[None, :] <= qpos[:, None], s, -jnp.inf)
        p = jax.nn.softmax(s, axis=-1)
        a = p[:, :, 0] - lam * p[:, :, 1]
        return jnp.einsum('bhqk,bkhe->bqhe', a.astype(v.dtype), v)

    o = lax.map(block, (qb, jnp.arange(nb)))
    return o.swapaxes(0, 1).reshape(B, S, H, v.shape[-1])

def hybrid_mixer(h, w_in, conv_w, lam_vecs, subln_g, w_out, lambda_init, cos, sin):
    B, S, _ = h.shape
    p = h @ w_in
    a_in, b_in = p[..., :A_IN], p[..., A_IN:]
    gate_b, gate_c, u = jnp.split(a_in, 3, axis=-1)
    y_a = gate_b * short_conv(gate_c * u, conv_w)
    q = b_in[..., :DIFF_QK].reshape(B, S, DIFF_HEADS, 2, DIFF_DK)
    k = b_in[..., DIFF_QK:2 * DIFF_QK].reshape(B, S, DIFF_HEADS, 2, DIFF_DK)
    v = b_in[..., 2 * DIFF_QK:].reshape(B, S, DIFF_HEADS, DIFF_DV)
    q = rope_partial(q, cos, sin)
    k = rope_partial(k, cos, sin)
    lf = lam_vecs.astype(jnp.float32)
    lam = jnp.exp(jnp.sum(lf[0] * lf[1])) - jnp.exp(jnp.sum(lf[2] * lf[3])) + lambda_init
    o = diff_attention(q, k, v, lam)
    o = rmsnorm(o, subln_g) * (1.0 - lambda_init)
    y_b = o.reshape(B, S, DIFF_HEADS * DIFF_DV)
    return jnp.concatenate([y_a, y_b], axis=-1) @ w_out

def swa_mixer(h, w_qkv, b_qkv, sinks, w_out, b_out, cos, sin):
    B, S, _ = h.shape
    G = SWA_Q_HEADS // SWA_KV_HEADS
    nb = S // BLOCK
    p = h @ w_qkv + b_qkv
    q = p[..., :SWA_QW].reshape(B, S, SWA_Q_HEADS, SWA_HEAD_DIM)
    k = p[..., SWA_QW:SWA_QW + SWA_KVW].reshape(B, S, SWA_KV_HEADS, SWA_HEAD_DIM)
    v = p[..., SWA_QW + SWA_KVW:].reshape(B, S, SWA_KV_HEADS, SWA_HEAD_DIM)
    q = rope_partial(q, cos, sin)
    k = rope_partial(k, cos, sin)
    qb = q.reshape(B, nb, BLOCK, SWA_KV_HEADS, G, SWA_HEAD_DIM)

    def band(t):
        tb = t.reshape(B, nb, BLOCK, SWA_KV_HEADS, SWA_HEAD_DIM)
        prev = jnp.concatenate([jnp.zeros_like(tb[:, :1]), tb[:, :-1]], axis=1)
        return jnp.concatenate([prev, tb], axis=2)

    kb, vb = band(k), band(v)
    s = jnp.einsum('bnqkgd,bnskd->bnkgqs', qb, kb).astype(jnp.float32) * (SWA_HEAD_DIM ** -0.5)
    qi = jnp.arange(BLOCK)[:, None]
    si = jnp.arange(2 * BLOCK)[None, :]
    rel = si - BLOCK - qi
    in_win = (rel <= 0) & (rel > -SWA_WINDOW)
    kabs = jnp.arange(nb)[:, None, None] * BLOCK + si[None] - BLOCK
    mask = in_win[None] & (kabs >= 0)
    s = jnp.where(mask[None, :, None, None], s, -jnp.inf)
    sink = jnp.broadcast_to(sinks.astype(jnp.float32).reshape(1, 1, SWA_KV_HEADS, G, 1, 1),
                            s.shape[:-1] + (1,))
    pr = jax.nn.softmax(jnp.concatenate([s, sink], axis=-1), axis=-1)[..., :-1]
    o = jnp.einsum('bnkgqs,bnskd->bnqkgd', pr.astype(vb.dtype), vb).reshape(B, S, SWA_QW)
    return o @ w_out + b_out

def cross_attention(h, mem_k, mem_v, w_q, w_o):
    B, S, _ = h.shape
    q = (h @ w_q).reshape(B, S, XATTN_HEADS, XATTN_HEAD_DIM)
    s = jnp.einsum('bshd,bmhd->bhsm', q, mem_k).astype(jnp.float32) * (XATTN_HEAD_DIM ** -0.5)
    p = jax.nn.softmax(s, axis=-1)
    o = jnp.einsum('bhsm,bmhd->bshd', p.astype(mem_v.dtype), mem_v).reshape(B, S, XATTN_W)
    return o @ w_o

def hier_moe(h, w_group, b_group, w_router, b_router, w_gate_up, w_down):
    B, S, D = h.shape
    t = h.reshape(-1, D)
    T = t.shape[0]
    p_group = jax.nn.softmax((t @ w_group + b_group).astype(jnp.float32), axis=-1)
    g_sel = jnp.argmax(p_group, axis=-1)
    p_g = jnp.take_along_axis(p_group, g_sel[:, None], axis=1)[:, 0]
    e_logits = (t @ w_router + b_router).astype(jnp.float32).reshape(T, N_GROUPS, EXPERTS_PER_GROUP)
    e_logits = jnp.take_along_axis(e_logits, g_sel[:, None, None], axis=1)[:, 0]
    top_w, top_i = lax.top_k(jax.nn.softmax(e_logits, axis=-1), TOP_K)
    top_w = top_w / jnp.sum(top_w, axis=-1, keepdims=True) * p_g[:, None]
    expert_id = (g_sel[:, None] * EXPERTS_PER_GROUP + top_i).reshape(-1)
    flat_w = top_w.reshape(-1)
    flat_tok = jnp.repeat(jnp.arange(T), TOP_K)
    order = jnp.argsort(expert_id)
    tok_sorted = flat_tok[order]
    xs = t[tok_sorted]
    group_sizes = jnp.bincount(expert_id, length=N_EXPERTS).astype(jnp.int32)
    gu = lax.ragged_dot(xs, w_gate_up, group_sizes)
    hid = jax.nn.silu(gu[:, :EXPERT_HIDDEN]) * gu[:, EXPERT_HIDDEN:]
    y = lax.ragged_dot(hid, w_down, group_sizes) * flat_w[order][:, None].astype(hid.dtype)
    out = jax.ops.segment_sum(y, tok_sorted, num_segments=T)
    return out.reshape(B, S, D)

def setup_inputs(seed: int = 0) -> dict:
    key = jax.random.key(seed)
    ks = iter(jax.random.split(key, 32))
    n_even = (DEPTH + 1) // 2
    n_odd = DEPTH // 2
    f32 = jnp.float32

    def nrm(shape, scale):
        return jax.random.normal(next(ks), shape, f32) * scale

    def gain(shape):
        return 1.0 + 0.05 * jax.random.normal(next(ks), shape, f32)

    D = D_MODEL
    return {
        "x": nrm((BATCH, SEQ, D), 1.0),
        "mem": nrm((BATCH, MEM_LEN, D), 1.0),
        "mem_norm": gain((D,)),
        "mem_w_kv": nrm((D, 2 * XATTN_W), D ** -0.5),
        "norm_mix": gain((DEPTH, D)),
        "norm_xattn": gain((DEPTH, D)),
        "norm_ffn": gain((DEPTH, D)),
        "hyb_w_in": nrm((n_even, D, HYB_IN), D ** -0.5),
        "hyb_conv_w": nrm((n_even, CONV_K, CONV_CH), CONV_K ** -0.5),
        "diff_lambda": nrm((n_even, 4, DIFF_DK), 0.1),
        "diff_subln": gain((n_even, DIFF_DV)),
        "hyb_w_out": nrm((n_even, HYB_OUT, D), HYB_OUT ** -0.5),
        "swa_w_qkv": nrm((n_odd, D, SWA_IN), D ** -0.5),
        "swa_b_qkv": nrm((n_odd, SWA_IN), 0.02),
        "swa_sinks": nrm((n_odd, SWA_Q_HEADS), 0.5),
        "swa_w_out": nrm((n_odd, SWA_QW, D), SWA_QW ** -0.5),
        "swa_b_out": nrm((n_odd, D), 0.02),
        "xattn_w_q": nrm((DEPTH, D, XATTN_W), D ** -0.5),
        "xattn_w_o": nrm((DEPTH, XATTN_W, D), XATTN_W ** -0.5),
        "moe_w_group": nrm((DEPTH, D, N_GROUPS), D ** -0.5),
        "moe_b_group": nrm((DEPTH, N_GROUPS), 0.01),
        "moe_w_router": nrm((DEPTH, D, N_EXPERTS), D ** -0.5),
        "moe_b_router": nrm((DEPTH, N_EXPERTS), 0.01),
        "moe_w_gate_up": nrm((DEPTH, N_EXPERTS, D, 2 * EXPERT_HIDDEN), D ** -0.5),
        "moe_w_down": nrm((DEPTH, N_EXPERTS, EXPERT_HIDDEN, D), EXPERT_HIDDEN ** -0.5),
        "final_norm": gain((D,)),
    }

def reference(x, mem, mem_norm, mem_w_kv, norm_mix, norm_xattn, norm_ffn,
              hyb_w_in, hyb_conv_w, diff_lambda, diff_subln, hyb_w_out,
              swa_w_qkv, swa_b_qkv, swa_sinks, swa_w_out, swa_b_out,
              xattn_w_q, xattn_w_o, moe_w_group, moe_b_group, moe_w_router, moe_b_router,
              moe_w_gate_up, moe_w_down, final_norm):
    B, S, _ = x.shape
    M = mem.shape[1]
    mkv = rmsnorm(mem, mem_norm) @ mem_w_kv
    mem_k = mkv[..., :XATTN_W].reshape(B, M, XATTN_HEADS, XATTN_HEAD_DIM)
    mem_v = mkv[..., XATTN_W:].reshape(B, M, XATTN_HEADS, XATTN_HEAD_DIM)
    cos_d, sin_d = rotary_tables(S, DIFF_DK)
    cos_s, sin_s = rotary_tables(S, SWA_HEAD_DIM)
    for l in range(DEPTH):
        h = rmsnorm(x, norm_mix[l])
        if l % 2 == 0:
            e = l // 2
            lambda_init = 0.8 - 0.6 * math.exp(-0.3 * l)
            x = x + hybrid_mixer(h, hyb_w_in[e], hyb_conv_w[e], diff_lambda[e], diff_subln[e],
                                 hyb_w_out[e], lambda_init, cos_d, sin_d)
        else:
            o = l // 2
            x = x + swa_mixer(h, swa_w_qkv[o], swa_b_qkv[o], swa_sinks[o], swa_w_out[o],
                              swa_b_out[o], cos_s, sin_s)
        x = x + cross_attention(rmsnorm(x, norm_xattn[l]), mem_k, mem_v, xattn_w_q[l], xattn_w_o[l])
        x = x + hier_moe(rmsnorm(x, norm_ffn[l]), moe_w_group[l], moe_b_group[l], moe_w_router[l],
                         moe_b_router[l], moe_w_gate_up[l], moe_w_down[l])
    return rmsnorm(x, final_norm)


_drawn_inputs = setup_inputs


def setup_inputs(seed=0):
    import zlib

    import numpy as np

    out = dict(_drawn_inputs(seed))
    spreads = {}
    factors = {'norm_xattn': 3.13, 'swa_sinks': 5.827, 'moe_b_group': 3.819, 'moe_b_router': 3.401}
    for name, (base, spread) in spreads.items():
        noise = np.random.default_rng([zlib.crc32(name.encode()), seed]).standard_normal(out[name].shape)
        drawn = base * np.exp(spread * noise) if base else spread * noise
        out[name] = __import__('jax').numpy.asarray(drawn.astype(out[name].dtype))
    for name, factor in factors.items():
        out[name] = (out[name] * factor).astype(out[name].dtype)
    return out
```

```python
import math
from contextlib import ExitStack

import concourse.bass as bass
from concourse import mybir

P = 128
ALU = mybir.AluOpType
ACT = mybir.ActivationFunctionType
F32 = mybir.dt.float32
BF16 = mybir.dt.bfloat16
U32 = mybir.dt.uint32
I32 = mybir.dt.int32
AX = mybir.AxisListType.X

D = 1024
S = 1024
KD = D // P
NB = S // P
MEM = 256
MB = MEM // P
CONV_CH, DIFF_HEADS = 512, 4
SWA_KV = 4
XH = 4
NG, EPG, NE = 4, 8, 32
EH = 512
EPS = 1e-6
NEG = -1.0e30
LAMBDA_INIT = 0.8 - 0.6 * math.exp(-0.3 * 0)

TS = 112
XT = 2 * S // TS
NT_MAX = NE + XT
NTT = NT_MAX + 2
JT = -(-S // TS) - 1

C_ID, C_R, C_TRI, C_CAUSAL, C_PREV, C_IOTA, C_TOK, C_ALL = 0, 128, 256, 384, 512, 640, 768, 776


def build(nc, x, mem, mem_norm, mem_w_kv, norm_mix, norm_xattn, norm_ffn, hyb_w_in, hyb_conv_w,
          diff_lambda, diff_subln, hyb_w_out, swa_w_qkv, swa_b_qkv, swa_sinks, swa_w_out, swa_b_out,
          xattn_w_q, xattn_w_o, moe_w_group, moe_b_group, moe_w_router, moe_b_router,
          moe_w_gate_up, moe_w_down, final_norm, rope_tables, constants, out):
    ctx = ExitStack()
    with ctx:
        def sb(name, shape, dt=F32):
            return ctx.enter_context(nc.sbuf_tensor(name, shape, dt))

        phase = []

        def sem(name, keep=False):
            s = nc.alloc_semaphore(name=name)
            if not keep:
                phase.append(s)
            return s

        def end_phase():
            nc.clear_and_free_semaphores(list(phase))
            phase.clear()
            nc.all_engine_barrier()

        xs = sb("xs", [P, NB, D])
        hT = sb("hT", [P, KD, S])
        yT = sb("yT", [P, KD, S])
        W = sb("W", [P, 14336])
        prob = sb("prob", [P, 2048])
        probT = sb("probT", [P, 1024])
        qk = sb("qk", [P, 3, S])
        raw = sb("raw", [P, S])
        tmp = sb("tmp", [P, S])
        val = sb("val", [P, 1024])
        rope = sb("rope", [P, 2, S])
        memK = sb("memK", [P, XH, MEM])
        memV = sb("memV", [P, MB, XH * P])
        ident = sb("ident", [P, P])
        rot = sb("rot", [P, P])
        iota = sb("iota", [P, P])
        tok_id = sb("tok_id", [P, NB])
        ident_b = sb("ident_b", [P, P], BF16)
        tri_b = sb("tri_b", [P, P], BF16)
        ones_b = sb("ones_b", [P, P], BF16)
        mask_b = sb("mask_b", [P, 2, P], BF16)
        gains = sb("gains", [P, 7, KD])
        conv_w = sb("conv_w", [P, 3, 4])
        subln = sb("subln", [P, 1])
        neg_lam = sb("neg_lam", [P, 1])
        lamv = sb("lamv", [P, 4])
        q_bias = sb("q_bias", [P, 8])
        k_bias = sb("k_bias", [P, SWA_KV])
        sinks = sb("sinks", [P, 2, 16])
        mhalf = sb("mhalf", [P, NB])
        ssum = sb("ssum", [P, NB])
        msq = sb("msq", [P, NB])
        rstd = sb("rstd", [P, NB])
        nmax = sb("nmax", [P, 2, 4])
        psum_ = sb("psum_", [P, 2, 4])
        rsum = sb("rsum", [P, 2, 4])
        ratio = sb("ratio", [P, 2])
        slots = raw[:, 0:NTT].bitcast(U32)
        pos_u = sb("pos_u", [P, 2, NB], U32)
        wgt = sb("wgt", [P, 2, NB])
        tile_e = raw[:, 128:128 + NTT].bitcast(I32)
        ntile = sb("ntile", [P, 1], I32)
        icol = sb("icol", [P, 1], U32)
        sinkx = sb("sinkx", [P, 2, 4])

        pairs = [ctx.enter_context(nc.psum_tensor(f"pair{i}", [P, 1024], F32)) for i in range(3)]
        A, B, C = (t[:, :] for t in pairs)
        pO = ctx.enter_context(nc.psum_tensor("pO", [P, 512], F32))
        pU = ctx.enter_context(nc.psum_tensor("pU", [P, 512], F32))

        h_dram = nc.dram_tensor("h_rows", [S, D], F32, kind="Internal").ap()
        y_dram = nc.dram_tensor("y_rows", [NT_MAX * TS, D], F32, kind="Internal").ap()

        slot = [W[:, 1024 * b:1024 * (b + 1)].rearrange("p (k n) -> p k n", k=KD) for b in range(6)]
        w_out = W[:, 6144:14336].rearrange("p (k n) -> p k n", k=KD)
        chunk = [W[:, 2048 * c:2048 * (c + 1)] for c in range(6)]
        yflat = yT[:, :, :].rearrange("p k n -> p (k n)")

        s_const = sem("const_loaded", keep=True)
        s_x = sem("x_loaded", keep=True)
        s_zero = sem("rows_cleared", keep=True)
        s_wo = [sem(f"out_weights_loaded{i}", keep=True) for i in range(4)]

        def setup():
            cast_done = sem("constants_cast")
            zeroed = sem("zero_rows_ready")
            zero_rows = yflat[:, 4096:5120]
            lam1, lam2, lam3, lam4 = (sem(f"lambda_step{i}") for i in range(4))
            lraw = raw[:, 0:512].rearrange("p (a b) -> p a b", a=4)
            with nc.Block() as block:
                @block.sync
                def _(sp):
                    small = [
                        (ident[:], constants[:, C_ID:C_ID + P]), (rot[:], constants[:, C_R:C_R + P]),
                        (iota[:], constants[:, C_IOTA:C_IOTA + P]),
                        (tok_id[:], constants[:, C_TOK:C_TOK + NB]),
                        (prob[:, 0:384], constants[:, C_TRI:C_TRI + 384]),
                        (rope[:, :, :], rope_tables),
                        (conv_w[:, :, :], hyb_conv_w[0].rearrange("j (b p) -> p j b", p=P)),
                        (subln[:, :], diff_subln.rearrange("a p -> p a")),
                        (raw[:, 0:256], diff_lambda[0].rearrange("a b -> (a b)").partition_broadcast(P)),
                        (q_bias[:, :], swa_b_qkv[0, 0:1024].rearrange("(b p) -> p b", p=P)),
                        (k_bias[0:64, :], swa_b_qkv[0, 1024:1280].rearrange("(b p) -> p b", p=64)),
                        (k_bias[64:128, :], swa_b_qkv[0, 1024:1280].rearrange("(b p) -> p b", p=64)),
                        (raw[:, 256:272], swa_sinks[0].partition_broadcast(P)),
                    ]
                    for i, g in enumerate([mem_norm, norm_mix[0], norm_xattn[0], norm_ffn[0],
                                           norm_mix[1], norm_xattn[1], norm_ffn[1]]):
                        small.append((gains[:, i, :], g.rearrange("(k p) -> p k", p=P)))
                    for dst, src in small:
                        sp.dma_start(dst, src, allow_slow_non_contiguous=True).then_inc(s_const, 16)
                    assert len(small) == 20
                    for c in range(NB):
                        sp.dma_start(xs[:, c, :], x[0, c * P:(c + 1) * P, :]).then_inc(s_x, 16)

                @block.vector
                def _(dve):
                    nc.vector.memset(zero_rows, 0.0).then_inc(zeroed, 1)
                    dve.wait_ge(s_const, 320)
                    nc.vector.tensor_copy(ident_b[:], ident[:])
                    nc.vector.tensor_copy(tri_b[:], prob[:, 0:128])
                    nc.vector.tensor_copy(mask_b[:, 1, :], prob[:, 128:256])
                    nc.vector.tensor_copy(mask_b[:, 0, :], prob[:, 256:384])
                    nc.vector.memset(ones_b[:], 1.0)
                    nc.vector.memset(mhalf[:], -0.5)
                    nc.vector.tensor_tensor(tmp[:, 0:64], raw[:, 0:64], raw[:, 64:128], ALU.mult)
                    nc.vector.tensor_tensor(tmp[:, 64:128], raw[:, 128:192], raw[:, 192:256],
                                            ALU.mult).then_inc(lam1, 1)
                    dve.wait_ge(lam1, 1)
                    nc.vector.tensor_reduce(lamv[:, 0:2], tmp[:, 0:128].rearrange("p (a b) -> p a b", a=2),
                                            AX, ALU.add).then_inc(lam2, 1)
                    dve.wait_ge(lam3, 1)
                    nc.vector.tensor_tensor(lamv[:, 0:1], lamv[:, 3:4], lamv[:, 2:3],
                                            ALU.subtract).then_inc(lam4, 1)
                    dve.wait_ge(lam4, 1)
                    nc.vector.tensor_scalar(neg_lam[:], lamv[:, 0:1], -LAMBDA_INIT, None, ALU.add)
                    nc.vector.tensor_scalar(subln[:], subln[:], 1.0 - LAMBDA_INIT, None, ALU.mult)
                    nc.vector.tensor_scalar(q_bias[:], q_bias[:], 0.125, None, ALU.mult)
                    for row, sign in ((0, 1.0), (1, -1.0)):
                        ins = nc.vector.tensor_scalar(
                            sinks[:, row, :].rearrange("p (g l i) -> p g l i", g=4, l=2),
                            raw[:, 256:272].rearrange("p (g i l) -> p g l i", g=4, l=2), sign, None, ALU.mult)
                    ins.then_inc(cast_done, 1)
                    dve.wait_ge(cast_done, 1)

                @block.scalar
                def _(act):
                    act.wait_ge(zeroed, 1)
                    for t in range(NE, NT_MAX):
                        act.dma_start(y_dram[t * TS:(t + 1) * TS, :], zero_rows[0:TS, :]).then_inc(s_zero, 16)
                    act.wait_ge(lam2, 1)
                    nc.scalar.activation(lamv[:, 2:4], lamv[:, 0:2], ACT.Exp).then_inc(lam3, 1)

        def stream(name, nblk, src, gain, feed, kin=0, w_ready=None, bias=None, dst=hT, rows=False,
                   final=False, preload=None):
            x_done = sem(name + "_x_done")
            ss_done = sem(name + "_sumsq_done")
            ms_done = sem(name + "_meansq_done")
            rs_done = sem(name + "_rstd_done")
            xn_done = sem(name + "_normed")
            tr_done = sem(name + "_transposed")
            ev_done = sem(name + "_evacuated")
            pr_done = sem(name + "_projected")
            ad_done = sem(name + "_added")
            st_done = [sem(name + f"_rows_stored{i}") for i in range(2)]
            ga_done = [[sem(name + f"_gathered{j}{i}") for i in range(2)] for j in range(2)]
            gfin = sem(name + "_gain_loaded")
            fin_done = sem(name + "_gained")
            xn = [prob[:, 0:1024], prob[:, 1024:2048]]
            got = [[yflat[:, 1024 * (2 * i + j):1024 * (2 * i + j + 1)] for j in range(2)] for i in range(2)]
            fin = [yflat[:, 4096:5120], yflat[:, 5120:6144]]
            gbc = val[:, :]
            bbc = val[:, :]
            with nc.Block() as block:
                @block.sync
                def _(sp):
                    if final:
                        sp.dma_start(gbc, final_norm.partition_broadcast(P)).then_inc(gfin, 16)
                    if bias is not None:
                        sp.dma_start(bbc, bias.partition_broadcast(P)).then_inc(gfin, 16)
                    if preload:
                        preload(sp)
                    if rows:
                        for c in range(nblk):
                            sp.wait_ge(xn_done, c + 1)
                            sp.dma_start(h_dram[c * P:(c + 1) * P, :], xn[c % 2]).then_inc(st_done[c % 2], 16)
                    if final:
                        for c in range(nblk):
                            sp.wait_ge(fin_done, c + 1)
                            sp.dma_start(out[0, c * P:(c + 1) * P, :], fin[c % 2]).then_inc(st_done[c % 2], 16)
                    if rows or final:
                        for i in range(2):
                            sp.wait_ge(st_done[i], 16 * (nblk // 2))

                @block.gpsimd
                def _(pool):
                    for c in range(nblk + 1):
                        if feed == "combine" and c < nblk:
                            if c >= 2:
                                pool.wait_ge(x_done, c - 1)
                            for j in range(2):
                                pool.indirect_dma_start(
                                    got[c % 2][j], None, y_dram,
                                    bass.IndirectOffsetOnAxis(ap=pos_u[:, j, c:c + 1], axis=0),
                                ).then_inc(ga_done[c % 2][j], 16)
                        if c >= 1:
                            pool.wait_ge(ms_done, c)
                            nc.gpsimd.tensor_tensor(rstd[:, c - 1:c], msq[:, c - 1:c], mhalf[:, 0:1],
                                                    ALU.pow).then_inc(rs_done, 1)

                @block.scalar
                def _(act):
                    for c in range(nblk):
                        if feed == "load":
                            act.wait_ge(s_x if src is xs else s_mem, 16 * (nblk))
                        else:
                            act.wait_ge(x_done, c + 1)
                        if c:
                            act.wait_ge(ss_done, c)
                        nc.scalar.activation(tmp[:, :], src[:, c, :], ACT.Square,
                                             accum_out=ssum[:, c:c + 1]).then_inc(ss_done, 1)

                @block.vector
                def _(dve):
                    if final or bias is not None:
                        dve.wait_ge(gfin, 16)

                    def evacuate(c):
                        for h in range(2):
                            dve.wait_ge(tr_done, 2 * c + h + 1)
                            g4 = gains[:, gain, 4 * h:4 * h + 4].unsqueeze(2).broadcast_to([P, 4, P])
                            nc.vector.tensor_tensor(
                                dst[:, 4 * h:4 * h + 4, c * P:(c + 1) * P],
                                C[:, 512 * h:512 * h + 512].rearrange("p (k n) -> p k n", k=4), g4,
                                ALU.mult).then_inc(ev_done, 1)

                    for c in range(nblk):
                        if feed == "project":
                            for h in range(2):
                                xh = src[:, c, 512 * h:512 * h + 512]
                                if bias is not None:
                                    nc.vector.tensor_tensor(xh, xh, bbc[:, 512 * h:512 * h + 512],
                                                            ALU.add).then_inc(ad_done, 1)
                                    dve.wait_ge(ad_done, 2 * c + h + 1)
                                dve.wait_ge(pr_done, 2 * c + h + 1)
                                ins = nc.vector.tensor_tensor(xh, xh, (A, B)[c % 2][:, 512 * h:512 * h + 512], ALU.add)
                            ins.then_inc(x_done, 1)
                        if feed == "combine":
                            for j in range(2):
                                dve.wait_ge(ga_done[c % 2][j], 16 * (c // 2 + 1))
                                if j:
                                    dve.wait_ge(ad_done, c + 1)
                                ins = nc.vector.scalar_tensor_tensor(
                                    src[:, c, :], got[c % 2][j], wgt[:, j, c:c + 1], src[:, c, :],
                                    ALU.mult, ALU.add)
                                ins.then_inc(x_done if j else ad_done, 1)
                        if c and not final:
                            evacuate(c - 1)
                        dve.wait_ge(ss_done, c + 1)
                        nc.vector.tensor_scalar(msq[:, c:c + 1], ssum[:, c:c + 1], 1.0 / D, EPS,
                                                ALU.mult, ALU.add).then_inc(ms_done, 1)
                        dve.wait_ge(rs_done, c + 1)
                        if c >= 2 and not final:
                            dve.wait_ge(tr_done, 2 * (c - 1))
                            if rows:
                                dve.wait_ge(st_done[c % 2], 16 * (c // 2))
                        if c >= 2 and final:
                            dve.wait_ge(fin_done, c - 1)
                        nc.vector.tensor_scalar(xn[c % 2], src[:, c, :], rstd[:, c:c + 1], None,
                                                ALU.mult).then_inc(xn_done, 1)
                        if final:
                            dve.wait_ge(xn_done, c + 1)
                            if c >= 2:
                                dve.wait_ge(st_done[c % 2], 16 * (c // 2))
                            nc.vector.tensor_tensor(fin[c % 2], xn[c % 2], gbc, ALU.mult).then_inc(fin_done, 1)
                    if not final:
                        evacuate(nblk - 1)

                @block.tensor
                def _(pe):
                    def transposes(c):
                        pe.wait_ge(xn_done, c + 1)
                        for h in range(2):
                            if c:
                                pe.wait_ge(ev_done, 2 * (c - 1) + h + 1)
                            for b in range(4):
                                k = 4 * h + b
                                ins = nc.tensor.transpose(C[:, k * P:(k + 1) * P],
                                                          xn[c % 2][:, k * P:(k + 1) * P], ident[:])
                            ins.then_inc(tr_done, 1)

                    if feed == "project":
                        pe.wait_ge(w_ready, 16)
                    for c in range(nblk):
                        if feed == "project":
                            if c >= 2:
                                pe.wait_ge(x_done, c - 1)
                            for h in range(2):
                                for k in range(kin):
                                    ins = nc.tensor.matmul((A, B)[c % 2][:, 512 * h:512 * h + 512],
                                                           yT[:, k, c * P:(c + 1) * P],
                                                           w_out[:, k, 512 * h:512 * h + 512],
                                                           start=(k == 0), stop=(k == kin - 1))
                                ins.then_inc(pr_done, 1)
                            if c and not final:
                                transposes(c - 1)
                        elif not final:
                            transposes(c)
                    if feed == "project" and not final:
                        transposes(nblk - 1)

        s_mem = sem("memory_loaded", keep=True)
        s_kv = sem("memory_weights_loaded", keep=True)
        memx = yflat[:, 0:2048].rearrange("p (c n) -> p c n", c=MB)
        memT = yflat[:, 2048:4096].rearrange("p (k n) -> p k n", k=KD)

        def memory_kv():
            mm_done = sem("memkv_product")
            with nc.Block() as block:
                @block.tensor
                def _(pe):
                    pe.wait_ge(s_kv, 16)
                    for h in range(XH):
                        for k in range(KD):
                            ins = nc.tensor.matmul((A, B)[h // 2][:, 512 * (h % 2):512 * (h % 2) + MEM], w_out[:, k, h * P:(h + 1) * P],
                                                   memT[:, k, :], start=(k == 0), stop=(k == KD - 1))
                        ins.then_inc(mm_done, 1)
                    for m in range(MB):
                        for k in range(KD):
                            ins = nc.tensor.matmul(C[:, 512 * m:512 * m + 512], memT[:, k, m * P:(m + 1) * P],
                                                   w_out[:, k, 512:1024], start=(k == 0), stop=(k == KD - 1))
                        ins.then_inc(mm_done, 1)

                @block.scalar
                def _(act):
                    for h in range(XH):
                        act.wait_ge(mm_done, h + 1)
                        nc.scalar.activation(memK[:, h, :], (A, B)[h // 2][:, 512 * (h % 2):512 * (h % 2) + MEM], ACT.Copy)
                    for m in range(MB):
                        act.wait_ge(mm_done, XH + m + 1)
                        nc.scalar.activation(memV[:, m, :], C[:, 512 * m:512 * m + 512], ACT.Copy)

        def hybrid():
            W_C, W_U, W_B, W_Q, W_K, W_V = range(6)
            col0 = {W_B: 0, W_C: CONV_CH, W_U: 2 * CONV_CH, W_Q: 1536, W_K: 2048, W_V: 2560}
            w_in = hyb_w_in[0].rearrange("(k p) n -> p k n", p=P)
            w_loaded = [sem(f"hyb_w{b}_loaded") for b in range(6)]
            product = [sem(f"hyb_product{b}") for b in range(6)]
            c_copied = sem("hyb_c_copied")
            cu_done = sem("hyb_cu_done")
            conv_step = sem("hyb_conv_step")
            gated = sem("hyb_gated")
            raw_done = sem("hyb_raw")
            swapped = sem("hyb_swapped")
            rope_step = sem("hyb_rope_step")
            v_copied = sem("hyb_v_copied")
            scored = sem("hyb_scores")
            maxed = sem("hyb_max")
            exped = sem("hyb_exp")
            ratio_step = sem("hyb_ratio_step")
            combined = sem("hyb_combined")
            turned0 = sem("hyb_probT_low")
            turned1 = sem("hyb_probT_high")
            copied0 = sem("hyb_probT_low_copied")
            copied1 = sem("hyb_probT_high_copied")
            weighed = sem("hyb_pv")
            o_copied = sem("hyb_o_copied")
            sub_step = sem("hyb_subln_step")
            sub_rstd = sem("hyb_subln_rstd")
            o_turned = sem("hyb_oT_psum")
            o_stored = sem("hyb_oT_copied")
            passed = sem("hyb_passed")
            gc, gu = prob[:, 0:1024], prob[:, 1024:2048]
            ofull = tmp[:, :].rearrange("p (n e) -> p n e", n=NB)
            osq = raw[:, :].rearrange("p (n e) -> p n e", n=NB)
            vv = val[:, :].rearrange("p (n e) -> p n e", n=NB)
            with nc.Block() as block:
                @block.sync
                def _(sp):
                    with sp.Fori(0, 4) as j:
                        for b in range(6):
                            col = j * P + col0[b]
                            sp.wait_ge(product[b], j)
                            if col0[b] == 0:
                                sp.sem_inc(passed, 1)
                            sp.dma_start(slot[b], w_in[:, :, bass.ds(col, P)]).then_inc(w_loaded[b], 16)
                    sp.dma_start(w_out, hyb_w_out[0].rearrange("(k p) n -> p k n", p=P)).then_inc(s_wo[0], 16)

                @block.tensor
                def _(pe):
                    def project(j, b, pair):
                        pe.wait_ge(w_loaded[b], j * 16 + 16)
                        for n in range(2):
                            for k in range(KD):
                                ins = nc.tensor.matmul(pair[:, 512 * n:512 * n + 512], slot[b][:, k, :],
                                                       hT[:, k, 512 * n:512 * n + 512],
                                                       start=(k == 0), stop=(k == KD - 1))
                        ins.then_inc(product[b], 1)

                    def swap_halves():
                        for n in range(2):
                            ins = nc.tensor.matmul(C[:, 512 * n:512 * n + 512], rot[:],
                                                   raw[:, 512 * n:512 * n + 512], start=True, stop=True)
                        ins.then_inc(swapped, 1)

                    def scores(j, n):
                        w = (n + 1) * P
                        for m in range(2):
                            pair = (A, B)[m]
                            if n:
                                pe.wait_ge(exped, j * 16 + 2 * (n - 1) + m + 1)
                            for f in range(0, w, 512):
                                f1 = min(w, f + 512)
                                nc.tensor.matmul(pair[:, f:f1], qk[64 * m:64 * m + 64, 0, n * P:(n + 1) * P],
                                                 qk[64 * m:64 * m + 64, 1, f:f1], start=True, stop=f1 != w)
                            nc.tensor.matmul(pair[:, w - P:w], ident_b[:], mask_b[:, 1, :],
                                             start=False, stop=True).then_inc(scored, 1)

                    def turn(j, n):
                        pe.wait_ge(combined, j * 8 + n + 1)
                        for b in range(n + 1):
                            ins = nc.tensor.transpose(C[:, b * P:(b + 1) * P], prob[:, b * P:(b + 1) * P], ident[:])
                            if b == min(n, 3):
                                ins.then_inc(turned0, 1)
                        if n > 3:
                            ins.then_inc(turned1, 1)

                    def weigh(j, n):
                        pe.wait_ge(copied0, j * 8 + n + 1)
                        if n > 3:
                            pe.wait_ge(copied1, j * 4 + n - 3)
                        if n:
                            pe.wait_ge(o_copied, j * 8 + n)
                        for b in range(n + 1):
                            ins = nc.tensor.matmul(pO[:, 0:P], probT[:, b * P:(b + 1) * P], vv[:, b, :],
                                                   start=(b == 0), stop=(b == n))
                        ins.then_inc(weighed, 1)

                    with pe.Fori(0, 4) as j:
                        pe.wait_ge(exped, j * 16)
                        project(j, W_C, A)
                        project(j, W_U, B)
                        pe.wait_ge(c_copied, j + 1)
                        project(j, W_B, A)
                        pe.wait_ge(cu_done, j + 1)
                        project(j, W_Q, B)
                        pe.wait_ge(gated, j + 1)
                        project(j, W_K, A)
                        pe.wait_ge(o_stored, j * 2)
                        pe.wait_ge(raw_done, j * 2 + 1)
                        swap_halves()
                        pe.wait_ge(w_loaded[W_V], j * 16 + 16)
                        for n in range(NB):
                            for k in range(KD):
                                ins = nc.tensor.matmul(B[:, n * P:(n + 1) * P], hT[:, k, n * P:(n + 1) * P],
                                                       slot[W_V][:, k, :], start=(k == 0), stop=(k == KD - 1))
                        ins.then_inc(product[W_V], 1)
                        pe.wait_ge(rope_step, j * 6 + 2)
                        pe.wait_ge(raw_done, j * 2 + 2)
                        swap_halves()
                        pe.wait_ge(rope_step, j * 6 + 6)
                        pe.wait_ge(v_copied, j + 1)
                        scores(j, 0)
                        for n in range(NB):
                            turn(j, n)
                            if n + 1 < NB:
                                scores(j, n + 1)
                            weigh(j, n)
                        pe.wait_ge(sub_step, j * 4 + 4)
                        for b in range(NB):
                            ins = nc.tensor.transpose(C[:, b * P:(b + 1) * P], ofull[:, b, :], ident[:])
                            if b % 4 == 3:
                                ins.then_inc(o_turned, 1)

                @block.scalar
                def _(act):
                    with act.Fori(0, 4) as j:
                        act.wait_ge(product[W_C], j + 1)
                        nc.scalar.activation(gc, A, ACT.Copy).then_inc(c_copied, 1)
                        act.wait_ge(product[W_Q], j + 1)
                        act.wait_ge(sub_step, j * 4)
                        nc.scalar.activation(raw[:, :], B, ACT.Copy, scale=0.125).then_inc(raw_done, 1)
                        act.wait_ge(product[W_K], j + 1)
                        act.wait_ge(rope_step, j * 6 + 1)
                        act.wait_ge(swapped, j * 2 + 1)
                        nc.scalar.activation(raw[:, :], A, ACT.Copy).then_inc(raw_done, 1)
                        act.wait_ge(product[W_V], j + 1)
                        nc.scalar.activation(val[:, :], B, ACT.Copy).then_inc(v_copied, 1)
                        act.wait_ge(gated, j + 1)
                        for n in range(NB):
                            w = (n + 1) * P
                            for m in range(2):
                                act.wait_ge(maxed, j * 16 + 2 * n + m + 1)
                                if n and m == 0:
                                    act.wait_ge(turned0, j * 8 + n)
                                    if n > 4:
                                        act.wait_ge(turned1, j * 4 + n - 4)
                                nc.scalar.activation(prob[:, 1024 * m:1024 * m + w], (A, B)[m][:, 0:w],
                                                     ACT.Exp, bias=nmax[:, 0, m:m + 1],
                                                     accum_out=psum_[:, 0, m:m + 1]).then_inc(exped, 1)
                            act.wait_ge(turned0, j * 8 + n + 1)
                            if n:
                                act.wait_ge(weighed, j * 8 + n)
                            w0 = min(w, 512)
                            nc.scalar.activation(probT[:, 0:w0], C[:, 0:w0], ACT.Copy).then_inc(copied0, 1)
                        for h in range(2):
                            act.wait_ge(o_turned, j * 2 + h + 1)
                            nc.scalar.activation(
                                yT[:, bass.ds(j + 4, 1), 512 * h:512 * h + 512].rearrange("p a n -> p (a n)"),
                                C[:, 512 * h:512 * h + 512], ACT.Copy, scale=subln[:, 0:1]).then_inc(o_stored, 1)

                @block.gpsimd
                def _(pool):
                    with pool.Fori(0, 4) as j:
                        pool.wait_ge(sub_step, j * 4 + 3)
                        nc.gpsimd.tensor_tensor(rstd[:, :], msq[:, :], mhalf[:, :], ALU.pow).then_inc(sub_rstd, 1)

                @block.vector
                def _(dve):
                    with dve.Fori(0, 4) as j:
                        dve.wait_ge(product[W_U], j + 1)
                        dve.wait_ge(c_copied, j + 1)
                        nc.vector.tensor_tensor(gu, gc, B, ALU.mult).then_inc(cu_done, 1)
                        dve.wait_ge(cu_done, j + 1)

                        def tap(t):
                            return conv_w[:, t, bass.ds(j, 1)]

                        nc.vector.tensor_scalar(gc, gu, tap(2), None, ALU.mult).then_inc(conv_step, 1)
                        dve.wait_ge(conv_step, j * 3 + 1)
                        nc.vector.scalar_tensor_tensor(gc[:, 1:S], gu[:, 0:S - 1], tap(1), gc[:, 1:S],
                                                       ALU.mult, ALU.add).then_inc(conv_step, 1)
                        dve.wait_ge(conv_step, j * 3 + 2)
                        nc.vector.scalar_tensor_tensor(gc[:, 2:S], gu[:, 0:S - 2], tap(0), gc[:, 2:S],
                                                       ALU.mult, ALU.add).then_inc(conv_step, 1)
                        dve.wait_ge(conv_step, j * 3 + 3)
                        dve.wait_ge(product[W_B], j + 1)
                        nc.vector.tensor_tensor(yT[:, bass.ds(j, 1), :].rearrange("p a n -> p (a n)"),
                                                gc, A, ALU.mult).then_inc(gated, 1)
                        for t in range(2):
                            dve.wait_ge(raw_done, j * 2 + t + 1)
                            nc.vector.tensor_tensor(qk[:, t, :], raw[:, :], rope[:, 0, :],
                                                    ALU.mult).then_inc(rope_step, 1)
                            if t == 0:
                                dve.wait_ge(o_stored, j * 2)
                            else:
                                dve.wait_ge(rope_step, j * 6 + 3)
                            dve.wait_ge(swapped, j * 2 + t + 1)
                            nc.vector.tensor_tensor(tmp[:, :], C, rope[:, 1, :], ALU.mult).then_inc(rope_step, 1)
                            dve.wait_ge(rope_step, j * 6 + 3 * t + 2)
                            nc.vector.tensor_tensor(qk[:, t, :], qk[:, t, :], tmp[:, :],
                                                    ALU.add).then_inc(rope_step, 1)
                        dve.wait_ge(rope_step, j * 6 + 6)
                        for n in range(NB):
                            w = (n + 1) * P
                            for m in range(2):
                                dve.wait_ge(scored, j * 16 + 2 * n + m + 1)
                                nc.vector.tensor_reduce(nmax[:, 0, m:m + 1], (A, B)[m][:, 0:w], AX, ALU.max,
                                                        negate=True).then_inc(maxed, 1)
                            dve.wait_ge(exped, j * 16 + 2 * n + 2)
                            dve.wait_ge(o_copied, j * 8 + n)
                            nc.vector.reciprocal(rsum[:, 0, 0:2], psum_[:, 0, 0:2]).then_inc(ratio_step, 1)
                            dve.wait_ge(ratio_step, j * 16 + 2 * n + 1)
                            nc.vector.tensor_scalar(ratio[:, 0:1], psum_[:, 0, 0:1], rsum[:, 0, 1:2],
                                                    neg_lam[:, 0:1], ALU.mult, ALU.mult).then_inc(ratio_step, 1)
                            dve.wait_ge(ratio_step, j * 16 + 2 * n + 2)
                            nc.vector.scalar_tensor_tensor(prob[:, 0:w], prob[:, 1024:1024 + w], ratio[:, 0:1],
                                                           prob[:, 0:w], ALU.mult, ALU.add).then_inc(combined, 1)
                            if n > 3:
                                dve.wait_ge(turned1, j * 4 + n - 3)
                                dve.wait_ge(weighed, j * 8 + n)
                                nc.vector.tensor_copy(probT[:, 512:w], C[:, 512:w]).then_inc(copied1, 1)
                            dve.wait_ge(weighed, j * 8 + n + 1)
                            nc.vector.tensor_scalar(ofull[:, n, :], pO[:, 0:P], rsum[:, 0, 0:1], None,
                                                    ALU.mult).then_inc(o_copied, 1)
                        dve.wait_ge(o_copied, j * 8 + 8)
                        nc.vector.tensor_tensor(osq, ofull, ofull, ALU.mult).then_inc(sub_step, 1)
                        dve.wait_ge(sub_step, j * 4 + 1)
                        nc.vector.tensor_reduce(ssum[:, :], osq, AX, ALU.add).then_inc(sub_step, 1)
                        dve.wait_ge(sub_step, j * 4 + 2)
                        nc.vector.tensor_scalar(msq[:, :], ssum[:, :], 1.0 / P, EPS, ALU.mult,
                                                ALU.add).then_inc(sub_step, 1)
                        dve.wait_ge(sub_rstd, j + 1)
                        nc.vector.tensor_tensor(ofull, ofull, rstd[:, :].unsqueeze(2).broadcast_to([P, NB, P]),
                                                ALU.mult).then_inc(sub_step, 1)

        def short_attention(name, windowed, w_src, w_next, n_steps, loops):
            nproj = 4 if windowed else 1
            w_loaded = [sem(name + f"_w{b}_loaded") for b in range(nproj)]
            product = [sem(name + f"_product{b}") for b in range(nproj)]
            raw_done = sem(name + "_raw")
            swapped = sem(name + "_swapped")
            rope_step = sem(name + "_rope_step")
            v_added = sem(name + "_v_added")
            scored = sem(name + "_scores")
            max_step = sem(name + "_max_step")
            maxed = sem(name + "_max")
            exped = sem(name + "_exp")
            sunk = sem(name + "_sink_difference")
            sunk_e = sem(name + "_sink_exp")
            recip_step = sem(name + "_recip_step")
            turned = sem(name + "_probT_psum")
            copied0 = sem(name + "_probT_low_copied")
            copied1 = sem(name + "_probT_high_copied")
            weighed = sem(name + "_pv")
            scaled = sem(name + "_o_scaled")
            o_turned = sem(name + "_oT_psum")
            o_stored = sem(name + "_oT_stored")
            s_bias = sem(name + "_v_bias_loaded")
            NS = n_steps
            ow = 64 if windowed else P
            vbias = val[:, 768:1024]
            if windowed:
                vv = val[:, 0:512].rearrange("p (n e) -> p n e", n=NB)
            osb = val[:, 512:768] if windowed else tmp[:, 0:512]
            PR = [prob[:, 0:1024].rearrange("p (r w) -> p r w", r=4),
                  prob[:, 1024:2048].rearrange("p (r w) -> p r w", r=4)]
            SC = [t.rearrange("p (r w) -> p r w", r=4) for t in (A, B)]

            def width(n):
                return P if windowed and n == 0 else 256

            with nc.Block() as block:
                @block.sync
                def _(sp):
                    if windowed:
                        sp.dma_start(vbias, swa_b_qkv[0, 1280:1536].partition_broadcast(P)).then_inc(s_bias, 16)
                    with sp.Fori(0, loops) as j:
                        for b in range(nproj):
                            sp.wait_ge(product[b], j)
                            if windowed and b == 2:
                                for i in range(2):
                                    sp.dma_start(slot[b][:, :, 64 * i:64 * i + 64],
                                                 w_src[:, :, bass.ds(j * 64 + 1024, 64)]).then_inc(w_loaded[b], 16)
                            elif windowed and b == 3:
                                sp.dma_start(slot[b][:, :, 0:64],
                                             w_src[:, :, bass.ds(j * 64 + 1280, 64)]).then_inc(w_loaded[b], 16)
                            elif windowed:
                                sp.dma_start(slot[b], w_src[:, :, bass.ds(j * 256 + b * P, P)]).then_inc(w_loaded[b], 16)
                            else:
                                sp.dma_start(slot[b], w_src[:, :, bass.ds(j * P, P)]).then_inc(w_loaded[b], 16)
                    w_next(sp)

                @block.tensor
                def _(pe):
                    def project(j, b, pair):
                        pe.wait_ge(w_loaded[b], (j * 16 + 16) * (2 if windowed and b == 2 else 1))
                        for n in range(2):
                            for k in range(KD):
                                ins = nc.tensor.matmul(pair[:, 512 * n:512 * n + 512], slot[b][:, k, :],
                                                       hT[:, k, 512 * n:512 * n + 512],
                                                       start=(k == 0), stop=(k == KD - 1))
                        ins.then_inc(product[b], 1)

                    def scores(j, n):
                        if n >= 2:
                            pe.wait_ge(exped, j * NS + n - 1)
                        sc, w = SC[n % 2], width(n)
                        for r in range(4):
                            if windowed:
                                lo = 64 * (r // 2)
                                k0 = (n - 1) * P if n else 0
                                nc.tensor.matmul(sc[:, r, 0:w], qk[lo:lo + 64, r % 2, n * P:(n + 1) * P],
                                                 qk[lo:lo + 64, 2, k0:k0 + w], start=True, stop=False)
                                ins = nc.tensor.matmul(sc[:, r, 0:w], ident_b[:],
                                                       mask_b[:, :, :].rearrange("p a b -> p (a b)")[:, 256 - w:256],
                                                       start=False, stop=True)
                            else:
                                q0 = (4 * n + r) * P
                                ins = nc.tensor.matmul(sc[:, r, :], qk[:, 0, q0:q0 + P],
                                                       memK[:, bass.ds(j, 1), :].rearrange("p a m -> p (a m)"),
                                                       start=True, stop=True)
                        ins.then_inc(scored, 1)

                    def turn(j, n):
                        pe.wait_ge(exped, j * NS + n + 1)
                        nb = width(n) // P
                        for r in range(4):
                            for b in range(nb):
                                ins = nc.tensor.transpose(C[:, (2 * r + b) * P:(2 * r + b + 1) * P],
                                                          PR[n % 2][:, r, b * P:(b + 1) * P], ident[:])
                            if r % 2:
                                ins.then_inc(turned, 1)

                    def weigh(j, n):
                        pe.wait_ge(copied0, j * NS + n + 1)
                        pe.wait_ge(copied1, j * NS + n + 1)
                        pe.wait_ge(scaled, j * NS + n)
                        nb = width(n) // P
                        for r in range(4):
                            for b in range(nb):
                                if windowed:
                                    v = vv[:, n - nb + 1 + b, :]
                                else:
                                    v = memV[:, b, bass.ds(j * P, P)]
                                ins = nc.tensor.matmul(pO[:, r * ow:(r + 1) * ow],
                                                       probT[:, (2 * r + b) * P:(2 * r + b + 1) * P], v,
                                                       start=(b == 0), stop=(b == nb - 1))
                        ins.then_inc(weighed, 1)

                    def turn_out(j, n):
                        pe.wait_ge(scaled, j * NS + n + 1)
                        pe.wait_ge(o_stored, j * NS + n)
                        for b in range(4 * ow // P):
                            ins = nc.tensor.transpose(pU[:, b * P:(b + 1) * P], osb[:, b * P:(b + 1) * P], ident[:])
                        ins.then_inc(o_turned, 1)

                    if windowed:
                        pe.wait_ge(s_bias, 16)
                    with pe.Fori(0, loops) as j:
                        pe.wait_ge(exped, j * NS)
                        if windowed:
                            project(j, 0, A)
                            project(j, 1, B)
                            for t in range(3):
                                pe.wait_ge(raw_done, j * 3 + t + 1)
                                if t:
                                    pe.wait_ge(rope_step, j * 9 + 3 * t - 1)
                                else:
                                    pe.wait_ge(copied0, j * NS)
                                    pe.wait_ge(copied1, j * NS)
                                for n in range(2):
                                    ins = nc.tensor.matmul(C[:, 512 * n:512 * n + 512], rot[:],
                                                           raw[:, 512 * n:512 * n + 512], start=True, stop=True)
                                ins.then_inc(swapped, 1)
                                if t == 0:
                                    project(j, 2, A)
                                if t == 1:
                                    pe.wait_ge(w_loaded[3], j * 16 + 16)
                                    for n in range(NB):
                                        for k in range(KD):
                                            ins = nc.tensor.matmul(B[:, n * 64:(n + 1) * 64],
                                                                   hT[:, k, n * P:(n + 1) * P],
                                                                   slot[3][:, k, 0:64],
                                                                   start=(k == 0), stop=(k == KD - 1))
                                    ins.then_inc(product[3], 1)
                            pe.wait_ge(rope_step, j * 9 + 9)
                            pe.wait_ge(v_added, j + 1)
                        else:
                            project(j, 0, A)
                            pe.wait_ge(raw_done, j + 1)
                        scores(j, 0)
                        for n in range(NS):
                            turn(j, n)
                            if n + 1 < NS:
                                scores(j, n + 1)
                            weigh(j, n)
                            turn_out(j, n)

                @block.scalar
                def _(act):
                    with act.Fori(0, loops) as j:
                        if windowed:
                            for t in range(3):
                                act.wait_ge(product[t], j + 1)
                                if t:
                                    act.wait_ge(rope_step, j * 9 + 3 * t - 2)
                                    act.wait_ge(swapped, j * 3 + t)
                                bias = k_bias[:, bass.ds(j, 1)] if t == 2 else q_bias[:, bass.ds(2 * j + t, 1)]
                                nc.scalar.activation(raw[:, :], B if t == 1 else A, ACT.Identity, bias=bias,
                                                     scale=1.0 if t == 2 else 0.125).then_inc(raw_done, 1)
                        else:
                            act.wait_ge(product[0], j + 1)
                            nc.scalar.activation(qk[:, 0, :], A, ACT.Copy, scale=float(P) ** -0.5).then_inc(raw_done, 1)
                        for n in range(NS):
                            w = width(n)
                            act.wait_ge(maxed, j * NS + n + 1)
                            if n >= 2:
                                act.wait_ge(turned, 2 * (j * NS + n - 1))
                            for r in range(4):
                                ins = nc.scalar.activation(PR[n % 2][:, r, 0:w], SC[n % 2][:, r, 0:w], ACT.Exp,
                                                           bias=nmax[:, n % 2, r:r + 1],
                                                           accum_out=psum_[:, n % 2, r:r + 1])
                            ins.then_inc(exped, 1)
                            if windowed:
                                act.wait_ge(sunk, j * NS + n + 1)
                                nc.scalar.activation(sinkx[:, 1, :], sinkx[:, 0, :], ACT.Exp).then_inc(sunk_e, 1)
                            act.wait_ge(turned, 2 * (j * NS + n) + 1)
                            act.wait_ge(weighed, j * NS + n)
                            src = C[:, 0:512].rearrange("p (r w) -> p r w", r=2)[:, :, 0:w]
                            dst = probT[:, 0:512].rearrange("p (r w) -> p r w", r=2)[:, :, 0:w]
                            nc.scalar.activation(dst, src, ACT.Copy).then_inc(copied0, 1)
                            act.wait_ge(o_turned, j * NS + n + 1)
                            if windowed:
                                nc.scalar.activation(yT[:, bass.ds(2 * j, 2), n * P:(n + 1) * P],
                                                     pU[:, 0:256].rearrange("p (b n) -> p b n", b=2),
                                                     ACT.Copy).then_inc(o_stored, 1)
                            else:
                                nc.scalar.activation(
                                    yT[:, bass.ds(j, 1), 512 * n:512 * n + 512].rearrange("p a n -> p (a n)"),
                                    pU[:, :], ACT.Copy).then_inc(o_stored, 1)

                @block.vector
                def _(dve):
                    if windowed:
                        dve.wait_ge(s_bias, 16)
                    with dve.Fori(0, loops) as j:
                        if windowed:
                            for t in range(3):
                                dve.wait_ge(raw_done, j * 3 + t + 1)
                                nc.vector.tensor_tensor(qk[:, t, :], raw[:, :], rope[:, 0, :],
                                                        ALU.mult).then_inc(rope_step, 1)
                                dve.wait_ge(swapped, j * 3 + t + 1)
                                dve.wait_ge(rope_step, j * 9 + 3 * t)
                                nc.vector.tensor_tensor(tmp[:, :], C, rope[:, 1, :], ALU.mult).then_inc(rope_step, 1)
                                dve.wait_ge(rope_step, j * 9 + 3 * t + 2)
                                nc.vector.tensor_tensor(qk[:, t, :], qk[:, t, :], tmp[:, :],
                                                        ALU.add).then_inc(rope_step, 1)
                            dve.wait_ge(product[3], j + 1)
                            vb = vbias[:, bass.ds(j * 64, 64)].unsqueeze(1).broadcast_to([P, NB, 64])
                            nc.vector.tensor_tensor(vv, B[:, 0:512].rearrange("p (n e) -> p n e", n=NB), vb,
                                                    ALU.add).then_inc(v_added, 1)
                        for n in range(NS):
                            w, i = width(n), n % 2
                            dve.wait_ge(scored, j * NS + n + 1)
                            if n >= 1:
                                dve.wait_ge(exped, j * NS + n)
                            ins = nc.vector.tensor_reduce(nmax[:, i, :], SC[i][:, :, 0:w], AX, ALU.max, negate=True)
                            if windowed:
                                ins.then_inc(max_step, 1)
                                dve.wait_ge(max_step, j * NS + n + 1)
                                nc.vector.tensor_tensor(nmax[:, i, :], nmax[:, i, :],
                                                        sinks[:, 1, bass.ds(j * 4, 4)], ALU.min).then_inc(maxed, 1)
                                dve.wait_ge(maxed, j * NS + n + 1)
                                nc.vector.tensor_tensor(sinkx[:, 0, :], nmax[:, i, :],
                                                        sinks[:, 0, bass.ds(j * 4, 4)], ALU.add).then_inc(sunk, 1)
                                dve.wait_ge(exped, j * NS + n + 1)
                                dve.wait_ge(sunk_e, j * NS + n + 1)
                                nc.vector.tensor_tensor(psum_[:, i, :], psum_[:, i, :], sinkx[:, 1, :],
                                                        ALU.add).then_inc(recip_step, 1)
                                dve.wait_ge(recip_step, 2 * (j * NS + n) + 1)
                            else:
                                ins.then_inc(maxed, 1)
                                dve.wait_ge(exped, j * NS + n + 1)
                            nc.vector.reciprocal(rsum[:, i, :], psum_[:, i, :]).then_inc(recip_step, 1)
                            dve.wait_ge(turned, 2 * (j * NS + n) + 2)
                            dve.wait_ge(weighed, j * NS + n)
                            src = C[:, 512:1024].rearrange("p (r w) -> p r w", r=2)[:, :, 0:w]
                            dst = probT[:, 512:1024].rearrange("p (r w) -> p r w", r=2)[:, :, 0:w]
                            nc.vector.tensor_copy(dst, src).then_inc(copied1, 1)
                            dve.wait_ge(weighed, j * NS + n + 1)
                            dve.wait_ge(recip_step, (2 if windowed else 1) * (j * NS + n + 1))
                            dve.wait_ge(o_turned, j * NS + n)
                            if windowed:
                                rb = rsum[:, i, :].rearrange("p (l i) -> p l i", l=2)
                                nc.vector.tensor_tensor(
                                    osb[:, 0:256].rearrange("p (i l e) -> p l i e", i=2, l=2),
                                    pO[:, 0:256].rearrange("p (l i e) -> p l i e", i=2, l=2),
                                    rb.unsqueeze(3).broadcast_to([P, 2, 2, 64]), ALU.mult).then_inc(scaled, 1)
                            else:
                                rb = rsum[:, i, :].unsqueeze(2).broadcast_to([P, 4, P])
                                nc.vector.tensor_tensor(osb.rearrange("p (r e) -> p r e", r=4),
                                                        pO[:, :].rearrange("p (r e) -> p r e", r=4), rb,
                                                        ALU.mult).then_inc(scaled, 1)

        def router(l):
            n_ = f"route{l}"
            ld = sem(n_ + "_loaded")
            lg = sem(n_ + "_logits")
            st = sem(n_ + "_step")
            ge1, ge2 = sem(n_ + "_group_exp"), sem(n_ + "_pair_exp")
            oh = sem(n_ + "_onehots")
            rk = sem(n_ + "_ranks")
            sl = sem(n_ + "_slot_onehots")
            sp_ = sem(n_ + "_slot_list")
            NP = 2 * NB
            at = [0]

            def room(*shape):
                n = math.prod(shape)
                v = yflat[:, at[0]:at[0] + n]
                at[0] += n
                if len(shape) == 2:
                    return v.rearrange("p (a b) -> p a b", a=shape[0])
                if len(shape) == 3:
                    return v.rearrange("p (a b c) -> p a b c", a=shape[0], b=shape[1])
                return v

            wr = room(KD, NG + NE)
            rb = room(NG + NE)
            lgt = room(NB, NG + NE)
            gmax, gsum, gmin = room(NB), room(NB), room(NB)
            gexp, geq, gcand, goh = (room(NB, NG) for _ in range(4))
            emask = room(NB, NE)
            top = room(2, NB)
            low = room(2, NB)
            eeq, ecand = room(NB, NE), room(NB, NE)
            oneh = room(2, NB, NE)
            both = room(NB, NE)
            pe2, w1 = room(NB), room(NB)
            cnt, nx, xe, base2 = room(NE), room(NE), room(NE), room(NE)
            over = room(NE, JT)
            rank = room(NB, NE)
            where, far = room(NB, NE), room(NB, NE)
            pos = room(2, NB)
            xcmp = room(XT, NE)
            xid = room(XT)
            wide = room(NP, NTT + 1)
            tile_oh = room(NP, NTT)
            tsum, rem = room(NP), room(NP)
            slot_oh = room(NP, TS)
            both_b = probT[:, 0:128].bitcast(BF16)
            assert at[0] <= KD * S
            R = pO
            with nc.Block() as block:
                @block.sync
                def _(sp):
                    sp.dma_start(wr[:, :, 0:NG], moe_w_group[l].rearrange("(k p) n -> p k n", p=P)).then_inc(ld, 16)
                    sp.dma_start(wr[:, :, NG:NG + NE],
                                 moe_w_router[l].rearrange("(k p) n -> p k n", p=P)).then_inc(ld, 16)
                    sp.dma_start(rb[:, 0:NG], moe_b_group[l].partition_broadcast(P)).then_inc(ld, 16)
                    sp.dma_start(rb[:, NG:NG + NE], moe_b_router[l].partition_broadcast(P)).then_inc(ld, 16)

                @block.tensor
                def _(pe):
                    pe.wait_ge(ld, 64)
                    for c in range(NB):
                        for k in range(KD):
                            ins = nc.tensor.matmul(R[:, c * 36:(c + 1) * 36], hT[:, k, c * P:(c + 1) * P],
                                                   wr[:, k, :], start=(k == 0), stop=(k == KD - 1))
                    ins.then_inc(lg, 1)
                    pe.wait_ge(oh, 1)
                    for c in range(NB + 1):
                        for b in range(min(c + 1, NB)):
                            ins = nc.tensor.matmul(pU[:, c * NE:(c + 1) * NE],
                                                   (tri_b if b == c else ones_b)[:],
                                                   both_b[:, b * NE:(b + 1) * NE],
                                                   start=(b == 0), stop=(b == min(c, NB - 1)))
                    ins.then_inc(rk, 1)
                    pe.wait_ge(sl, 1)
                    for i in range(NP):
                        ins = nc.tensor.matmul(A[0:TS, 0:NTT], slot_oh[:, i, :], tile_oh[:, i, :],
                                               start=(i == 0), stop=(i == NP - 1))
                    ins.then_inc(sp_, 1)

                @block.scalar
                def _(act):
                    act.wait_ge(ge1, 1)
                    nc.scalar.activation(gexp, gexp, ACT.Exp).then_inc(ge1, 1)
                    act.wait_ge(ge2, 1)
                    nc.scalar.activation(pe2, pe2, ACT.Exp).then_inc(ge2, 1)

                @block.vector
                def _(dve):
                    done = [0]

                    def then(ins):
                        done[0] += 1
                        ins.then_inc(st, 1)
                        dve.wait_ge(st, done[0])

                    def bc(ap, n):
                        return ap.unsqueeze(2).broadcast_to([P, ap.shape[1], n])

                    def iota_bc(n, m):
                        return iota[:, 0:m].unsqueeze(1).broadcast_to([P, n, m])

                    dve.wait_ge(lg, 1)
                    dve.wait_ge(ld, 64)
                    then(nc.vector.tensor_tensor(lgt, R[:, 0:NB * 36].rearrange("p (c n) -> p c n", c=NB),
                                                 rb.unsqueeze(1).broadcast_to([P, NB, 36]), ALU.add))
                    then(nc.vector.tensor_reduce(gmax, lgt[:, :, 0:NG], AX, ALU.max))
                    nc.vector.tensor_tensor(gexp, lgt[:, :, 0:NG], bc(gmax, NG), ALU.subtract).then_inc(ge1, 1)

                    def first_of_max(values, best, eq, cand, least, onehot, n):
                        then(nc.vector.tensor_tensor(eq, values, bc(best, n), ALU.is_equal))
                        then(nc.vector.scalar_tensor_tensor(cand, eq, -1000.0, iota_bc(NB, n), ALU.mult, ALU.add))
                        then(nc.vector.tensor_reduce(least, cand, AX, ALU.min))
                        then(nc.vector.tensor_tensor(onehot, cand, bc(least, n), ALU.is_equal))

                    first_of_max(lgt[:, :, 0:NG], gmax, geq, gcand, gmin, goh, NG)
                    ohx = goh.unsqueeze(3).broadcast_to([P, NB, NG, EPG])
                    el = lgt[:, :, NG:NG + NE].rearrange("p c (g e) -> p c g e", g=NG)
                    em = emask.rearrange("p c (g e) -> p c g e", g=NG)
                    eq4 = eeq.rearrange("p c (g e) -> p c g e", g=NG)
                    for c in range(NB):
                        ohc = goh[:, c, :].unsqueeze(2).broadcast_to([P, NG, EPG])
                        nc.vector.tensor_tensor(em[:, c], el[:, c], ohc, ALU.mult)
                        ins = nc.vector.tensor_scalar(eq4[:, c], ohc, -NEG, NEG, ALU.mult, ALU.add)
                    then(ins)
                    then(nc.vector.tensor_tensor(emask, emask, eeq, ALU.add))
                    for i in range(2):
                        then(nc.vector.tensor_reduce(top[:, i, :], emask, AX, ALU.max))
                        first_of_max(emask, top[:, i, :], eeq, ecand, low[:, i, :], oneh[:, i], NE)
                        if i == 0:
                            then(nc.vector.scalar_tensor_tensor(emask, oneh[:, 0], 3.0 * NEG, emask,
                                                                ALU.mult, ALU.add))
                    then(nc.vector.tensor_tensor(both, oneh[:, 0], oneh[:, 1], ALU.add))
                    nc.vector.tensor_copy(both_b, both.rearrange("p c e -> p (c e)")).then_inc(oh, 1)
                    nc.vector.tensor_tensor(pe2, top[:, 1, :], top[:, 0, :], ALU.subtract).then_inc(ge2, 1)
                    dve.wait_ge(ge1, 2)
                    then(nc.vector.tensor_reduce(gsum, gexp, AX, ALU.add))
                    dve.wait_ge(ge2, 2)
                    then(nc.vector.tensor_scalar(w1, pe2, 1.0, None, ALU.add))
                    then(nc.vector.tensor_tensor(w1, w1, gsum, ALU.mult))
                    then(nc.vector.reciprocal(wgt[:, 0, :], w1))
                    then(nc.vector.tensor_tensor(wgt[:, 1, :], wgt[:, 0, :], pe2, ALU.mult))
                    dve.wait_ge(rk, 1)
                    nc.vector.tensor_copy(rank, pU[:, 0:NB * NE].rearrange("p (c e) -> p c e", c=NB))
                    then(nc.vector.tensor_copy(cnt, pU[:, NB * NE:(NB + 1) * NE]))
                    for t in range(JT):
                        ins = nc.vector.tensor_scalar(over[:, :, t], cnt, float((t + 1) * TS), None, ALU.is_gt)
                    then(ins)
                    then(nc.vector.tensor_reduce(nx, over, AX, ALU.add))
                    then(nc.vector.tensor_tensor_scan(xe, ones_b[:, 0:NE], nx, 0.0, ALU.mult, ALU.add))
                    then(nc.vector.tensor_tensor(base2, xe, nx, ALU.subtract))
                    then(nc.vector.tensor_scalar(base2, base2, float(NE - 1), float(TS), ALU.add, ALU.mult))
                    then(nc.vector.scalar_tensor_tensor(base2, iota[:, 0:NE], -float(TS), base2, ALU.mult, ALU.add))
                    then(nc.vector.tensor_scalar(ntile[:], xe[:, NE - 1:NE], float(NE), None, ALU.add))
                    nc.vector.tensor_copy(tile_e[:, 0:NE], iota[:, 0:NE])
                    then(nc.vector.tensor_tensor(
                        xcmp, xe.unsqueeze(1).broadcast_to([P, XT, NE]),
                        iota[:, 0:XT].unsqueeze(2).broadcast_to([P, XT, NE]), ALU.is_le))
                    then(nc.vector.tensor_reduce(xid, xcmp, AX, ALU.add))
                    then(nc.vector.tensor_scalar(tile_e[:, NE:NE + XT], xid, float(NE - 1), None, ALU.min))
                    then(nc.vector.tensor_scalar(far, rank, float(TS), None, ALU.is_ge))
                    then(nc.vector.tensor_tensor(far, far, base2.unsqueeze(1).broadcast_to([P, NB, NE]), ALU.mult))
                    then(nc.vector.tensor_tensor(where, rank, far, ALU.add))
                    then(nc.vector.scalar_tensor_tensor(where, iota_bc(NB, NE), float(TS), where,
                                                        ALU.mult, ALU.add))
                    for i in range(2):
                        then(nc.vector.tensor_tensor(far, where, oneh[:, i], ALU.mult))
                        then(nc.vector.tensor_reduce(pos[:, i, :], far, AX, ALU.add))
                    nc.vector.tensor_copy(pos_u[:, :, :], pos)
                    posf = pos.rearrange("p i c -> p (i c)")
                    for t in range(NTT + 1):
                        ins = nc.vector.tensor_scalar(wide[:, :, t], posf, float(t * TS), None, ALU.is_ge)
                    then(ins)
                    then(nc.vector.tensor_reduce(tsum, wide, AX, ALU.add))
                    then(nc.vector.tensor_scalar(tsum, tsum, -1.0, -float(TS), ALU.add, ALU.mult))
                    then(nc.vector.tensor_tensor(rem, posf, tsum, ALU.add))
                    then(nc.vector.tensor_tensor(tile_oh, wide[:, :, 0:NTT], wide[:, :, 1:NTT + 1], ALU.subtract))
                    for i in range(2):
                        ti = tile_oh[:, i * NB:(i + 1) * NB, :]
                        ins = nc.vector.tensor_tensor(ti, ti, bc(tok_id[:, :], NTT), ALU.mult)
                    then(ins)
                    nc.vector.tensor_tensor(slot_oh, iota_bc(NP, TS), bc(rem, TS), ALU.is_equal).then_inc(sl, 1)
                    dve.wait_ge(sp_, 1)
                    nc.vector.tensor_copy(slots[0:TS, :], A[0:TS, 0:NTT]).then_inc(sl, 1)
                    dve.wait_ge(sl, 2)

        def experts(l):
            n_ = f"moe{l}"
            wl = [sem(n_ + f"_chunk{c}_loaded") for c in range(6)]
            wu = [sem(n_ + f"_chunk{c}_used") for c in range(6)]
            idx_ready = sem(n_ + "_index")
            gathered = sem(n_ + "_gathered")
            x_turned = sem(n_ + "_xT_psum")
            x_ready = sem(n_ + "_xT_ready")
            silu_done = sem(n_ + "_silu")
            hid_done = sem(n_ + "_hidden")
            y0, y1 = sem(n_ + "_y_low_copied"), sem(n_ + "_y_high_copied")
            stored = sem(n_ + "_stored")
            passed = sem(n_ + "_passed")
            xg = yflat[:, 0:1024]
            xT = yflat[:, 1024:2048].rearrange("p (k n) -> p k n", k=KD)
            gate = yflat[:, 2048:2560].rearrange("p (f n) -> p f n", f=4)
            hid = yflat[:, 2560:3072].rearrange("p (f n) -> p f n", f=4)
            ysb = yflat[:, 3072:4096]
            GU = [A[:, 0:512], A[:, 512:1024], B[:, 0:512], B[:, 512:1024]]
            Y = [C[:, 0:512], C[:, 512:1024]]
            T = [pO[:, :], pU[:, :]]

            def loop(eng):
                n = eng.value_load(ntile[0:1, 0:1], min_val=NE, max_val=NT_MAX)
                return eng.Fori(0, n)

            wgu = moe_w_gate_up[l].rearrange("e (k p) (t f) -> e p k t f", p=P, t=2)
            wdn = moe_w_down[l].rearrange("e (k p) n -> e p k n", p=P)
            with nc.Block() as block:
                @block.sync
                def _(sp):
                    with loop(sp) as t:
                        e = sp.value_load(tile_e[0:1, bass.ds(t, 1)], min_val=0, max_val=NE - 1)
                        for c in range(4):
                            sp.wait_ge(wu[c], t)
                            cv = chunk[c].rearrange("p (t k f) -> p t k f", t=2, k=KD)
                            for i in range(2):
                                sp.dma_start(cv[:, i], wgu[bass.ds(e, 1), :, :, i, c * P:(c + 1) * P]
                                             .rearrange("a p k f -> (a p) k f")).then_inc(wl[c], 16)
                        for c in range(2):
                            sp.wait_ge(wu[4 + c], t)
                            sp.dma_start(chunk[4 + c].rearrange("p (k n) -> p k n", k=4),
                                         wdn[bass.ds(e, 1), :, :, 512 * c:512 * c + 512]
                                         .rearrange("a p k n -> (a p) k n")).then_inc(wl[4 + c], 16)

                @block.gpsimd
                def _(pool):
                    def gather(t):
                        nc.gpsimd.tensor_copy(icol[0:TS, :], slots[0:TS, bass.ds(t, 1)]).then_inc(idx_ready, 1)
                        pool.wait_ge(idx_ready, t + 1)
                        pool.sem_inc(passed, 1)
                        pool.indirect_dma_start(xg[0:TS, :], None, h_dram,
                                                bass.IndirectOffsetOnAxis(ap=icol[0:TS, 0:1], axis=0)
                                                ).then_inc(gathered, 16)

                    gather(0)
                    with loop(pool) as t:
                        pool.wait_ge(gathered, t * 16 + 16)
                        pool.wait_ge(x_turned, t * 2 + 2)
                        gather(t + 1)
                    n = pool.value_load(ntile[0:1, 0:1], min_val=NE, max_val=NT_MAX)
                    pool.wait_ge(gathered, n * 16 + 16)
                    pool.sem_inc(passed, 1)

                @block.tensor
                def _(pe):
                    def turn(t):
                        pe.wait_ge(gathered, t * 16 + 16)
                        for h in range(2):
                            for b in range(4):
                                k = 4 * h + b
                                ins = nc.tensor.transpose(T[h][:, b * P:b * P + TS], xg[0:TS, k * P:(k + 1) * P],
                                                          ident[0:TS, 0:TS])
                            ins.then_inc(x_turned, 1)

                    turn(0)
                    with loop(pe) as t:
                        pe.wait_ge(x_ready, t * 2 + 2)
                        pe.wait_ge(hid_done, t * 4)
                        for f in range(4):
                            pe.wait_ge(wl[f], t * 32 + 32)
                            cv = chunk[f].rearrange("p (t k f) -> p t k f", t=2, k=KD)
                            for i in range(2):
                                for k in range(KD):
                                    ins = nc.tensor.matmul(GU[f][:, i * P:i * P + TS], cv[:, i, k, :],
                                                           xT[:, k, 0:TS], start=(k == 0), stop=(k == KD - 1))
                            ins.then_inc(wu[f], 1)
                        turn(t + 1)
                        pe.wait_ge(hid_done, t * 4 + 4)
                        for c in range(2):
                            pe.wait_ge((y0, y1)[c], t)
                            pe.wait_ge(wl[4 + c], t * 16 + 16)
                            wd = chunk[4 + c].rearrange("p (k n) -> p k n", k=4)
                            for f in range(4):
                                ins = nc.tensor.matmul(Y[c][0:TS, :], hid[:, f, 0:TS], wd[:, f, :],
                                                       start=(f == 0), stop=(f == 3))
                            ins.then_inc(wu[4 + c], 1)

                @block.scalar
                def _(act):
                    with loop(act) as t:
                        for f in range(4):
                            act.wait_ge(wu[f], t + 1)
                            act.wait_ge(hid_done, t * 4)
                            nc.scalar.activation(gate[:, f, 0:TS], GU[f][:, 0:TS], ACT.Silu).then_inc(silu_done, 1)
                        act.wait_ge(wu[4], t + 1)
                        act.wait_ge(stored, t * 16)
                        nc.scalar.activation(ysb[0:TS, 0:512], Y[0][0:TS, :], ACT.Copy).then_inc(y0, 1)
                        act.wait_ge(y0, t + 1)
                        act.wait_ge(y1, t + 1)
                        act.dma_start(y_dram[bass.ds(t * TS, TS), :], ysb[0:TS, :]).then_inc(stored, 16)
                    n = act.value_load(ntile[0:1, 0:1], min_val=NE, max_val=NT_MAX)
                    act.wait_ge(stored, n * 16)
                    act.sem_inc(passed, 1)

                @block.vector
                def _(dve):
                    def keep(t):
                        for h in range(2):
                            dve.wait_ge(x_turned, t * 2 + h + 1)
                            g4 = gains[:, 3 + 3 * l, 4 * h:4 * h + 4].unsqueeze(2).broadcast_to([P, 4, TS])
                            nc.vector.tensor_tensor(
                                xT[:, 4 * h:4 * h + 4, 0:TS],
                                T[h].rearrange("p (k n) -> p k n", k=4)[:, :, 0:TS], g4,
                                ALU.mult).then_inc(x_ready, 1)

                    keep(0)
                    with loop(dve) as t:
                        for f in range(4):
                            dve.wait_ge(silu_done, t * 4 + f + 1)
                            if f == 0:
                                dve.wait_ge(wu[4], t)
                                dve.wait_ge(wu[5], t)
                            nc.vector.tensor_tensor(hid[:, f, 0:TS], gate[:, f, 0:TS], GU[f][:, P:P + TS],
                                                    ALU.mult).then_inc(hid_done, 1)
                        dve.wait_ge(wu[3], t + 1)
                        keep(t + 1)
                        dve.wait_ge(wu[5], t + 1)
                        dve.wait_ge(stored, t * 16)
                        nc.vector.tensor_copy(ysb[0:TS, 512:1024], Y[1][0:TS, :]).then_inc(y1, 1)

        def load_out_matrix(w, i):
            def go(sp):
                k = w.shape[0] // P
                sp.dma_start(w_out[:, 0:k, :], w.rearrange("(k p) n -> p k n", p=P)).then_inc(s_wo[i], 16)
            return go

        setup()
        end_phase()

        def load_memory(sp):
            for c in range(MB):
                sp.dma_start(memx[:, c, :], mem[0, c * P:(c + 1) * P, :]).then_inc(s_mem, 16)
            sp.dma_start(w_out, mem_w_kv.rearrange("(k p) n -> p k n", p=P)).then_inc(s_kv, 16)

        stream("memory", MB, memx, 0, "load", dst=memT, preload=load_memory)
        end_phase()
        memory_kv()
        end_phase()

        def rows_cleared(sp):
            sp.wait_ge(s_zero, 16 * XT)

        stream("in0", NB, xs, 1, "load", preload=rows_cleared)
        end_phase()
        hybrid()
        end_phase()
        stream("mix0", NB, xs, 2, "project", kin=KD, w_ready=s_wo[0])
        end_phase()
        short_attention("cross0", False, xattn_w_q[0].rearrange("(k p) n -> p k n", p=P),
                        load_out_matrix(xattn_w_o[0], 1), 2, XH)
        end_phase()
        stream("att0", NB, xs, 3, "project", kin=4, w_ready=s_wo[1], rows=True)
        end_phase()
        router(0)
        end_phase()
        experts(0)
        end_phase()
        stream("moe0_in", NB, xs, 4, "combine")
        end_phase()
        short_attention("window", True, swa_w_qkv[0].rearrange("(k p) n -> p k n", p=P),
                        load_out_matrix(swa_w_out[0], 2), NB, SWA_KV)
        end_phase()
        stream("mix1", NB, xs, 5, "project", kin=KD, w_ready=s_wo[2], bias=swa_b_out[0])
        end_phase()
        short_attention("cross1", False, xattn_w_q[1].rearrange("(k p) n -> p k n", p=P),
                        load_out_matrix(xattn_w_o[1], 3), 2, XH)
        end_phase()
        stream("att1", NB, xs, 6, "project", kin=4, w_ready=s_wo[3], rows=True)
        end_phase()
        router(1)
        end_phase()
        experts(1)
        end_phase()
        stream("moe1_in", NB, xs, 6, "combine", final=True)
        end_phase()


_INS = ["x", "mem", "mem_norm", "mem_w_kv", "norm_mix", "norm_xattn", "norm_ffn", "hyb_w_in",
        "hyb_conv_w", "diff_lambda", "diff_subln", "hyb_w_out", "swa_w_qkv", "swa_b_qkv", "swa_sinks",
        "swa_w_out", "swa_b_out", "xattn_w_q", "xattn_w_o", "moe_w_group", "moe_b_group",
        "moe_w_router", "moe_b_router", "moe_w_gate_up", "moe_w_down", "final_norm"]


def shape_constants():
    import numpy as np
    f = np.float32
    inv = f(500000.0) ** (-np.arange(0, 16, 2, dtype=f) / f(16))
    ang = (np.arange(S, dtype=f)[:, None] * inv.astype(f)[None, :]).astype(f)
    cos, sin = np.cos(ang).T.astype(f), np.sin(ang).T.astype(f)
    rope = np.zeros((P, 2, S), f)
    rope[:, 0] = 1.0
    swap = np.zeros((P, P), f)
    for h in (0, 64):
        rope[h:h + 8, 0] = rope[h + 8:h + 16, 0] = cos
        rope[h:h + 8, 1], rope[h + 8:h + 16, 1] = -sin, sin
        for i in range(8):
            swap[h + i, h + 8 + i] = swap[h + 8 + i, h + i] = 1.0
    r = np.arange(P)
    c = np.zeros((P, C_ALL), f)
    c[:, C_ID:C_ID + P] = np.eye(P)
    c[:, C_R:C_R + P] = swap
    c[:, C_TRI:C_TRI + P] = r[:, None] < r[None, :]
    c[:, C_CAUSAL:C_CAUSAL + P] = np.where(r[None, :] > r[:, None], NEG, 0.0)
    c[:, C_PREV:C_PREV + P] = np.where(r[None, :] <= r[:, None], NEG, 0.0)
    c[:, C_IOTA:C_IOTA + P] = r[None, :]
    c[:, C_TOK:C_TOK + NB] = r[:, None] + P * np.arange(NB)[None, :]
    return rope, c


def kernel(**inputs):
    import numpy as _np
    import concourse.bacc as _bacc
    from concourse.bass_utils import run_bass_kernel_spmd as _run

    nc = _bacc.Bacc("TRN2", target_bir_lowering=False, num_devices=1)
    arrays, args = {}, []
    given = [(name, _np.ascontiguousarray(inputs[name])) for name in _INS]
    given += list(zip(("rope_tables", "constants"), shape_constants()))
    for name, a in given:
        arrays[f"in_{name}_dram"] = a
        args.append(nc.dram_tensor(f"in_{name}_dram", a.shape, mybir.dt.from_np(a.dtype),
                                   kind="ExternalInput").ap())
    args.append(nc.dram_tensor("out_dram", (1, S, D), F32, kind="ExternalOutput").ap())
    build(nc, *args)
    r = _run(nc, [arrays], core_ids=[0])
    return r.results[0]["out_dram"]
```

```python
import math
from contextlib import ExitStack

import concourse.bass as bass
from concourse import mybir

P = 128
ALU = mybir.AluOpType
ACT = mybir.ActivationFunctionType
F32 = mybir.dt.float32
BF16 = mybir.dt.bfloat16
U32 = mybir.dt.uint32
I32 = mybir.dt.int32
AX = mybir.AxisListType.X

D = 1024
S = 1024
KD = D // P
NB = S // P
MEM = 256
MB = MEM // P
CONV_CH, DIFF_HEADS = 512, 4
SWA_KV = 4
XH = 4
NG, EPG, NE = 4, 8, 32
EH = 512
EPS = 1e-6
NEG = -1.0e30
LAMBDA_INIT = 0.8 - 0.6 * math.exp(-0.3 * 0)

TS = 128
XT = 2 * S // TS
NT_MAX = NE + XT
NTT = NT_MAX + 2
assert NE % 2 == 0 and XT % 2 == 0
JT = -(-S // TS) - 1

C_ID, C_R, C_TRI, C_CAUSAL, C_PREV, C_IOTA, C_TOK, C_ALL = 0, 128, 256, 384, 512, 640, 768, 776

V_GAIN = 0
V_CONV = V_GAIN + 7 * KD
V_SUBLN = V_CONV + 3 * 4
V_QB = V_SUBLN + 1
V_KB = V_QB + 8
V_LAM = V_KB + 2
V_SINK = V_LAM + 256
V_VB = V_SINK + 16
V_ALL = V_VB + 256
V_KEEP = V_LAM


def build(nc, x, mem, mem_norm, mem_w_kv, norm_mix, norm_xattn, norm_ffn, hyb_w_in, hyb_conv_w,
          diff_lambda, diff_subln, hyb_w_out, swa_w_qkv, swa_b_qkv, swa_sinks, swa_w_out, swa_b_out,
          xattn_w_q, xattn_w_o, moe_w_group, moe_b_group, moe_w_router, moe_b_router,
          moe_w_gate_up, moe_w_down, final_norm, rope_tables, constants, vectors, out):
    ctx = ExitStack()
    with ctx:
        def sb(name, shape, dt=F32):
            return ctx.enter_context(nc.sbuf_tensor(name, shape, dt))

        phase = []

        def sem(name, keep=False):
            s = nc.alloc_semaphore(name=name)
            if not keep:
                phase.append(s)
            return s

        credits = []

        def loop_sem(name, credit):
            s = sem(name)
            credits.append((s, credit))
            return s

        def give_credits(sp):
            for s, credit in credits:
                sp.sem_inc(s, credit)
            credits.clear()

        def end_phase():
            nc.clear_and_free_semaphores(list(phase))
            phase.clear()
            nc.all_engine_barrier()

        xs = sb("xs", [P, NB, D])
        hT = sb("hT", [P, KD, S])
        yT = sb("yT", [P, KD, S])
        W = sb("W", [P, 14336])
        prob = sb("prob", [P, 2048])
        probT = sb("probT", [P, 1024])
        qk = sb("qk", [P, 3, S])
        raw = sb("raw", [P, S])
        tmp = sb("tmp", [P, S])
        val = sb("val", [P, 1024])
        rope = sb("rope", [P, 2, S])
        memK = sb("memK", [P, XH, MEM])
        memV = sb("memV", [P, MB, XH * P])
        ident = sb("ident", [P, P])
        rot = sb("rot", [P, P])
        iota = sb("iota", [P, P])
        tok_id = sb("tok_id", [P, NB])
        ident_b = sb("ident_b", [P, P], BF16)
        tri_b = sb("tri_b", [P, P], BF16)
        ones_b = sb("ones_b", [P, P], BF16)
        mask_b = sb("mask_b", [P, 2, P], BF16)
        vecs = sb("vecs", [P, V_KEEP])
        gains = vecs[:, V_GAIN:V_CONV].rearrange("p (g k) -> p g k", g=7)
        conv_w = vecs[:, V_CONV:V_SUBLN].rearrange("p (t b) -> p t b", t=3)
        subln = vecs[:, V_SUBLN:V_QB]
        q_bias = vecs[:, V_QB:V_KB]
        k_bias = vecs[:, V_KB:V_KEEP]
        neg_lam = sb("neg_lam", [P, 1])
        lamv = sb("lamv", [P, 4])
        sinks = sb("sinks", [P, 2, 16])
        mhalf = sb("mhalf", [P, NB])
        ssum = sb("ssum", [P, NB])
        msq = sb("msq", [P, NB])
        rstd = sb("rstd", [P, NB])
        nmax = sb("nmax", [P, 2, 4])
        psum_ = sb("psum_", [P, 2, 4])
        rsum = sb("rsum", [P, 2, 4])
        ratio = sb("ratio", [P, 2])
        slots = raw[:, 0:NTT].bitcast(U32)
        pos_u = sb("pos_u", [P, 2, NB], U32)
        wgt = sb("wgt", [P, 2, NB])
        tile_e = raw[:, 128:128 + NTT].bitcast(I32)
        nround = sb("nround", [P, 1], I32)
        icol = sb("icol", [P, 2], U32)
        sinkx = sb("sinkx", [P, 4, 4])

        pairs = [ctx.enter_context(nc.psum_tensor(f"pair{i}", [P, 1024], F32)) for i in range(3)]
        A, B, C = (t[:, :] for t in pairs)
        pO = ctx.enter_context(nc.psum_tensor("pO", [P, 512], F32))
        pU = ctx.enter_context(nc.psum_tensor("pU", [P, 512], F32))

        h_dram = nc.dram_tensor("h_rows", [S, D], F32, kind="Internal").ap()
        y_dram = nc.dram_tensor("y_rows", [NT_MAX * TS, D], F32, kind="Internal").ap()

        slot = [W[:, 1024 * b:1024 * (b + 1)].rearrange("p (k n) -> p k n", k=KD) for b in range(6)]
        w_out = W[:, 6144:14336].rearrange("p (k n) -> p k n", k=KD)
        yflat = yT[:, :, :].rearrange("p k n -> p (k n)")

        s_const = sem("const_loaded", keep=True)
        s_x = sem("x_loaded", keep=True)
        s_zero = sem("rows_cleared", keep=True)
        s_wo = [sem(f"out_weights_loaded{i}", keep=True) for i in range(4)]

        s_mem = sem("memory_loaded", keep=True)
        s_kv = sem("memory_weights_loaded", keep=True)
        memx = yflat[:, 0:2048].rearrange("p (c n) -> p c n", c=MB)
        memT = yflat[:, 2048:4096].rearrange("p (k n) -> p k n", k=KD)

        def load_memory(sp):
            for c in range(MB):
                sp.dma_start(memx[:, c, :], mem[0, c * P:(c + 1) * P, :]).then_inc(s_mem, 16)
            sp.dma_start(w_out, mem_w_kv.rearrange("(k p) n -> p k n", p=P)).then_inc(s_kv, 16)

        def setup():
            cast_done = sem("constants_cast")
            zeroed = sem("zero_rows_ready")
            zero_rows = yflat[:, 4096:5120]
            lam1, lam2, lam3, lam4 = (sem(f"lambda_step{i}") for i in range(4))
            lraw = raw[:, 0:512].rearrange("p (a b) -> p a b", a=4)
            with nc.Block() as block:
                @block.sync
                def _(sp):
                    small = [
                        (ident[:], constants[:, C_ID:C_ID + P]), (rot[:], constants[:, C_R:C_R + P]),
                        (iota[:], constants[:, C_IOTA:C_IOTA + P]),
                        (tok_id[:], constants[:, C_TOK:C_TOK + NB]),
                        (prob[:, 0:384], constants[:, C_TRI:C_TRI + 384]),
                        (rope[:, :, :], rope_tables),
                        (vecs[:, :], vectors[:, 0:V_KEEP]),
                        (raw[:, 0:272], vectors[:, V_LAM:V_VB]),
                    ]
                    for dst, src in small:
                        sp.dma_start(dst, src).then_inc(s_const, 16)
                    assert len(small) == 8
                    load_memory(sp)
                    for c in range(NB):
                        sp.dma_start(xs[:, c, :], x[0, c * P:(c + 1) * P, :]).then_inc(s_x, 16)

                @block.vector
                def _(dve):
                    nc.vector.memset(zero_rows, 0.0).then_inc(zeroed, 1)
                    dve.wait_ge(s_const, 128)
                    nc.vector.tensor_copy(ident_b[:], ident[:])
                    nc.vector.tensor_copy(tri_b[:], prob[:, 0:128])
                    nc.vector.tensor_copy(mask_b[:, 1, :], prob[:, 128:256])
                    nc.vector.tensor_copy(mask_b[:, 0, :], prob[:, 256:384])
                    nc.vector.memset(ones_b[:], 1.0)
                    nc.vector.memset(mhalf[:], -0.5)
                    nc.vector.tensor_tensor(tmp[:, 0:64], raw[:, 0:64], raw[:, 64:128], ALU.mult)
                    nc.vector.tensor_tensor(tmp[:, 64:128], raw[:, 128:192], raw[:, 192:256],
                                            ALU.mult).then_inc(lam1, 1)
                    dve.wait_ge(lam1, 1)
                    nc.vector.tensor_reduce(lamv[:, 0:2], tmp[:, 0:128].rearrange("p (a b) -> p a b", a=2),
                                            AX, ALU.add).then_inc(lam2, 1)
                    dve.wait_ge(lam3, 1)
                    nc.vector.tensor_tensor(lamv[:, 0:1], lamv[:, 3:4], lamv[:, 2:3],
                                            ALU.subtract).then_inc(lam4, 1)
                    dve.wait_ge(lam4, 1)
                    nc.vector.tensor_scalar(neg_lam[:], lamv[:, 0:1], -LAMBDA_INIT, None, ALU.add)
                    nc.vector.tensor_scalar(subln[:], subln[:], 1.0 - LAMBDA_INIT, None, ALU.mult)
                    nc.vector.tensor_scalar(q_bias[:], q_bias[:], 0.125, None, ALU.mult)
                    for row, sign in ((0, 1.0), (1, -1.0)):
                        ins = nc.vector.tensor_scalar(
                            sinks[:, row, :], raw[:, 256:272], sign, None, ALU.mult)
                    ins.then_inc(cast_done, 1)
                    dve.wait_ge(cast_done, 1)

                @block.scalar
                def _(act):
                    act.wait_ge(zeroed, 1)
                    for t in range(NE, NT_MAX):
                        act.dma_start(y_dram[t * TS:(t + 1) * TS, :], zero_rows[0:TS, :]).then_inc(s_zero, 16)
                    act.wait_ge(lam2, 1)
                    nc.scalar.activation(lamv[:, 2:4], lamv[:, 0:2], ACT.Exp).then_inc(lam3, 1)

        def stream(name, nblk, src, gain, feed, kin=0, w_ready=None, bias=None, dst=hT, rows=False,
                   final=False, preload=None):
            x_done = sem(name + "_x_done")
            ss_done = sem(name + "_sumsq_done")
            ms_done = sem(name + "_meansq_done")
            rs_done = sem(name + "_rstd_done")
            xn_done = sem(name + "_normed")
            tr_done = sem(name + "_transposed")
            ev_done = sem(name + "_evacuated")
            pr_done = sem(name + "_projected")
            ad_done = sem(name + "_added")
            st_done = [sem(name + f"_rows_stored{i}") for i in range(2)]
            ga_done = [[sem(name + f"_gathered{j}{i}") for i in range(2)] for j in range(2)]
            gfin = sem(name + "_gain_loaded")
            fin_done = sem(name + "_gained")
            xn = [prob[:, 0:1024], prob[:, 1024:2048]]
            got = [[yflat[:, 1024 * (2 * i + j):1024 * (2 * i + j + 1)] for j in range(2)] for i in range(2)]
            fin = [yflat[:, 4096:5120], yflat[:, 5120:6144]]
            gbc = val[:, :]
            bbc = val[:, :]
            with nc.Block() as block:
                @block.sync
                def _(sp):
                    if final:
                        sp.dma_start(gbc, final_norm.partition_broadcast(P)).then_inc(gfin, 16)
                    if bias is not None:
                        sp.dma_start(bbc, bias.partition_broadcast(P)).then_inc(gfin, 16)
                    if preload:
                        preload(sp)
                    if rows:
                        for c in range(nblk):
                            sp.wait_ge(xn_done, c + 1)
                            sp.dma_start(h_dram[c * P:(c + 1) * P, :], xn[c % 2]).then_inc(st_done[c % 2], 16)
                    if final:
                        for c in range(nblk):
                            sp.wait_ge(fin_done, c + 1)
                            sp.dma_start(out[0, c * P:(c + 1) * P, :], fin[c % 2]).then_inc(st_done[c % 2], 16)
                    if rows or final:
                        for i in range(2):
                            sp.wait_ge(st_done[i], 16 * (nblk // 2))

                @block.gpsimd
                def _(pool):
                    for c in range(nblk + 1):
                        if feed == "combine" and c < nblk:
                            if c >= 2:
                                pool.wait_ge(x_done, c - 1)
                            for j in range(2):
                                pool.indirect_dma_start(
                                    got[c % 2][j], None, y_dram,
                                    bass.IndirectOffsetOnAxis(ap=pos_u[:, j, c:c + 1], axis=0),
                                ).then_inc(ga_done[c % 2][j], 16)
                        if c >= 1:
                            pool.wait_ge(ms_done, c)
                            nc.gpsimd.tensor_tensor(rstd[:, c - 1:c], msq[:, c - 1:c], mhalf[:, 0:1],
                                                    ALU.pow).then_inc(rs_done, 1)

                @block.scalar
                def _(act):
                    for c in range(nblk):
                        if feed == "load":
                            act.wait_ge(s_x if src is xs else s_mem, 16 * (nblk))
                        else:
                            act.wait_ge(x_done, c + 1)
                        if c:
                            act.wait_ge(ss_done, c)
                        nc.scalar.activation(tmp[:, :], src[:, c, :], ACT.Square,
                                             accum_out=ssum[:, c:c + 1]).then_inc(ss_done, 1)

                @block.vector
                def _(dve):
                    if final or bias is not None:
                        dve.wait_ge(gfin, 16)

                    def evacuate(c):
                        for h in range(2):
                            dve.wait_ge(tr_done, 2 * c + h + 1)
                            g4 = gains[:, gain, 4 * h:4 * h + 4].unsqueeze(2).broadcast_to([P, 4, P])
                            nc.vector.tensor_tensor(
                                dst[:, 4 * h:4 * h + 4, c * P:(c + 1) * P],
                                C[:, 512 * h:512 * h + 512].rearrange("p (k n) -> p k n", k=4), g4,
                                ALU.mult).then_inc(ev_done, 1)

                    for c in range(nblk):
                        if feed == "project":
                            for h in range(2):
                                xh = src[:, c, 512 * h:512 * h + 512]
                                if bias is not None:
                                    nc.vector.tensor_tensor(xh, xh, bbc[:, 512 * h:512 * h + 512],
                                                            ALU.add).then_inc(ad_done, 1)
                                    dve.wait_ge(ad_done, 2 * c + h + 1)
                                dve.wait_ge(pr_done, 2 * c + h + 1)
                                ins = nc.vector.tensor_tensor(xh, xh, (A, B)[c % 2][:, 512 * h:512 * h + 512], ALU.add)
                            ins.then_inc(x_done, 1)
                        if feed == "combine":
                            for j in range(2):
                                dve.wait_ge(ga_done[c % 2][j], 16 * (c // 2 + 1))
                                if j:
                                    dve.wait_ge(ad_done, c + 1)
                                ins = nc.vector.scalar_tensor_tensor(
                                    src[:, c, :], got[c % 2][j], wgt[:, j, c:c + 1], src[:, c, :],
                                    ALU.mult, ALU.add)
                                ins.then_inc(x_done if j else ad_done, 1)
                        if c and not final:
                            evacuate(c - 1)
                        dve.wait_ge(ss_done, c + 1)
                        nc.vector.tensor_scalar(msq[:, c:c + 1], ssum[:, c:c + 1], 1.0 / D, EPS,
                                                ALU.mult, ALU.add).then_inc(ms_done, 1)
                        dve.wait_ge(rs_done, c + 1)
                        if c >= 2 and not final:
                            dve.wait_ge(tr_done, 2 * (c - 1))
                            if rows:
                                dve.wait_ge(st_done[c % 2], 16 * (c // 2))
                        if c >= 2 and final:
                            dve.wait_ge(fin_done, c - 1)
                        nc.vector.tensor_scalar(xn[c % 2], src[:, c, :], rstd[:, c:c + 1], None,
                                                ALU.mult).then_inc(xn_done, 1)
                        if final:
                            dve.wait_ge(xn_done, c + 1)
                            if c >= 2:
                                dve.wait_ge(st_done[c % 2], 16 * (c // 2))
                            nc.vector.tensor_tensor(fin[c % 2], xn[c % 2], gbc, ALU.mult).then_inc(fin_done, 1)
                    if not final:
                        evacuate(nblk - 1)

                @block.tensor
                def _(pe):
                    def transposes(c):
                        pe.wait_ge(xn_done, c + 1)
                        for h in range(2):
                            if c:
                                pe.wait_ge(ev_done, 2 * (c - 1) + h + 1)
                            for b in range(4):
                                k = 4 * h + b
                                ins = nc.tensor.transpose(C[:, k * P:(k + 1) * P],
                                                          xn[c % 2][:, k * P:(k + 1) * P], ident[:])
                            ins.then_inc(tr_done, 1)

                    if feed == "project":
                        pe.wait_ge(*w_ready)
                    for c in range(nblk):
                        if feed == "project":
                            if c >= 2:
                                pe.wait_ge(x_done, c - 1)
                            for h in range(2):
                                for k in range(kin):
                                    ins = nc.tensor.matmul((A, B)[c % 2][:, 512 * h:512 * h + 512],
                                                           yT[:, k, c * P:(c + 1) * P],
                                                           w_out[:, k, 512 * h:512 * h + 512],
                                                           start=(k == 0), stop=(k == kin - 1))
                                ins.then_inc(pr_done, 1)
                            if c and not final:
                                transposes(c - 1)
                        elif not final:
                            transposes(c)
                    if feed == "project" and not final:
                        transposes(nblk - 1)


        def memory_kv():
            mm_done = sem("memkv_product")
            with nc.Block() as block:
                @block.tensor
                def _(pe):
                    pe.wait_ge(s_kv, 16)
                    for h in range(XH):
                        for k in range(KD):
                            ins = nc.tensor.matmul((A, B)[h // 2][:, 512 * (h % 2):512 * (h % 2) + MEM], w_out[:, k, h * P:(h + 1) * P],
                                                   memT[:, k, :], start=(k == 0), stop=(k == KD - 1))
                        ins.then_inc(mm_done, 1)
                    for m in range(MB):
                        for k in range(KD):
                            ins = nc.tensor.matmul(C[:, 512 * m:512 * m + 512], memT[:, k, m * P:(m + 1) * P],
                                                   w_out[:, k, 512:1024], start=(k == 0), stop=(k == KD - 1))
                        ins.then_inc(mm_done, 1)

                @block.scalar
                def _(act):
                    for h in range(XH):
                        act.wait_ge(mm_done, h + 1)
                        nc.scalar.activation(memK[:, h, :], (A, B)[h // 2][:, 512 * (h % 2):512 * (h % 2) + MEM], ACT.Copy)
                    for m in range(MB):
                        act.wait_ge(mm_done, XH + m + 1)
                        nc.scalar.activation(memV[:, m, :], C[:, 512 * m:512 * m + 512], ACT.Copy)

        def hybrid():
            W_Q, W_K, W_V, W_C, W_U, W_B = range(6)
            col0 = {W_B: 0, W_C: CONV_CH, W_U: 2 * CONV_CH, W_Q: 1536, W_K: 2048, W_V: 2560}
            w_in = hyb_w_in[0].rearrange("(k p) n -> p k n", p=P)
            w_loaded = [sem(f"hyb_w{b}_loaded") for b in range(6)]
            product = [loop_sem(f"hyb_product{b}", 1) for b in range(3)]
            raw_done = loop_sem("hyb_raw", 2)
            swapped = loop_sem("hyb_swapped", 2)
            rope_step = loop_sem("hyb_rope_step", 6)
            v_copied = loop_sem("hyb_v_copied", 1)
            chunk = loop_sem("hyb_conv_chunk", 12)
            c_copied = loop_sem("hyb_c_copied", 4)
            cu_done = loop_sem("hyb_cu_done", 4)
            tapped = loop_sem("hyb_conv_tap", 12)
            gated = loop_sem("hyb_gated", 4)
            scored = loop_sem("hyb_scores", 16)
            maxed = loop_sem("hyb_max", 16)
            exped = loop_sem("hyb_exp", 16)
            ratio_step = loop_sem("hyb_ratio_step", 16)
            combined = loop_sem("hyb_combined", 8)
            turned0 = loop_sem("hyb_probT_low", 8)
            turned1 = loop_sem("hyb_probT_high", 4)
            copied0 = loop_sem("hyb_probT_low_copied", 8)
            copied1 = loop_sem("hyb_probT_high_copied", 4)
            weighed = loop_sem("hyb_pv", 8)
            o_copied = loop_sem("hyb_o_copied", 8)
            sub_step = loop_sem("hyb_subln_step", 4)
            sub_rstd = loop_sem("hyb_subln_rstd", 1)
            o_turned = loop_sem("hyb_oT_psum", 2)
            o_stored = loop_sem("hyb_oT_copied", 2)
            passed = sem("hyb_passed")
            CH = 256
            conv = raw[:, :]
            gu = w_out[:, KD - 1, :]
            Kz = [qk[:, 1, :], qk[:, 2, :]]
            ofull = tmp[:, :].rearrange("p (n e) -> p n e", n=NB)
            osq = prob[:, 0:1024].rearrange("p (n e) -> p n e", n=NB)
            vv = val[:, :].rearrange("p (n e) -> p n e", n=NB)
            FIRST, BEHIND = 2, (1, 1, 1, 1, 1, 1, 1, 2)
            assert FIRST + 1 + sum(BEHIND) == 12

            def chunk_at(n):
                return FIRST + 1 + sum(BEHIND[:n])

            with nc.Block() as block:
                @block.sync
                def _(sp):
                    give_credits(sp)
                    with sp.Fori(1, 5) as j:
                        for b in range(6):
                            if b in (W_C, W_U, W_B):
                                sp.wait_ge({W_C: c_copied, W_U: cu_done, W_B: gated}[b], j * 4)
                            else:
                                sp.wait_ge(product[b], j)
                            sp.sem_inc(passed, 1)
                            sp.dma_start(slot[b], w_in[:, :, bass.ds((j - 1) * P + col0[b], P)]
                                         ).then_inc(w_loaded[b], 16)
                    wo = hyb_w_out[0].rearrange("(k p) n -> p k n", p=P)
                    sp.dma_start(w_out[:, 0:KD - 1, :], wo[:, 0:KD - 1, :]).then_inc(s_wo[0], 16)
                    sp.wait_ge(gated, 4 * 5)
                    sp.dma_start(w_out[:, KD - 1, :], wo[:, KD - 1, :]).then_inc(s_wo[0], 16)

                @block.tensor
                def _(pe):
                    def project(j, b, pair):
                        pe.wait_ge(w_loaded[b], j * 16)
                        for n in range(2):
                            for k in range(KD):
                                ins = nc.tensor.matmul(pair[:, 512 * n:512 * n + 512], slot[b][:, k, :],
                                                       hT[:, k, 512 * n:512 * n + 512],
                                                       start=(k == 0), stop=(k == KD - 1))
                        ins.then_inc(product[b], 1)

                    def project_chunk(j, i):
                        q, kind = i // 3, i % 3
                        b = (W_C, W_U, W_B)[kind]
                        pe.wait_ge(w_loaded[b], j * 16)
                        pe.wait_ge((gated, c_copied, cu_done)[kind], j * 4 + q + (1 if kind else 0))
                        for k in range(KD):
                            ins = nc.tensor.matmul(pU[:, 0:CH], slot[b][:, k, :], hT[:, k, q * CH:(q + 1) * CH],
                                                   start=(k == 0), stop=(k == KD - 1))
                        ins.then_inc(chunk, 1)

                    def swap_halves():
                        for n in range(2):
                            ins = nc.tensor.matmul(C[:, 512 * n:512 * n + 512], rot[:],
                                                   raw[:, 512 * n:512 * n + 512], start=True, stop=True)
                        ins.then_inc(swapped, 1)

                    def scores(j, n):
                        w = (n + 1) * P
                        for m in range(2):
                            pair = (A, B)[m]
                            pe.wait_ge(exped, j * 16 + 2 * (n - 1) + m + 1)
                            for f in range(0, w, 512):
                                f1 = min(w, f + 512)
                                nc.tensor.matmul(pair[:, f:f1], qk[:, 0, n * P:(n + 1) * P],
                                                 Kz[m][:, f:f1], start=True, stop=f1 != w)
                            nc.tensor.matmul(pair[:, w - P:w], ident_b[:], mask_b[:, 1, :],
                                             start=False, stop=True).then_inc(scored, 1)

                    def turn(j, n):
                        pe.wait_ge(combined, j * 8 + n + 1)
                        pe.wait_ge(copied0, j * 8 + n)
                        if n > 3:
                            pe.wait_ge(copied1, j * 4 + n - 4)
                        for b in range(n + 1):
                            ins = nc.tensor.transpose(C[:, b * P:(b + 1) * P], prob[:, b * P:(b + 1) * P], ident[:])
                            if b == min(n, 3):
                                ins.then_inc(turned0, 1)
                        if n > 3:
                            ins.then_inc(turned1, 1)

                    def weigh(j, n):
                        pe.wait_ge(copied0, j * 8 + n + 1)
                        pe.wait_ge(o_copied, j * 8 + n)
                        for b in range(n + 1):
                            if b == 4:
                                pe.wait_ge(copied1, j * 4 + n - 3)
                            ins = nc.tensor.matmul(pO[:, 0:P], probT[:, b * P:(b + 1) * P], vv[:, b, :],
                                                   start=(b == 0), stop=(b == n))
                        ins.then_inc(weighed, 1)

                    with pe.Fori(1, 5) as j:
                        pe.wait_ge(exped, j * 16)
                        project(j, W_Q, A)
                        project(j, W_K, B)
                        pe.wait_ge(o_stored, j * 2)
                        pe.wait_ge(raw_done, j * 2 + 1)
                        swap_halves()
                        pe.wait_ge(w_loaded[W_V], j * 16)
                        for n in range(NB):
                            for k in range(KD):
                                ins = nc.tensor.matmul(A[:, n * P:(n + 1) * P], hT[:, k, n * P:(n + 1) * P],
                                                       slot[W_V][:, k, :], start=(k == 0), stop=(k == KD - 1))
                        ins.then_inc(product[W_V], 1)
                        pe.wait_ge(rope_step, j * 6 + 2)
                        pe.wait_ge(raw_done, j * 2 + 2)
                        swap_halves()
                        for i in range(FIRST):
                            project_chunk(j, i)
                        pe.wait_ge(rope_step, j * 6 + 6)
                        pe.wait_ge(v_copied, j + 1)
                        scores(j, 0)
                        project_chunk(j, FIRST)
                        for n in range(NB):
                            turn(j, n)
                            if n + 1 < NB:
                                scores(j, n + 1)
                            weigh(j, n)
                            for i in range(BEHIND[n]):
                                project_chunk(j, chunk_at(n) + i)
                        pe.wait_ge(sub_step, j * 4 + 4)
                        pe.wait_ge(copied1, j * 4 + 4)
                        pe.wait_ge(copied0, j * 8 + 8)
                        for b in range(NB):
                            ins = nc.tensor.transpose(C[:, b * P:(b + 1) * P], ofull[:, b, :], ident[:])
                            if b % 4 == 3:
                                ins.then_inc(o_turned, 1)

                @block.scalar
                def _(act):
                    def c_chunk(j, i):
                        if i % 3 == 0:
                            q = i // 3
                            act.wait_ge(chunk, j * 12 + i + 1)
                            act.wait_ge(rope_step, j * 6 + 4)
                            act.wait_ge(swapped, j * 2 + 2)
                            nc.scalar.activation(conv[:, q * CH:(q + 1) * CH], pU[:, 0:CH],
                                                 ACT.Copy).then_inc(c_copied, 1)

                    def exps(j, n):
                        w = (n + 1) * P
                        for m in range(2):
                            act.wait_ge(maxed, j * 16 + 2 * n + m + 1)
                            if m == 0:
                                act.wait_ge(turned0, j * 8 + n)
                                act.wait_ge(combined, j * 8 + n)
                                if n > 4:
                                    act.wait_ge(turned1, j * 4 + n - 4)
                            nc.scalar.activation(prob[:, 1024 * m:1024 * m + w], (A, B)[m][:, 0:w],
                                                 ACT.Exp, bias=nmax[:, 0, m:m + 1],
                                                 accum_out=psum_[:, 0, m:m + 1]).then_inc(exped, 1)

                    with act.Fori(1, 5) as j:
                        act.wait_ge(product[W_Q], j + 1)
                        act.wait_ge(gated, j * 4)
                        nc.scalar.activation(raw[:, :], A, ACT.Copy, scale=0.125).then_inc(raw_done, 1)
                        act.wait_ge(product[W_K], j + 1)
                        act.wait_ge(rope_step, j * 6 + 1)
                        act.wait_ge(swapped, j * 2 + 1)
                        nc.scalar.activation(raw[:, :], B, ACT.Copy).then_inc(raw_done, 1)
                        act.wait_ge(product[W_V], j + 1)
                        nc.scalar.activation(val[:, :], A, ACT.Copy).then_inc(v_copied, 1)
                        for i in range(FIRST):
                            c_chunk(j, i)
                        act.wait_ge(sub_step, j * 4)
                        act.wait_ge(turned1, j * 4)
                        exps(j, 0)
                        c_chunk(j, FIRST)
                        for n in range(NB):
                            act.wait_ge(turned0, j * 8 + n + 1)
                            act.wait_ge(weighed, j * 8 + n)
                            w0 = min((n + 1) * P, 512)
                            nc.scalar.activation(probT[:, 0:w0], C[:, 0:w0], ACT.Copy).then_inc(copied0, 1)
                            if n + 1 < NB:
                                exps(j, n + 1)
                            for i in range(BEHIND[n]):
                                c_chunk(j, chunk_at(n) + i)
                        for h in range(2):
                            act.wait_ge(o_turned, j * 2 + h + 1)
                            nc.scalar.activation(
                                yT[:, bass.ds(j + 3, 1), 512 * h:512 * h + 512].rearrange("p a n -> p (a n)"),
                                C[:, 512 * h:512 * h + 512], ACT.Copy, scale=subln[:, 0:1]).then_inc(o_stored, 1)

                @block.gpsimd
                def _(pool):
                    with pool.Fori(1, 5) as j:
                        pool.wait_ge(sub_step, j * 4 + 3)
                        nc.gpsimd.tensor_tensor(rstd[:, :], msq[:, :], mhalf[:, :], ALU.pow).then_inc(sub_rstd, 1)

                @block.vector
                def _(dve):
                    def ub_chunk(j, i):
                        q, kind = i // 3, i % 3
                        c0, c1 = q * CH, (q + 1) * CH
                        if kind == 1:
                            dve.wait_ge(chunk, j * 12 + i + 1)
                            dve.wait_ge(c_copied, j * 4 + q + 1)
                            dve.wait_ge(gated, j * 4 + q)
                            nc.vector.tensor_tensor(gu[:, c0:c1], conv[:, c0:c1], pU[:, 0:CH],
                                                    ALU.mult).then_inc(cu_done, 1)
                            dve.wait_ge(cu_done, j * 4 + q + 1)
                            nc.vector.tensor_scalar(conv[:, c0:c1], gu[:, c0:c1], conv_w[:, 2, bass.ds(j - 1, 1)],
                                                    None, ALU.mult).then_inc(tapped, 1)
                            for t in (1, 2):
                                lo = max(c0, t)
                                dve.wait_ge(tapped, j * 12 + 3 * q + t)
                                nc.vector.scalar_tensor_tensor(conv[:, lo:c1], gu[:, lo - t:c1 - t],
                                                               conv_w[:, 2 - t, bass.ds(j - 1, 1)],
                                                               conv[:, lo:c1], ALU.mult, ALU.add
                                                               ).then_inc(tapped, 1)
                        if kind == 2:
                            dve.wait_ge(chunk, j * 12 + i + 1)
                            dve.wait_ge(tapped, j * 12 + 3 * q + 3)
                            nc.vector.tensor_tensor(
                                yT[:, bass.ds(j - 1, 1), c0:c1].rearrange("p a n -> p (a n)"),
                                conv[:, c0:c1], pU[:, 0:CH], ALU.mult).then_inc(gated, 1)

                    def maxima(j, n):
                        for m in range(2):
                            dve.wait_ge(scored, j * 16 + 2 * n + m + 1)
                            dve.wait_ge(exped, j * 16 + 2 * n + m - 1)
                            nc.vector.tensor_reduce(nmax[:, 0, m:m + 1], (A, B)[m][:, 0:(n + 1) * P], AX, ALU.max,
                                                    negate=True).then_inc(maxed, 1)

                    def combine(j, n):
                        w = (n + 1) * P
                        dve.wait_ge(exped, j * 16 + 2 * n + 2)
                        dve.wait_ge(o_copied, j * 8 + n)
                        nc.vector.reciprocal(rsum[:, 0, 0:2], psum_[:, 0, 0:2]).then_inc(ratio_step, 1)
                        dve.wait_ge(ratio_step, j * 16 + 2 * n + 1)
                        nc.vector.tensor_scalar(ratio[:, 0:1], psum_[:, 0, 0:1], rsum[:, 0, 1:2],
                                                neg_lam[:, 0:1], ALU.mult, ALU.mult).then_inc(ratio_step, 1)
                        dve.wait_ge(ratio_step, j * 16 + 2 * n + 2)
                        nc.vector.scalar_tensor_tensor(prob[:, 0:w], prob[:, 1024:1024 + w], ratio[:, 0:1],
                                                       prob[:, 0:w], ALU.mult, ALU.add).then_inc(combined, 1)

                    nc.vector.memset(Kz[0][64:128, :], 0.0)
                    nc.vector.memset(Kz[1][0:64, :], 0.0)
                    with dve.Fori(1, 5) as j:
                        for t, parts in enumerate([[(qk[:, 0, :], 0, P)], [(Kz[0], 0, 64), (Kz[1], 64, 128)]]):
                            dve.wait_ge(raw_done, j * 2 + t + 1)
                            dve.wait_ge(scored, j * 16)
                            for dst, lo, hi in parts:
                                ins = nc.vector.tensor_tensor(dst[lo:hi, :], raw[lo:hi, :], rope[lo:hi, 0, :], ALU.mult)
                            ins.then_inc(rope_step, 1)
                            dve.wait_ge(rope_step, j * 6 + 3 * t)
                            dve.wait_ge(o_turned, j * 2)
                            dve.wait_ge(swapped, j * 2 + t + 1)
                            nc.vector.tensor_tensor(tmp[:, :], C, rope[:, 1, :], ALU.mult).then_inc(rope_step, 1)
                            dve.wait_ge(rope_step, j * 6 + 3 * t + 2)
                            for dst, lo, hi in parts:
                                ins = nc.vector.tensor_tensor(dst[lo:hi, :], dst[lo:hi, :], tmp[lo:hi, :], ALU.add)
                            ins.then_inc(rope_step, 1)
                        for i in range(FIRST):
                            ub_chunk(j, i)
                        dve.wait_ge(rope_step, j * 6 + 6)
                        maxima(j, 0)
                        combine(j, 0)
                        ub_chunk(j, FIRST)
                        for n in range(NB):
                            w = (n + 1) * P
                            if n > 3:
                                dve.wait_ge(turned1, j * 4 + n - 3)
                                dve.wait_ge(weighed, j * 8 + n)
                                nc.vector.tensor_copy(probT[:, 512:w], C[:, 512:w]).then_inc(copied1, 1)
                            if n + 1 < NB:
                                maxima(j, n + 1)
                            dve.wait_ge(weighed, j * 8 + n + 1)
                            nc.vector.tensor_scalar(ofull[:, n, :], pO[:, 0:P], rsum[:, 0, 0:1], None,
                                                    ALU.mult).then_inc(o_copied, 1)
                            if n + 1 < NB:
                                combine(j, n + 1)
                                for i in range(BEHIND[n]):
                                    ub_chunk(j, chunk_at(n) + i)
                        dve.wait_ge(o_copied, j * 8 + 8)
                        dve.wait_ge(turned0, j * 8 + 8)
                        nc.vector.tensor_tensor(osq, ofull, ofull, ALU.mult).then_inc(sub_step, 1)
                        for i in range(BEHIND[NB - 1] - 1):
                            ub_chunk(j, chunk_at(NB - 1) + i)
                        dve.wait_ge(sub_step, j * 4 + 1)
                        nc.vector.tensor_reduce(ssum[:, :], osq, AX, ALU.add).then_inc(sub_step, 1)
                        dve.wait_ge(sub_step, j * 4 + 2)
                        nc.vector.tensor_scalar(msq[:, :], ssum[:, :], 1.0 / P, EPS, ALU.mult,
                                                ALU.add).then_inc(sub_step, 1)
                        dve.wait_ge(sub_rstd, j + 1)
                        nc.vector.tensor_tensor(ofull, ofull, rstd[:, :].unsqueeze(2).broadcast_to([P, NB, P]),
                                                ALU.mult).then_inc(sub_step, 1)
                        ub_chunk(j, 11)

        def window_attention():
            NBLK, NS = 6, 2 * NB
            K_, V_ = 4, 5
            w_loaded = [sem(f"win_w{b}_loaded") for b in range(NBLK)]
            product = [loop_sem(f"win_product{b}", 1) for b in range(NBLK)]
            vb_loaded = sem("win_v_bias_loaded")
            raw_done = loop_sem("win_raw", 5)
            swapped = loop_sem("win_swapped", 5)
            rope_step = loop_sem("win_rope_step", 15)
            v_added = loop_sem("win_v_added", 1)
            scored = loop_sem("win_scores", NS)
            max_step = loop_sem("win_max_step", NS)
            maxed = loop_sem("win_max", NS)
            sunk = loop_sem("win_sink_difference", NS)
            exped = loop_sem("win_exp", NS)
            sunk_e = loop_sem("win_sink_exp", NS)
            summed = loop_sem("win_sum", NS)
            inverted = loop_sem("win_reciprocal", NS)
            turned0 = loop_sem("win_probT_psum_low", NS)
            turned1 = loop_sem("win_probT_psum_high", NS)
            copied0 = loop_sem("win_probT_low_copied", NS)
            copied1 = loop_sem("win_probT_high_copied", NS)
            weighed = loop_sem("win_pv", NS)
            scaled = loop_sem("win_o_scaled", NS)
            o_turned = loop_sem("win_oT_psum", NS)
            o_stored = loop_sem("win_oT_stored", NS)
            passed = sem("win_passed")
            w_src = swa_w_qkv[0].rearrange("(k p) n -> p k n", p=P)
            flat = [W[:, 1024 * b:1024 * (b + 1)] for b in range(6)]
            Q = [qk[:, 0, :], qk[:, 1, :], qk[:, 2, :], flat[3]]
            Kz = [flat[4], flat[5]]
            vv = val[:, :].rearrange("p (n e) -> p n e", n=NB)
            vbias = prob[:, 1024:1152]
            osb = [tmp[:, 0:256], tmp[:, 256:512]]
            PR = [prob[:, 1024 * i:1024 * (i + 1)].rearrange("p (r w) -> p r w", r=4) for i in range(2)]
            SC = [t.rearrange("p (r w) -> p r w", r=4) for t in (A, B)]
            cT = C.rearrange("p (r w) -> p r w", r=4)
            pT = probT[:, :].rearrange("p (r w) -> p r w", r=4)

            def width(s):
                return P if s < 2 else 256

            def at(j, s):
                return j * NS + s + 1

            with nc.Block() as block:
                @block.sync
                def _(sp):
                    give_credits(sp)
                    with sp.Fori(1, 3) as j:
                        for b in range(NBLK):
                            sp.wait_ge(product[(b + 3) % 6], j + 1 if b >= 3 else j)
                            sp.sem_inc(passed, 1)
                            if b == V_:
                                sp.dma_start(slot[b % 3], w_src[:, :, bass.ds((j - 1) * P + 1280, P)]
                                             ).then_inc(w_loaded[b], 16)
                                sp.wait_ge(turned1, j * NS)
                                sp.sem_inc(passed, 1)
                                sp.dma_start(vbias, vectors[:, bass.ds((j - 1) * P + V_VB, P)]
                                             ).then_inc(vb_loaded, 16)
                            elif b == K_:
                                sp.dma_start(slot[b % 3], w_src[:, :, bass.ds((j - 1) * P + 1024, P)]
                                             ).then_inc(w_loaded[b], 16)
                            else:
                                for h in range(2):
                                    sp.dma_start(slot[b % 3][:, :, 64 * h:64 * h + 64],
                                                 w_src[:, :, bass.ds((j - 1) * 512 + 256 * h + 64 * b, 64)]
                                                 ).then_inc(w_loaded[b], 16)
                    load_out_matrix(swa_w_out[0], 2)(sp)

                @block.tensor
                def _(pe):
                    def project(j, b):
                        pe.wait_ge(w_loaded[b], j * (16 if b == K_ else 32))
                        for n in range(2):
                            for k in range(KD):
                                ins = nc.tensor.matmul((A, B)[b % 2][:, 512 * n:512 * n + 512], slot[b % 3][:, k, :],
                                                       hT[:, k, 512 * n:512 * n + 512],
                                                       start=(k == 0), stop=(k == KD - 1))
                        ins.then_inc(product[b], 1)

                    def swap_halves(j, t):
                        pe.wait_ge(raw_done, j * 5 + t + 1)
                        pe.wait_ge(rope_step, j * 15 + 3 * t - 1)
                        for n in range(2):
                            ins = nc.tensor.matmul(C[:, 512 * n:512 * n + 512], rot[:],
                                                   raw[:, 512 * n:512 * n + 512], start=True, stop=True)
                        ins.then_inc(swapped, 1)

                    def scores(j, s):
                        n, g, w = s // 2, s % 2, width(s)
                        pe.wait_ge(exped, at(j, s - 2))
                        k0 = (n - 1) * P if n else 0
                        for r in range(4):
                            nc.tensor.matmul(SC[s % 2][:, r, 0:w], Q[r][:, n * P:(n + 1) * P],
                                             Kz[g][:, k0:k0 + w], start=True, stop=False)
                            ins = nc.tensor.matmul(SC[s % 2][:, r, 0:w], ident_b[:],
                                                   mask_b[:, :, :].rearrange("p a b -> p (a b)")[:, 256 - w:256],
                                                   start=False, stop=True)
                        ins.then_inc(scored, 1)

                    def turn(j, s):
                        pe.wait_ge(exped, at(j, s))
                        for r in range(4):
                            if r == 0:
                                pe.wait_ge(copied0, at(j, s - 1))
                            if r == 2:
                                pe.wait_ge(copied1, at(j, s - 1))
                            for b in range(width(s) // P):
                                ins = nc.tensor.transpose(cT[:, r, b * P:(b + 1) * P],
                                                          PR[s % 2][:, r, b * P:(b + 1) * P], ident[:])
                            if r % 2:
                                ins.then_inc((turned0, turned1)[r // 2], 1)

                    def weigh(j, s):
                        n, g, nb = s // 2, s % 2, width(s) // P
                        pe.wait_ge(scaled, at(j, s - 1))
                        for r in range(4):
                            if r % 2 == 0:
                                pe.wait_ge((copied0, copied1)[r // 2], at(j, s))
                            for b in range(nb):
                                ins = nc.tensor.matmul(pO[:, r * 64:(r + 1) * 64], pT[:, r, b * P:(b + 1) * P],
                                                       vv[:, n - nb + 1 + b, 64 * g:64 * g + 64],
                                                       start=(b == 0), stop=(b == nb - 1))
                        ins.then_inc(weighed, 1)

                    def turn_out(j, s):
                        pe.wait_ge(scaled, at(j, s))
                        pe.wait_ge(o_stored, at(j, s - 1))
                        for b in range(2):
                            ins = nc.tensor.transpose(pU[:, b * P:(b + 1) * P],
                                                      osb[s % 2][:, b * P:(b + 1) * P], ident[:])
                        ins.then_inc(o_turned, 1)

                    with pe.Fori(1, 3) as j:
                        pe.wait_ge(exped, j * NS)
                        pe.wait_ge(copied1, j * NS)
                        pe.wait_ge(copied0, j * NS)
                        project(j, 0)
                        project(j, 1)
                        for b in range(2, NBLK):
                            swap_halves(j, b - 2)
                            if b == V_:
                                pe.wait_ge(w_loaded[V_], j * 16)
                                pe.wait_ge(raw_done, j * 5 + 4)
                                for n in range(NB):
                                    for k in range(KD):
                                        ins = nc.tensor.matmul(B[:, n * P:(n + 1) * P], hT[:, k, n * P:(n + 1) * P],
                                                               slot[V_ % 3][:, k, :],
                                                               start=(k == 0), stop=(k == KD - 1))
                                ins.then_inc(product[V_], 1)
                            else:
                                project(j, b)
                        swap_halves(j, 4)
                        pe.wait_ge(rope_step, j * 15 + 15)
                        pe.wait_ge(v_added, j + 1)
                        scores(j, 0)
                        scores(j, 1)
                        for s in range(NS):
                            turn(j, s)
                            if s + 2 < NS:
                                scores(j, s + 2)
                            if s:
                                turn_out(j, s - 1)
                            weigh(j, s)
                        turn_out(j, NS - 1)

                @block.scalar
                def _(act):
                    def exps(j, s):
                        w, i = width(s), s % 2
                        act.wait_ge(maxed, at(j, s))
                        act.wait_ge((turned0, turned1)[1], at(j, s - 2))
                        act.wait_ge(inverted, at(j, s - 2))
                        for r in range(4):
                            ins = nc.scalar.activation(PR[i][:, r, 0:w], SC[i][:, r, 0:w], ACT.Exp,
                                                       bias=nmax[:, i, r:r + 1], accum_out=psum_[:, i, r:r + 1])
                        ins.then_inc(exped, 1)
                        act.wait_ge(sunk, at(j, s))
                        nc.scalar.activation(sinkx[:, 2 + i, :], sinkx[:, i, :], ACT.Exp).then_inc(sunk_e, 1)

                    def store(j, s):
                        act.wait_ge(o_turned, at(j, s))
                        g, n = s % 2, s // 2
                        nc.scalar.activation(yT[:, bass.ds(4 * (j - 1) + 2 * g, 2), n * P:(n + 1) * P],
                                             pU[:, 0:256].rearrange("p (b n) -> p b n", b=2),
                                             ACT.Copy).then_inc(o_stored, 1)

                    with act.Fori(1, 3) as j:
                        for t in range(5):
                            act.wait_ge(product[t], j + 1)
                            act.wait_ge(rope_step, j * 15 + 3 * t - 2)
                            act.wait_ge(swapped, j * 5 + t)
                            bias = k_bias[:, bass.ds(j - 1, 1)] if t == K_ else q_bias[:, bass.ds(4 * (j - 1) + t, 1)]
                            nc.scalar.activation(raw[:, :], (A, B)[t % 2], ACT.Identity, bias=bias,
                                                 scale=1.0 if t == K_ else 0.125).then_inc(raw_done, 1)
                        act.wait_ge(v_added, j + 1)
                        exps(j, 0)
                        exps(j, 1)
                        for s in range(NS):
                            w = width(s)
                            act.wait_ge(turned0, at(j, s))
                            act.wait_ge(weighed, at(j, s - 1))
                            nc.scalar.activation(pT[:, 0:2, 0:w], cT[:, 0:2, 0:w], ACT.Copy).then_inc(copied0, 1)
                            if s:
                                store(j, s - 1)
                            if s + 2 < NS:
                                exps(j, s + 2)
                        store(j, NS - 1)

                @block.vector
                def _(dve):
                    def maxima(j, s):
                        w, i, g = width(s), s % 2, s % 2
                        dve.wait_ge(scored, at(j, s))
                        dve.wait_ge(exped, at(j, s - 2))
                        nc.vector.tensor_reduce(nmax[:, i, :], SC[i][:, :, 0:w], AX, ALU.max,
                                                negate=True).then_inc(max_step, 1)
                        dve.wait_ge(max_step, at(j, s))
                        nc.vector.tensor_tensor(nmax[:, i, :], nmax[:, i, :],
                                                sinks[:, 1, bass.ds(8 * (j - 1) + 4 * g, 4)],
                                                ALU.min).then_inc(maxed, 1)
                        dve.wait_ge(maxed, at(j, s))
                        dve.wait_ge(sunk_e, at(j, s - 2))
                        nc.vector.tensor_tensor(sinkx[:, i, :], nmax[:, i, :],
                                                sinks[:, 0, bass.ds(8 * (j - 1) + 4 * g, 4)],
                                                ALU.add).then_inc(sunk, 1)

                    nc.vector.memset(Kz[0][64:128, :], 0.0)
                    nc.vector.memset(Kz[1][0:64, :], 0.0)
                    with dve.Fori(1, 3) as j:
                        for t in range(5):
                            parts = [(Kz[0], 0, 64), (Kz[1], 64, 128)] if t == K_ else [(Q[t], 0, P)]
                            dve.wait_ge(raw_done, j * 5 + t + 1)
                            dve.wait_ge(scored, j * NS)
                            for dst, lo, hi in parts:
                                ins = nc.vector.tensor_tensor(dst[lo:hi, :], raw[lo:hi, :], rope[lo:hi, 0, :], ALU.mult)
                            ins.then_inc(rope_step, 1)
                            dve.wait_ge(swapped, j * 5 + t + 1)
                            dve.wait_ge(rope_step, j * 15 + 3 * t)
                            dve.wait_ge(o_turned, j * NS)
                            nc.vector.tensor_tensor(tmp[:, :], C, rope[:, 1, :], ALU.mult).then_inc(rope_step, 1)
                            dve.wait_ge(rope_step, j * 15 + 3 * t + 2)
                            for dst, lo, hi in parts:
                                ins = nc.vector.tensor_tensor(dst[lo:hi, :], dst[lo:hi, :], tmp[lo:hi, :], ALU.add)
                            ins.then_inc(rope_step, 1)
                        dve.wait_ge(product[V_], j + 1)
                        dve.wait_ge(vb_loaded, j * 16)
                        dve.wait_ge(weighed, j * NS)
                        nc.vector.tensor_tensor(vv, B.rearrange("p (n e) -> p n e", n=NB),
                                                vbias.unsqueeze(1).broadcast_to([P, NB, P]),
                                                ALU.add).then_inc(v_added, 1)
                        maxima(j, 0)
                        maxima(j, 1)
                        for s in range(NS):
                            w, i = width(s), s % 2
                            dve.wait_ge(exped, at(j, s))
                            dve.wait_ge(sunk_e, at(j, s))
                            nc.vector.tensor_tensor(psum_[:, i, :], psum_[:, i, :], sinkx[:, 2 + i, :],
                                                    ALU.add).then_inc(summed, 1)
                            dve.wait_ge(summed, at(j, s))
                            nc.vector.reciprocal(rsum[:, i, :], psum_[:, i, :]).then_inc(inverted, 1)
                            dve.wait_ge(turned1, at(j, s))
                            dve.wait_ge(weighed, at(j, s - 1))
                            nc.vector.tensor_copy(pT[:, 2:4, 0:w], cT[:, 2:4, 0:w]).then_inc(copied1, 1)
                            if s + 2 < NS:
                                maxima(j, s + 2)
                            dve.wait_ge(weighed, at(j, s))
                            dve.wait_ge(inverted, at(j, s))
                            dve.wait_ge(o_turned, at(j, s - 2))
                            nc.vector.tensor_tensor(osb[i].rearrange("p (r e) -> p r e", r=4),
                                                    pO[:, 0:256].rearrange("p (r e) -> p r e", r=4),
                                                    rsum[:, i, :].unsqueeze(2).broadcast_to([P, 4, 64]),
                                                    ALU.mult).then_inc(scaled, 1)

        def short_attention(name, windowed, w_src, w_next, n_steps, loops):
            nproj = 4 if windowed else 1
            w_loaded = [sem(name + f"_w{b}_loaded") for b in range(nproj)]
            product = [sem(name + f"_product{b}") for b in range(nproj)]
            raw_done = sem(name + "_raw")
            swapped = sem(name + "_swapped")
            rope_step = sem(name + "_rope_step")
            v_added = sem(name + "_v_added")
            scored = sem(name + "_scores")
            max_step = sem(name + "_max_step")
            maxed = sem(name + "_max")
            exped = sem(name + "_exp")
            sunk = sem(name + "_sink_difference")
            sunk_e = sem(name + "_sink_exp")
            recip_step = sem(name + "_recip_step")
            turned = sem(name + "_probT_psum")
            copied0 = sem(name + "_probT_low_copied")
            copied1 = sem(name + "_probT_high_copied")
            weighed = sem(name + "_pv")
            scaled = sem(name + "_o_scaled")
            o_turned = sem(name + "_oT_psum")
            o_stored = sem(name + "_oT_stored")
            s_bias = sem(name + "_v_bias_loaded")
            NS = n_steps
            ow = 64 if windowed else P
            vbias = val[:, 768:1024]
            if windowed:
                vv = val[:, 0:512].rearrange("p (n e) -> p n e", n=NB)
            osb = val[:, 512:768] if windowed else tmp[:, 0:512]
            PR = [prob[:, 0:1024].rearrange("p (r w) -> p r w", r=4),
                  prob[:, 1024:2048].rearrange("p (r w) -> p r w", r=4)]
            SC = [t.rearrange("p (r w) -> p r w", r=4) for t in (A, B)]

            def width(n):
                return P if windowed and n == 0 else 256

            with nc.Block() as block:
                @block.sync
                def _(sp):
                    if windowed:
                        sp.dma_start(vbias, swa_b_qkv[0, 1280:1536].partition_broadcast(P)).then_inc(s_bias, 16)
                    with sp.Fori(0, loops) as j:
                        for b in range(nproj):
                            sp.wait_ge(product[b], j)
                            if windowed and b == 2:
                                for i in range(2):
                                    sp.dma_start(slot[b][:, :, 64 * i:64 * i + 64],
                                                 w_src[:, :, bass.ds(j * 64 + 1024, 64)]).then_inc(w_loaded[b], 16)
                            elif windowed and b == 3:
                                sp.dma_start(slot[b][:, :, 0:64],
                                             w_src[:, :, bass.ds(j * 64 + 1280, 64)]).then_inc(w_loaded[b], 16)
                            elif windowed:
                                sp.dma_start(slot[b], w_src[:, :, bass.ds(j * 256 + b * P, P)]).then_inc(w_loaded[b], 16)
                            else:
                                sp.dma_start(slot[b], w_src[:, :, bass.ds(j * P, P)]).then_inc(w_loaded[b], 16)
                    w_next(sp)

                @block.tensor
                def _(pe):
                    def project(j, b, pair):
                        pe.wait_ge(w_loaded[b], (j * 16 + 16) * (2 if windowed and b == 2 else 1))
                        for n in range(2):
                            for k in range(KD):
                                ins = nc.tensor.matmul(pair[:, 512 * n:512 * n + 512], slot[b][:, k, :],
                                                       hT[:, k, 512 * n:512 * n + 512],
                                                       start=(k == 0), stop=(k == KD - 1))
                        ins.then_inc(product[b], 1)

                    def scores(j, n):
                        if n >= 2:
                            pe.wait_ge(exped, j * NS + n - 1)
                        sc, w = SC[n % 2], width(n)
                        for r in range(4):
                            if windowed:
                                lo = 64 * (r // 2)
                                k0 = (n - 1) * P if n else 0
                                nc.tensor.matmul(sc[:, r, 0:w], qk[lo:lo + 64, r % 2, n * P:(n + 1) * P],
                                                 qk[lo:lo + 64, 2, k0:k0 + w], start=True, stop=False)
                                ins = nc.tensor.matmul(sc[:, r, 0:w], ident_b[:],
                                                       mask_b[:, :, :].rearrange("p a b -> p (a b)")[:, 256 - w:256],
                                                       start=False, stop=True)
                            else:
                                q0 = (4 * n + r) * P
                                ins = nc.tensor.matmul(sc[:, r, :], qk[:, 0, q0:q0 + P],
                                                       memK[:, bass.ds(j, 1), :].rearrange("p a m -> p (a m)"),
                                                       start=True, stop=True)
                        ins.then_inc(scored, 1)

                    def turn(j, n):
                        pe.wait_ge(exped, j * NS + n + 1)
                        nb = width(n) // P
                        for r in range(4):
                            for b in range(nb):
                                ins = nc.tensor.transpose(C[:, (2 * r + b) * P:(2 * r + b + 1) * P],
                                                          PR[n % 2][:, r, b * P:(b + 1) * P], ident[:])
                            if r % 2:
                                ins.then_inc(turned, 1)

                    def weigh(j, n):
                        pe.wait_ge(copied0, j * NS + n + 1)
                        pe.wait_ge(copied1, j * NS + n + 1)
                        pe.wait_ge(scaled, j * NS + n)
                        nb = width(n) // P
                        for r in range(4):
                            for b in range(nb):
                                if windowed:
                                    v = vv[:, n - nb + 1 + b, :]
                                else:
                                    v = memV[:, b, bass.ds(j * P, P)]
                                ins = nc.tensor.matmul(pO[:, r * ow:(r + 1) * ow],
                                                       probT[:, (2 * r + b) * P:(2 * r + b + 1) * P], v,
                                                       start=(b == 0), stop=(b == nb - 1))
                        ins.then_inc(weighed, 1)

                    def turn_out(j, n):
                        pe.wait_ge(scaled, j * NS + n + 1)
                        pe.wait_ge(o_stored, j * NS + n)
                        for b in range(4 * ow // P):
                            ins = nc.tensor.transpose(pU[:, b * P:(b + 1) * P], osb[:, b * P:(b + 1) * P], ident[:])
                        ins.then_inc(o_turned, 1)

                    if windowed:
                        pe.wait_ge(s_bias, 16)
                    with pe.Fori(0, loops) as j:
                        pe.wait_ge(exped, j * NS)
                        if windowed:
                            project(j, 0, A)
                            project(j, 1, B)
                            for t in range(3):
                                pe.wait_ge(raw_done, j * 3 + t + 1)
                                if t:
                                    pe.wait_ge(rope_step, j * 9 + 3 * t - 1)
                                else:
                                    pe.wait_ge(copied0, j * NS)
                                    pe.wait_ge(copied1, j * NS)
                                for n in range(2):
                                    ins = nc.tensor.matmul(C[:, 512 * n:512 * n + 512], rot[:],
                                                           raw[:, 512 * n:512 * n + 512], start=True, stop=True)
                                ins.then_inc(swapped, 1)
                                if t == 0:
                                    project(j, 2, A)
                                if t == 1:
                                    pe.wait_ge(w_loaded[3], j * 16 + 16)
                                    for n in range(NB):
                                        for k in range(KD):
                                            ins = nc.tensor.matmul(B[:, n * 64:(n + 1) * 64],
                                                                   hT[:, k, n * P:(n + 1) * P],
                                                                   slot[3][:, k, 0:64],
                                                                   start=(k == 0), stop=(k == KD - 1))
                                    ins.then_inc(product[3], 1)
                            pe.wait_ge(rope_step, j * 9 + 9)
                            pe.wait_ge(v_added, j + 1)
                        else:
                            project(j, 0, A)
                            pe.wait_ge(raw_done, j + 1)
                        scores(j, 0)
                        for n in range(NS):
                            turn(j, n)
                            if n + 1 < NS:
                                scores(j, n + 1)
                            weigh(j, n)
                            turn_out(j, n)

                @block.scalar
                def _(act):
                    with act.Fori(0, loops) as j:
                        if windowed:
                            for t in range(3):
                                act.wait_ge(product[t], j + 1)
                                if t:
                                    act.wait_ge(rope_step, j * 9 + 3 * t - 2)
                                    act.wait_ge(swapped, j * 3 + t)
                                bias = k_bias[:, bass.ds(j, 1)] if t == 2 else q_bias[:, bass.ds(2 * j + t, 1)]
                                nc.scalar.activation(raw[:, :], B if t == 1 else A, ACT.Identity, bias=bias,
                                                     scale=1.0 if t == 2 else 0.125).then_inc(raw_done, 1)
                        else:
                            act.wait_ge(product[0], j + 1)
                            nc.scalar.activation(qk[:, 0, :], A, ACT.Copy, scale=float(P) ** -0.5).then_inc(raw_done, 1)
                        for n in range(NS):
                            w = width(n)
                            act.wait_ge(maxed, j * NS + n + 1)
                            if n >= 2:
                                act.wait_ge(turned, 2 * (j * NS + n - 1))
                            for r in range(4):
                                ins = nc.scalar.activation(PR[n % 2][:, r, 0:w], SC[n % 2][:, r, 0:w], ACT.Exp,
                                                           bias=nmax[:, n % 2, r:r + 1],
                                                           accum_out=psum_[:, n % 2, r:r + 1])
                            ins.then_inc(exped, 1)
                            if windowed:
                                act.wait_ge(sunk, j * NS + n + 1)
                                nc.scalar.activation(sinkx[:, 1, :], sinkx[:, 0, :], ACT.Exp).then_inc(sunk_e, 1)
                            act.wait_ge(turned, 2 * (j * NS + n) + 1)
                            act.wait_ge(weighed, j * NS + n)
                            src = C[:, 0:512].rearrange("p (r w) -> p r w", r=2)[:, :, 0:w]
                            dst = probT[:, 0:512].rearrange("p (r w) -> p r w", r=2)[:, :, 0:w]
                            nc.scalar.activation(dst, src, ACT.Copy).then_inc(copied0, 1)
                            act.wait_ge(o_turned, j * NS + n + 1)
                            if windowed:
                                nc.scalar.activation(yT[:, bass.ds(2 * j, 2), n * P:(n + 1) * P],
                                                     pU[:, 0:256].rearrange("p (b n) -> p b n", b=2),
                                                     ACT.Copy).then_inc(o_stored, 1)
                            else:
                                nc.scalar.activation(
                                    yT[:, bass.ds(j, 1), 512 * n:512 * n + 512].rearrange("p a n -> p (a n)"),
                                    pU[:, :], ACT.Copy).then_inc(o_stored, 1)

                @block.vector
                def _(dve):
                    if windowed:
                        dve.wait_ge(s_bias, 16)
                    with dve.Fori(0, loops) as j:
                        if windowed:
                            for t in range(3):
                                dve.wait_ge(raw_done, j * 3 + t + 1)
                                nc.vector.tensor_tensor(qk[:, t, :], raw[:, :], rope[:, 0, :],
                                                        ALU.mult).then_inc(rope_step, 1)
                                dve.wait_ge(swapped, j * 3 + t + 1)
                                dve.wait_ge(rope_step, j * 9 + 3 * t)
                                nc.vector.tensor_tensor(tmp[:, :], C, rope[:, 1, :], ALU.mult).then_inc(rope_step, 1)
                                dve.wait_ge(rope_step, j * 9 + 3 * t + 2)
                                nc.vector.tensor_tensor(qk[:, t, :], qk[:, t, :], tmp[:, :],
                                                        ALU.add).then_inc(rope_step, 1)
                            dve.wait_ge(product[3], j + 1)
                            vb = vbias[:, bass.ds(j * 64, 64)].unsqueeze(1).broadcast_to([P, NB, 64])
                            nc.vector.tensor_tensor(vv, B[:, 0:512].rearrange("p (n e) -> p n e", n=NB), vb,
                                                    ALU.add).then_inc(v_added, 1)
                        for n in range(NS):
                            w, i = width(n), n % 2
                            dve.wait_ge(scored, j * NS + n + 1)
                            if n >= 1:
                                dve.wait_ge(exped, j * NS + n)
                            ins = nc.vector.tensor_reduce(nmax[:, i, :], SC[i][:, :, 0:w], AX, ALU.max, negate=True)
                            if windowed:
                                ins.then_inc(max_step, 1)
                                dve.wait_ge(max_step, j * NS + n + 1)
                                nc.vector.tensor_tensor(nmax[:, i, :], nmax[:, i, :],
                                                        sinks[:, 1, bass.ds(j * 4, 4)], ALU.min).then_inc(maxed, 1)
                                dve.wait_ge(maxed, j * NS + n + 1)
                                nc.vector.tensor_tensor(sinkx[:, 0, :], nmax[:, i, :],
                                                        sinks[:, 0, bass.ds(j * 4, 4)], ALU.add).then_inc(sunk, 1)
                                dve.wait_ge(exped, j * NS + n + 1)
                                dve.wait_ge(sunk_e, j * NS + n + 1)
                                nc.vector.tensor_tensor(psum_[:, i, :], psum_[:, i, :], sinkx[:, 1, :],
                                                        ALU.add).then_inc(recip_step, 1)
                                dve.wait_ge(recip_step, 2 * (j * NS + n) + 1)
                            else:
                                ins.then_inc(maxed, 1)
                                dve.wait_ge(exped, j * NS + n + 1)
                            nc.vector.reciprocal(rsum[:, i, :], psum_[:, i, :]).then_inc(recip_step, 1)
                            dve.wait_ge(turned, 2 * (j * NS + n) + 2)
                            dve.wait_ge(weighed, j * NS + n)
                            src = C[:, 512:1024].rearrange("p (r w) -> p r w", r=2)[:, :, 0:w]
                            dst = probT[:, 512:1024].rearrange("p (r w) -> p r w", r=2)[:, :, 0:w]
                            nc.vector.tensor_copy(dst, src).then_inc(copied1, 1)
                            dve.wait_ge(weighed, j * NS + n + 1)
                            dve.wait_ge(recip_step, (2 if windowed else 1) * (j * NS + n + 1))
                            dve.wait_ge(o_turned, j * NS + n)
                            if windowed:
                                rb = rsum[:, i, :].rearrange("p (l i) -> p l i", l=2)
                                nc.vector.tensor_tensor(
                                    osb[:, 0:256].rearrange("p (i l e) -> p l i e", i=2, l=2),
                                    pO[:, 0:256].rearrange("p (l i e) -> p l i e", i=2, l=2),
                                    rb.unsqueeze(3).broadcast_to([P, 2, 2, 64]), ALU.mult).then_inc(scaled, 1)
                            else:
                                rb = rsum[:, i, :].unsqueeze(2).broadcast_to([P, 4, P])
                                nc.vector.tensor_tensor(osb.rearrange("p (r e) -> p r e", r=4),
                                                        pO[:, :].rearrange("p (r e) -> p r e", r=4), rb,
                                                        ALU.mult).then_inc(scaled, 1)

        def router(l, w_gu, w_dn):
            n_ = f"route{l}"
            ld = sem(n_ + "_loaded")
            lg = sem(n_ + "_logits")
            st = sem(n_ + "_step")
            ge1, ge2 = sem(n_ + "_group_exp"), sem(n_ + "_pair_exp")
            oh = sem(n_ + "_onehots")
            rk = sem(n_ + "_ranks")
            sl = sem(n_ + "_slot_onehots")
            sp_ = sem(n_ + "_slot_list")
            NP = 2 * NB
            at = [0]

            def room(*shape):
                n = math.prod(shape)
                v = yflat[:, at[0]:at[0] + n]
                at[0] += n
                if len(shape) == 2:
                    return v.rearrange("p (a b) -> p a b", a=shape[0])
                if len(shape) == 3:
                    return v.rearrange("p (a b c) -> p a b c", a=shape[0], b=shape[1])
                return v

            wr = room(KD, NG + NE)
            rb = room(NG + NE)
            lgt = room(NB, NG + NE)
            gmax, gsum, gmin = room(NB), room(NB), room(NB)
            gexp, geq, gcand, goh = (room(NB, NG) for _ in range(4))
            emask = room(NB, NE)
            top = room(2, NB)
            low = room(2, NB)
            eeq, ecand = room(NB, NE), room(NB, NE)
            oneh = room(2, NB, NE)
            both = room(NB, NE)
            pe2, w1 = room(NB), room(NB)
            cnt, nx, xe, base2 = room(NE), room(NE), room(NE), room(NE)
            over = room(NE, JT)
            rank = room(NB, NE)
            where, far = room(NB, NE), room(NB, NE)
            pos = room(2, NB)
            xcmp = room(XT, NE)
            xid = room(XT)
            half = room(XT // 2)
            wide = room(NP, NTT + 1)
            tile_oh = room(NP, NTT)
            tsum, rem = room(NP), room(NP)
            starts = room(NTT + 1)
            slot_oh = room(NP, TS)
            both_b = probT[:, 0:128].bitcast(BF16)
            assert at[0] <= KD * S
            R = pO
            with nc.Block() as block:
                @block.sync
                def _(sp):
                    sp.dma_start(wr[:, :, 0:NG], moe_w_group[l].rearrange("(k p) n -> p k n", p=P)).then_inc(ld, 16)
                    sp.dma_start(wr[:, :, NG:NG + NE],
                                 moe_w_router[l].rearrange("(k p) n -> p k n", p=P)).then_inc(ld, 16)
                    sp.dma_start(rb[:, 0:NG], moe_b_group[l].partition_broadcast(P)).then_inc(ld, 16)
                    sp.dma_start(rb[:, NG:NG + NE], moe_b_router[l].partition_broadcast(P)).then_inc(ld, 16)
                    load_expert(sp, l, 0, 0, w_gu, w_dn, lambda: None, lambda: None)

                @block.tensor
                def _(pe):
                    pe.wait_ge(ld, 64)
                    for c in range(NB):
                        for k in range(KD):
                            ins = nc.tensor.matmul(R[:, c * 36:(c + 1) * 36], hT[:, k, c * P:(c + 1) * P],
                                                   wr[:, k, :], start=(k == 0), stop=(k == KD - 1))
                    ins.then_inc(lg, 1)
                    pe.wait_ge(oh, 1)
                    for c in range(NB + 1):
                        for b in range(min(c + 1, NB)):
                            ins = nc.tensor.matmul(pU[:, c * NE:(c + 1) * NE],
                                                   (tri_b if b == c else ones_b)[:],
                                                   both_b[:, b * NE:(b + 1) * NE],
                                                   start=(b == 0), stop=(b == min(c, NB - 1)))
                    ins.then_inc(rk, 1)
                    pe.wait_ge(sl, 1)
                    for i in range(NP):
                        ins = nc.tensor.matmul(A[0:TS, 0:NTT], slot_oh[:, i, :], tile_oh[:, i, :],
                                               start=(i == 0), stop=(i == NP - 1))
                    ins.then_inc(sp_, 1)

                @block.scalar
                def _(act):
                    act.wait_ge(ge1, 1)
                    nc.scalar.activation(gexp, gexp, ACT.Exp).then_inc(ge1, 1)
                    act.wait_ge(ge2, 1)
                    nc.scalar.activation(pe2, pe2, ACT.Exp).then_inc(ge2, 1)

                @block.vector
                def _(dve):
                    done = [0]

                    def then(ins):
                        done[0] += 1
                        ins.then_inc(st, 1)
                        dve.wait_ge(st, done[0])

                    def bc(ap, n):
                        return ap.unsqueeze(2).broadcast_to([P, ap.shape[1], n])

                    def iota_bc(n, m):
                        return iota[:, 0:m].unsqueeze(1).broadcast_to([P, n, m])

                    dve.wait_ge(lg, 1)
                    dve.wait_ge(ld, 64)
                    then(nc.vector.tensor_tensor(lgt, R[:, 0:NB * 36].rearrange("p (c n) -> p c n", c=NB),
                                                 rb.unsqueeze(1).broadcast_to([P, NB, 36]), ALU.add))
                    then(nc.vector.tensor_reduce(gmax, lgt[:, :, 0:NG], AX, ALU.max))
                    nc.vector.tensor_tensor(gexp, lgt[:, :, 0:NG], bc(gmax, NG), ALU.subtract).then_inc(ge1, 1)

                    def first_of_max(values, best, eq, cand, least, onehot, n):
                        then(nc.vector.tensor_tensor(eq, values, bc(best, n), ALU.is_equal))
                        then(nc.vector.scalar_tensor_tensor(cand, eq, -1000.0, iota_bc(NB, n), ALU.mult, ALU.add))
                        then(nc.vector.tensor_reduce(least, cand, AX, ALU.min))
                        then(nc.vector.tensor_tensor(onehot, cand, bc(least, n), ALU.is_equal))

                    first_of_max(lgt[:, :, 0:NG], gmax, geq, gcand, gmin, goh, NG)
                    ohx = goh.unsqueeze(3).broadcast_to([P, NB, NG, EPG])
                    el = lgt[:, :, NG:NG + NE].rearrange("p c (g e) -> p c g e", g=NG)
                    em = emask.rearrange("p c (g e) -> p c g e", g=NG)
                    eq4 = eeq.rearrange("p c (g e) -> p c g e", g=NG)
                    for c in range(NB):
                        ohc = goh[:, c, :].unsqueeze(2).broadcast_to([P, NG, EPG])
                        nc.vector.tensor_tensor(em[:, c], el[:, c], ohc, ALU.mult)
                        ins = nc.vector.tensor_scalar(eq4[:, c], ohc, -NEG, NEG, ALU.mult, ALU.add)
                    then(ins)
                    then(nc.vector.tensor_tensor(emask, emask, eeq, ALU.add))
                    for i in range(2):
                        then(nc.vector.tensor_reduce(top[:, i, :], emask, AX, ALU.max))
                        first_of_max(emask, top[:, i, :], eeq, ecand, low[:, i, :], oneh[:, i], NE)
                        if i == 0:
                            then(nc.vector.scalar_tensor_tensor(emask, oneh[:, 0], 3.0 * NEG, emask,
                                                                ALU.mult, ALU.add))
                    then(nc.vector.tensor_tensor(both, oneh[:, 0], oneh[:, 1], ALU.add))
                    nc.vector.tensor_copy(both_b, both.rearrange("p c e -> p (c e)")).then_inc(oh, 1)
                    nc.vector.tensor_tensor(pe2, top[:, 1, :], top[:, 0, :], ALU.subtract).then_inc(ge2, 1)
                    dve.wait_ge(ge1, 2)
                    then(nc.vector.tensor_reduce(gsum, gexp, AX, ALU.add))
                    dve.wait_ge(ge2, 2)
                    then(nc.vector.tensor_scalar(w1, pe2, 1.0, None, ALU.add))
                    then(nc.vector.tensor_tensor(w1, w1, gsum, ALU.mult))
                    then(nc.vector.reciprocal(wgt[:, 0, :], w1))
                    then(nc.vector.tensor_tensor(wgt[:, 1, :], wgt[:, 0, :], pe2, ALU.mult))
                    dve.wait_ge(rk, 1)
                    nc.vector.tensor_copy(rank, pU[:, 0:NB * NE].rearrange("p (c e) -> p c e", c=NB))
                    then(nc.vector.tensor_copy(cnt, pU[:, NB * NE:(NB + 1) * NE]))
                    for t in range(JT):
                        ins = nc.vector.tensor_scalar(over[:, :, t], cnt, float((t + 1) * TS), None, ALU.is_gt)
                    then(ins)
                    then(nc.vector.tensor_reduce(nx, over, AX, ALU.add))
                    then(nc.vector.tensor_tensor_scan(xe, ones_b[:, 0:NE], nx, 0.0, ALU.mult, ALU.add))
                    then(nc.vector.tensor_tensor(base2, xe, nx, ALU.subtract))
                    then(nc.vector.tensor_scalar(base2, base2, float(NE - 1), float(TS), ALU.add, ALU.mult))
                    then(nc.vector.scalar_tensor_tensor(base2, iota[:, 0:NE], -float(TS), base2, ALU.mult, ALU.add))
                    then(nc.vector.tensor_scalar(half, iota[:, 0:XT // 2], 2.0, None, ALU.mult))
                    then(nc.vector.tensor_scalar(half, half, xe[:, NE - 1:NE], None, ALU.is_lt))
                    then(nc.vector.tensor_reduce(cnt[:, 0:1], half, AX, ALU.add))
                    then(nc.vector.tensor_scalar(nround[:], cnt[:, 0:1], float(NE // 2), None, ALU.add))
                    nc.vector.tensor_copy(tile_e[:, 0:NE], iota[:, 0:NE])
                    then(nc.vector.tensor_tensor(
                        xcmp, xe.unsqueeze(1).broadcast_to([P, XT, NE]),
                        iota[:, 0:XT].unsqueeze(2).broadcast_to([P, XT, NE]), ALU.is_le))
                    then(nc.vector.tensor_reduce(xid, xcmp, AX, ALU.add))
                    nc.vector.memset(tile_e[:, NT_MAX:NTT], 0)
                    then(nc.vector.tensor_scalar(tile_e[:, NE:NE + XT], xid, float(NE - 1), None, ALU.min))
                    then(nc.vector.tensor_scalar(far, rank, float(TS), None, ALU.is_ge))
                    then(nc.vector.tensor_tensor(far, far, base2.unsqueeze(1).broadcast_to([P, NB, NE]), ALU.mult))
                    then(nc.vector.tensor_tensor(where, rank, far, ALU.add))
                    then(nc.vector.scalar_tensor_tensor(where, iota_bc(NB, NE), float(TS), where,
                                                        ALU.mult, ALU.add))
                    for i in range(2):
                        then(nc.vector.tensor_tensor(far, where, oneh[:, i], ALU.mult))
                        then(nc.vector.tensor_reduce(pos[:, i, :], far, AX, ALU.add))
                    nc.vector.tensor_copy(pos_u[:, :, :], pos)
                    posf = pos.rearrange("p i c -> p (i c)")
                    then(nc.vector.tensor_scalar(starts, iota[:, 0:NTT + 1], float(TS), None, ALU.mult))
                    then(nc.vector.tensor_tensor(wide, bc(posf, NTT + 1),
                                                 starts.unsqueeze(1).broadcast_to([P, NP, NTT + 1]), ALU.is_ge))
                    then(nc.vector.tensor_reduce(tsum, wide, AX, ALU.add))
                    then(nc.vector.tensor_scalar(tsum, tsum, -1.0, -float(TS), ALU.add, ALU.mult))
                    then(nc.vector.tensor_tensor(rem, posf, tsum, ALU.add))
                    then(nc.vector.tensor_tensor(tile_oh, wide[:, :, 0:NTT], wide[:, :, 1:NTT + 1], ALU.subtract))
                    for i in range(2):
                        ti = tile_oh[:, i * NB:(i + 1) * NB, :]
                        ins = nc.vector.tensor_tensor(ti, ti, bc(tok_id[:, :], NTT), ALU.mult)
                    then(ins)
                    nc.vector.tensor_tensor(slot_oh, iota_bc(NP, TS), bc(rem, TS), ALU.is_equal).then_inc(sl, 1)
                    dve.wait_ge(sp_, 1)
                    nc.vector.tensor_copy(slots[0:TS, :], A[0:TS, 0:NTT]).then_inc(sl, 1)
                    dve.wait_ge(sl, 2)

        gu_set = [W[:, 0:8192].rearrange("p (k n) -> p k n", k=KD), hT]
        dn_set = [W[:, 8192:12288].rearrange("p (k n) -> p k n", k=4),
                  yflat[:, 4096:8192].rearrange("p (k n) -> p k n", k=4)]

        def load_expert(sp, l, e, s, s_gu, s_dn, before_gu, before_dn):
            wgu = moe_w_gate_up[l].rearrange("e (k p) f -> e p k f", p=P)
            wdn = moe_w_down[l].rearrange("e (k p) n -> e p k n", p=P)
            before_gu()
            for k in range(0, KD, 2):
                sp.dma_start(gu_set[s][:, k:k + 2, :],
                             wgu[bass.ds(e, 1), :, k:k + 2, :].rearrange("a p k f -> (a p) k f")
                             ).then_inc(s_gu[s], 16)
            before_dn()
            for k in range(0, 4, 2):
                sp.dma_start(dn_set[s][:, k:k + 2, :],
                             wdn[bass.ds(e, 1), :, k:k + 2, :].rearrange("a p k n -> (a p) k n")
                             ).then_inc(s_dn[s], 16)

        def experts(l, w_gu, w_dn):
            n_ = f"moe{l}"
            idx_ready = loop_sem(n_ + "_index", 2)
            gathered = [sem(n_ + f"_gathered{i}") for i in range(2)]
            x_turned = loop_sem(n_ + "_xT_psum", 4)
            x_ready = loop_sem(n_ + "_xT_ready", 4)
            gu_sum = loop_sem(n_ + "_gate_up", 8)
            silu_done = loop_sem(n_ + "_silu", 8)
            hid_done = loop_sem(n_ + "_hidden", 8)
            y_sum = loop_sem(n_ + "_y", 4)
            y0, y1 = loop_sem(n_ + "_y_low_copied", 2), loop_sem(n_ + "_y_high_copied", 2)
            stored = [loop_sem(n_ + f"_stored{i}", 16) for i in range(2)]
            passed = sem(n_ + "_passed")
            xg = [yflat[:, 0:1024], prob[:, 0:1024]]
            ysb = [yflat[:, 3072:4096], prob[:, 1024:2048]]
            xT = yflat[:, 1024:2048].rearrange("p (k n) -> p k n", k=KD)
            gate = yflat[:, 2048:2560].rearrange("p (f n) -> p f n", f=4)
            hid = yflat[:, 2560:3072].rearrange("p (f n) -> p f n", f=4)
            GU = [A[:, 0:512], A[:, 512:1024], B[:, 0:512], B[:, 512:1024]]
            Y = [C[:, 0:512], C[:, 512:1024]]
            T = [pO[:, :], pU[:, :]]

            def rounds(eng):
                return eng.value_load(nround[0:1, 0:1], min_val=NE // 2, max_val=NT_MAX // 2)

            with nc.Block() as block:
                @block.sync
                def _(sp):
                    give_credits(sp)

                    def load(v, s):
                        e = sp.value_load(tile_e[0:1, bass.ds(v - 2, 1)], min_val=0, max_val=NE - 1)
                        load_expert(sp, l, e, s, w_gu, w_dn,
                                    lambda: sp.wait_ge(gu_sum, (v - 1) * 4), lambda: sp.wait_ge(y_sum, (v - 1) * 2))

                    n = rounds(sp)
                    with sp.Fori(1, n) as r:
                        load(r * 2 + 1, 1)
                        load(r * 2 + 2, 0)
                    load(n * 2 + 1, 1)

                @block.gpsimd
                def _(pool):
                    def gather(at, i, register):
                        nc.gpsimd.tensor_copy(icol[0:TS, i:i + 1], slots[0:TS, bass.ds(at, 1)]).then_inc(idx_ready, 1)
                        pool.wait_ge(idx_ready, at + 3)
                        if register:
                            pool.sem_inc(passed, 1)
                        pool.indirect_dma_start(xg[i][0:TS, :], None, h_dram,
                                                bass.IndirectOffsetOnAxis(ap=icol[0:TS, i:i + 1], axis=0)
                                                ).then_inc(gathered[i], 16)

                    gather(0, 0, False)
                    gather(1, 1, False)
                    n = rounds(pool)
                    with pool.Fori(1, n + 1) as r:
                        for u in range(2):
                            v = r * 2 + u
                            pool.wait_ge(x_turned, (v + 1) * 2)
                            gather(v, u, True)
                    for u in range(2):
                        pool.wait_ge(gathered[u], n * 16 + 16)
                        pool.sem_inc(passed, 1)

                @block.tensor
                def _(pe):
                    def turn(i, count):
                        pe.wait_ge(gathered[i], count)
                        for h in range(2):
                            for b in range(4):
                                k = 4 * h + b
                                ins = nc.tensor.transpose(T[h][:, b * P:b * P + TS], xg[i][0:TS, k * P:(k + 1) * P],
                                                          ident[0:TS, 0:TS])
                            ins.then_inc(x_turned, 1)

                    turn(0, 16)
                    with pe.Fori(1, rounds(pe) + 1) as r:
                        for u in range(2):
                            v = r * 2 + u
                            pe.wait_ge(x_ready, (v + 1) * 2)
                            pe.wait_ge(hid_done, v * 4)
                            pe.wait_ge(w_gu[u], r * 64)
                            for f in range(4):
                                for i in range(2):
                                    for k in range(KD):
                                        c0 = i * EH + f * P
                                        ins = nc.tensor.matmul(GU[f][:, i * P:i * P + TS],
                                                               gu_set[u][:, k, c0:c0 + P], xT[:, k, 0:TS],
                                                               start=(k == 0), stop=(k == KD - 1))
                                ins.then_inc(gu_sum, 1)
                            turn(1 - u, (r + u) * 16)
                            pe.wait_ge(w_dn[u], r * 32)
                            pe.wait_ge(hid_done, v * 4 + 4)
                            for c in range(2):
                                pe.wait_ge((y0, y1)[c], v)
                                for f in range(4):
                                    ins = nc.tensor.matmul(Y[c][0:TS, :], hid[:, f, 0:TS],
                                                           dn_set[u][:, f, 512 * c:512 * c + 512],
                                                           start=(f == 0), stop=(f == 3))
                                ins.then_inc(y_sum, 1)

                @block.scalar
                def _(act):
                    n = rounds(act)
                    with act.Fori(1, n + 1) as r:
                        for u in range(2):
                            v = r * 2 + u
                            act.wait_ge(hid_done, v * 4)
                            for f in range(4):
                                act.wait_ge(gu_sum, v * 4 + f + 1)
                                nc.scalar.activation(gate[:, f, 0:TS], GU[f][:, 0:TS],
                                                     ACT.Silu).then_inc(silu_done, 1)
                            act.wait_ge(y_sum, v * 2 + 1)
                            act.wait_ge(stored[u], r * 16)
                            nc.scalar.activation(ysb[u][0:TS, 0:512], Y[0][0:TS, :], ACT.Copy).then_inc(y0, 1)
                            act.wait_ge(y0, v + 1)
                            act.wait_ge(y1, v + 1)
                            act.dma_start(y_dram[bass.ds((v - 2) * TS, TS), :], ysb[u][0:TS, :]
                                          ).then_inc(stored[u], 16)
                    for u in range(2):
                        act.wait_ge(stored[u], n * 16 + 16)
                        act.sem_inc(passed, 1)

                @block.vector
                def _(dve):
                    def keep(done):
                        for h in range(2):
                            dve.wait_ge(x_turned, done + h + 1)
                            g4 = gains[:, 3 + 3 * l, 4 * h:4 * h + 4].unsqueeze(2).broadcast_to([P, 4, TS])
                            nc.vector.tensor_tensor(
                                xT[:, 4 * h:4 * h + 4, 0:TS],
                                T[h].rearrange("p (k n) -> p k n", k=4)[:, :, 0:TS], g4,
                                ALU.mult).then_inc(x_ready, 1)

                    keep(4)
                    with dve.Fori(1, rounds(dve) + 1) as r:
                        for u in range(2):
                            v = r * 2 + u
                            dve.wait_ge(y_sum, v * 2)
                            for f in range(4):
                                dve.wait_ge(silu_done, v * 4 + f + 1)
                                nc.vector.tensor_tensor(hid[:, f, 0:TS], gate[:, f, 0:TS], GU[f][:, P:P + TS],
                                                        ALU.mult).then_inc(hid_done, 1)
                            dve.wait_ge(gu_sum, v * 4 + 4)
                            keep(v * 2 + 2)
                            dve.wait_ge(y_sum, v * 2 + 2)
                            dve.wait_ge(stored[u], r * 16)
                            nc.vector.tensor_copy(ysb[u][0:TS, 512:1024], Y[1][0:TS, :]).then_inc(y1, 1)

        def load_out_matrix(w, i):
            def go(sp):
                k = w.shape[0] // P
                sp.dma_start(w_out[:, 0:k, :], w.rearrange("(k p) n -> p k n", p=P)).then_inc(s_wo[i], 16)
            return go

        setup()
        end_phase()

        stream("memory", MB, memx, 0, "load", dst=memT)
        end_phase()
        memory_kv()
        end_phase()

        def rows_cleared(sp):
            sp.wait_ge(s_zero, 16 * XT)

        stream("in0", NB, xs, 1, "load", preload=rows_cleared)
        end_phase()
        hybrid()
        end_phase()
        stream("mix0", NB, xs, 2, "project", kin=KD, w_ready=(s_wo[0], 32))
        end_phase()
        short_attention("cross0", False, xattn_w_q[0].rearrange("(k p) n -> p k n", p=P),
                        load_out_matrix(xattn_w_o[0], 1), 2, XH)
        end_phase()
        stream("att0", NB, xs, 3, "project", kin=4, w_ready=(s_wo[1], 16), rows=True)
        end_phase()
        expert_w0 = [[sem(f"moe0_{w}_loaded{i}", keep=True) for i in range(2)] for w in ("gate_up", "down")]
        router(0, *expert_w0)
        end_phase()
        experts(0, *expert_w0)
        end_phase()
        stream("moe0_in", NB, xs, 4, "combine")
        end_phase()
        window_attention()
        end_phase()
        stream("mix1", NB, xs, 5, "project", kin=KD, w_ready=(s_wo[2], 16), bias=swa_b_out[0])
        end_phase()
        short_attention("cross1", False, xattn_w_q[1].rearrange("(k p) n -> p k n", p=P),
                        load_out_matrix(xattn_w_o[1], 3), 2, XH)
        end_phase()
        stream("att1", NB, xs, 6, "project", kin=4, w_ready=(s_wo[3], 16), rows=True)
        end_phase()
        expert_w1 = [[sem(f"moe1_{w}_loaded{i}", keep=True) for i in range(2)] for w in ("gate_up", "down")]
        router(1, *expert_w1)
        end_phase()
        experts(1, *expert_w1)
        end_phase()
        stream("moe1_in", NB, xs, 6, "combine", final=True)
        end_phase()


_INS = ["x", "mem", "mem_norm", "mem_w_kv", "norm_mix", "norm_xattn", "norm_ffn", "hyb_w_in",
        "hyb_conv_w", "diff_lambda", "diff_subln", "hyb_w_out", "swa_w_qkv", "swa_b_qkv", "swa_sinks",
        "swa_w_out", "swa_b_out", "xattn_w_q", "xattn_w_o", "moe_w_group", "moe_b_group",
        "moe_w_router", "moe_b_router", "moe_w_gate_up", "moe_w_down", "final_norm"]


def shape_constants():
    import numpy as np
    f = np.float32
    inv = f(500000.0) ** (-np.arange(0, 16, 2, dtype=f) / f(16))
    ang = (np.arange(S, dtype=f)[:, None] * inv.astype(f)[None, :]).astype(f)
    cos, sin = np.cos(ang).T.astype(f), np.sin(ang).T.astype(f)
    rope = np.zeros((P, 2, S), f)
    rope[:, 0] = 1.0
    swap = np.zeros((P, P), f)
    for h in (0, 64):
        rope[h:h + 8, 0] = rope[h + 8:h + 16, 0] = cos
        rope[h:h + 8, 1], rope[h + 8:h + 16, 1] = -sin, sin
        for i in range(8):
            swap[h + i, h + 8 + i] = swap[h + 8 + i, h + i] = 1.0
    r = np.arange(P)
    c = np.zeros((P, C_ALL), f)
    c[:, C_ID:C_ID + P] = np.eye(P)
    c[:, C_R:C_R + P] = swap
    c[:, C_TRI:C_TRI + P] = r[:, None] < r[None, :]
    c[:, C_CAUSAL:C_CAUSAL + P] = np.where(r[None, :] > r[:, None], NEG, 0.0)
    c[:, C_PREV:C_PREV + P] = np.where(r[None, :] <= r[:, None], NEG, 0.0)
    c[:, C_IOTA:C_IOTA + P] = r[None, :]
    c[:, C_TOK:C_TOK + NB] = r[:, None] + P * np.arange(NB)[None, :]
    return rope, c


def small_vectors(a):
    import numpy as np
    by_p = [np.reshape(g, (KD, P)).T for g in (a["mem_norm"], a["norm_mix"][0], a["norm_xattn"][0],
                                               a["norm_ffn"][0], a["norm_mix"][1], a["norm_xattn"][1],
                                               a["norm_ffn"][1])]
    by_p.append(np.reshape(a["hyb_conv_w"][0], (3 * 4, P)).T)
    by_p.append(np.reshape(a["diff_subln"], (1, P)).T)
    b = a["swa_b_qkv"][0]
    by_p.append(np.transpose(np.reshape(b[0:1024], (2, 2, 4, 64)), (1, 3, 0, 2)).reshape(P, 8))
    by_p.append(np.reshape(b[1024:1280], (2, P)).T)
    rows = [np.reshape(a["diff_lambda"][0], (1, 256)), np.reshape(a["swa_sinks"][0], (1, 16)),
            np.reshape(b[1280:1536], (1, 256))]
    return np.ascontiguousarray(np.concatenate(by_p + [np.repeat(r, P, axis=0) for r in rows], axis=1))


def kernel(**inputs):
    import numpy as _np
    import concourse.bacc as _bacc
    from concourse.bass_utils import run_bass_kernel_spmd as _run

    nc = _bacc.Bacc("TRN2", target_bir_lowering=False, num_devices=1)
    arrays, args = {}, []
    given = [(name, _np.ascontiguousarray(inputs[name])) for name in _INS]
    given += list(zip(("rope_tables", "constants"), shape_constants()))
    given.append(("vectors", small_vectors(dict(given))))
    for name, a in given:
        arrays[f"in_{name}_dram"] = a
        args.append(nc.dram_tensor(f"in_{name}_dram", a.shape, mybir.dt.from_np(a.dtype),
                                   kind="ExternalInput").ap())
    args.append(nc.dram_tensor("out_dram", (1, S, D), F32, kind="ExternalOutput").ap())
    build(nc, *args)
    r = _run(nc, [arrays], core_ids=[0])
    return r.results[0]["out_dram"]
```

```python
import math
from contextlib import ExitStack

import concourse.bass as bass
from concourse import mybir

P = 128
ALU = mybir.AluOpType
ACT = mybir.ActivationFunctionType
F32 = mybir.dt.float32
BF16 = mybir.dt.bfloat16
U32 = mybir.dt.uint32
I32 = mybir.dt.int32
AX = mybir.AxisListType.X

D = 1024
S = 1024
KD = D // P
NB = S // P
MEM = 256
MB = MEM // P
CONV_CH, DIFF_HEADS = 512, 4
SWA_KV = 4
XH = 4
NG, EPG, NE = 4, 8, 32
EH = 512
EPS = 1e-6
NEG = -1.0e30
LAMBDA_INIT = 0.8 - 0.6 * math.exp(-0.3 * 0)

TS = 128
XT = 2 * S // TS
NT_MAX = NE + XT
NTT = NT_MAX + 2
assert NE % 2 == 0 and XT % 2 == 0
JT = -(-S // TS) - 1

C_ID, C_R, C_TRI, C_CAUSAL, C_PREV, C_IOTA, C_TOK, C_ALL = 0, 128, 256, 384, 512, 640, 768, 776

V_GAIN = 0
V_CONV = V_GAIN + 7 * KD
V_SUBLN = V_CONV + 3 * 4
V_QB = V_SUBLN + 1
V_KB = V_QB + 8
V_LAM = V_KB + 2
V_SINK = V_LAM + 256
V_VB = V_SINK + 16
V_ALL = V_VB + 256
V_KEEP = V_LAM


def build(nc, x, mem, mem_norm, mem_w_kv, norm_mix, norm_xattn, norm_ffn, hyb_w_in, hyb_conv_w,
          diff_lambda, diff_subln, hyb_w_out, swa_w_qkv, swa_b_qkv, swa_sinks, swa_w_out, swa_b_out,
          xattn_w_q, xattn_w_o, moe_w_group, moe_b_group, moe_w_router, moe_b_router,
          moe_w_gate_up, moe_w_down, final_norm, rope_tables, constants, vectors, out):
    ctx = ExitStack()
    with ctx:
        def sb(name, shape, dt=F32):
            return ctx.enter_context(nc.sbuf_tensor(name, shape, dt))

        phase = []

        def sem(name, keep=False):
            s = nc.alloc_semaphore(name=name)
            if not keep:
                phase.append(s)
            return s

        credits = []

        def loop_sem(name, credit):
            s = sem(name)
            credits.append((s, credit))
            return s

        def give_credits(sp):
            for s, credit in credits:
                sp.sem_inc(s, credit)
            credits.clear()

        def end_phase():
            nc.clear_and_free_semaphores(list(phase))
            phase.clear()
            nc.all_engine_barrier()

        xs = sb("xs", [P, NB, D])
        hT = sb("hT", [P, KD, S])
        yT = sb("yT", [P, KD, S])
        W = sb("W", [P, 14336])
        prob = sb("prob", [P, 2048])
        probT = sb("probT", [P, 1024])
        qk = sb("qk", [P, 3, S])
        raw = sb("raw", [P, S])
        tmp = sb("tmp", [P, S])
        val = sb("val", [P, 1024])
        rope = sb("rope", [P, 2, S])
        memK = sb("memK", [P, XH, MEM])
        memV = sb("memV", [P, MB, XH * P])
        ident = sb("ident", [P, P])
        rot = sb("rot", [P, P])
        iota = sb("iota", [P, P])
        tok_id = sb("tok_id", [P, NB])
        ident_b = sb("ident_b", [P, P], BF16)
        tri_b = sb("tri_b", [P, P], BF16)
        ones_b = sb("ones_b", [P, P], BF16)
        mask_b = sb("mask_b", [P, 2, P], BF16)
        vecs = sb("vecs", [P, V_KEEP])
        gains = vecs[:, V_GAIN:V_CONV].rearrange("p (g k) -> p g k", g=7)
        conv_w = vecs[:, V_CONV:V_SUBLN].rearrange("p (t b) -> p t b", t=3)
        subln = vecs[:, V_SUBLN:V_QB]
        q_bias = vecs[:, V_QB:V_KB]
        k_bias = vecs[:, V_KB:V_KEEP]
        neg_lam = sb("neg_lam", [P, 1])
        lamv = sb("lamv", [P, 4])
        sinks = sb("sinks", [P, 2, 16])
        mhalf = sb("mhalf", [P, NB])
        ssum = sb("ssum", [P, NB])
        msq = sb("msq", [P, NB])
        rstd = sb("rstd", [P, NB])
        nmax = sb("nmax", [P, 2, 4])
        psum_ = sb("psum_", [P, 2, 4])
        rsum = sb("rsum", [P, 2, 4])
        ratio = sb("ratio", [P, 2])
        slots = raw[:, 0:NTT].bitcast(U32)
        pos_u = sb("pos_u", [P, 2, NB], U32)
        wgt = sb("wgt", [P, 2, NB])
        tile_e = raw[:, 128:128 + NTT].bitcast(I32)
        nround = sb("nround", [P, 1], I32)
        icol = sb("icol", [P, 2], U32)
        sinkx = sb("sinkx", [P, 4, 4])

        pairs = [ctx.enter_context(nc.psum_tensor(f"pair{i}", [P, 1024], F32)) for i in range(3)]
        A, B, C = (t[:, :] for t in pairs)
        pO = ctx.enter_context(nc.psum_tensor("pO", [P, 512], F32))
        pU = ctx.enter_context(nc.psum_tensor("pU", [P, 512], F32))

        h_dram = nc.dram_tensor("h_rows", [S, D], F32, kind="Internal").ap()
        y_dram = nc.dram_tensor("y_rows", [NT_MAX * TS, D], F32, kind="Internal").ap()

        slot = [W[:, 1024 * b:1024 * (b + 1)].rearrange("p (k n) -> p k n", k=KD) for b in range(6)]
        w_out = W[:, 6144:14336].rearrange("p (k n) -> p k n", k=KD)
        yflat = yT[:, :, :].rearrange("p k n -> p (k n)")

        s_const = sem("const_loaded", keep=True)
        s_x = [sem(f"x_loaded{c}", keep=True) for c in range(NB)]
        s_rope = sem("rope_loaded", keep=True)
        s_wo = [sem(f"out_weights_loaded{i}", keep=True) for i in range(4)]

        s_mem = [sem(f"memory_loaded{c}", keep=True) for c in range(MB)]
        s_kv = sem("memory_weights_loaded", keep=True)
        memx = yflat[:, 0:2048].rearrange("p (c n) -> p c n", c=MB)
        memT = yflat[:, 2048:4096].rearrange("p (k n) -> p k n", k=KD)

        def setup():
            cast_done = sem("constants_cast")
            lam1, lam2, lam3, lam4 = (sem(f"lambda_step{i}") for i in range(4))
            lraw = raw[:, 0:512].rearrange("p (a b) -> p a b", a=4)
            with nc.Block() as block:
                @block.sync
                def _(sp):
                    small = [
                        (ident[:], constants[:, C_ID:C_ID + P]), (rot[:], constants[:, C_R:C_R + P]),
                        (iota[:], constants[:, C_IOTA:C_IOTA + P]),
                        (tok_id[:], constants[:, C_TOK:C_TOK + NB]),
                        (prob[:, 0:384], constants[:, C_TRI:C_TRI + 384]),
                        (vecs[:, :], vectors[:, 0:V_KEEP]),
                        (raw[:, 0:272], vectors[:, V_LAM:V_VB]),
                    ]
                    for dst, src in small:
                        sp.dma_start(dst, src).then_inc(s_const, 16)
                    assert len(small) == 7
                    for c in range(MB):
                        sp.dma_start(memx[:, c, :], mem[0, c * P:(c + 1) * P, :]).then_inc(s_mem[c], 16)
                    for c in range(NB):
                        sp.dma_start(xs[:, c, :], x[0, c * P:(c + 1) * P, :]).then_inc(s_x[c], 16)
                    sp.dma_start(w_out, mem_w_kv.rearrange("(k p) n -> p k n", p=P)).then_inc(s_kv, 16)

                @block.vector
                def _(dve):
                    dve.wait_ge(s_const, 112)
                    nc.vector.tensor_copy(ident_b[:], ident[:])
                    nc.vector.tensor_copy(tri_b[:], prob[:, 0:128])
                    nc.vector.tensor_copy(mask_b[:, 1, :], prob[:, 128:256])
                    nc.vector.tensor_copy(mask_b[:, 0, :], prob[:, 256:384])
                    nc.vector.memset(ones_b[:], 1.0)
                    nc.vector.memset(mhalf[:], -0.5)
                    nc.vector.tensor_tensor(tmp[:, 0:64], raw[:, 0:64], raw[:, 64:128], ALU.mult)
                    nc.vector.tensor_tensor(tmp[:, 64:128], raw[:, 128:192], raw[:, 192:256],
                                            ALU.mult).then_inc(lam1, 1)
                    dve.wait_ge(lam1, 1)
                    nc.vector.tensor_reduce(lamv[:, 0:2], tmp[:, 0:128].rearrange("p (a b) -> p a b", a=2),
                                            AX, ALU.add).then_inc(lam2, 1)
                    dve.wait_ge(lam3, 1)
                    nc.vector.tensor_tensor(lamv[:, 0:1], lamv[:, 3:4], lamv[:, 2:3],
                                            ALU.subtract).then_inc(lam4, 1)
                    dve.wait_ge(lam4, 1)
                    nc.vector.tensor_scalar(neg_lam[:], lamv[:, 0:1], -LAMBDA_INIT, None, ALU.add)
                    nc.vector.tensor_scalar(subln[:], subln[:], 1.0 - LAMBDA_INIT, None, ALU.mult)
                    nc.vector.tensor_scalar(q_bias[:], q_bias[:], 0.125, None, ALU.mult)
                    for row, sign in ((0, 1.0), (1, -1.0)):
                        ins = nc.vector.tensor_scalar(
                            sinks[:, row, :], raw[:, 256:272], sign, None, ALU.mult)
                    ins.then_inc(cast_done, 1)
                    dve.wait_ge(cast_done, 1)

                @block.scalar
                def _(act):
                    act.wait_ge(lam2, 1)
                    nc.scalar.activation(lamv[:, 2:4], lamv[:, 0:2], ACT.Exp).then_inc(lam3, 1)

        def stream(name, nblk, src, gain, feed, kin=0, w_ready=None, bias=None, dst=hT, rows=False,
                   final=False, preload=None, pe_side=None, act_tail=None):
            x_done = sem(name + "_x_done")
            ss_done = sem(name + "_sumsq_done")
            ms_done = sem(name + "_meansq_done")
            rs_done = sem(name + "_rstd_done")
            xn_done = sem(name + "_normed")
            tr_done = sem(name + "_transposed")
            ev_done = sem(name + "_evacuated")
            pr_done = sem(name + "_projected")
            ad_done = sem(name + "_added")
            st_done = [sem(name + f"_rows_stored{i}") for i in range(2)]
            AHEAD = 4
            ga_done = [[sem(name + f"_gathered{j}{i}") for j in range(2)] for i in range(AHEAD)]
            gfin = sem(name + "_gain_loaded")
            xn = [prob[:, 0:1024], prob[:, 1024:2048]]
            got = [[yflat[:, 1024 * (2 * i + j):1024 * (2 * i + j + 1)] for j in range(2)] for i in range(AHEAD)]
            gbc = val[:, :]
            bbc = val[:, :]
            with nc.Block() as block:
                @block.sync
                def _(sp):
                    if final:
                        sp.dma_start(gbc, final_norm.partition_broadcast(P)).then_inc(gfin, 16)
                    if bias is not None:
                        sp.dma_start(bbc, bias.partition_broadcast(P)).then_inc(gfin, 16)
                    if preload:
                        preload(sp)
                    if rows:
                        for c in range(nblk):
                            sp.wait_ge(xn_done, c + 1)
                            sp.dma_start(h_dram[c * P:(c + 1) * P, :], xn[c % 2]).then_inc(st_done[c % 2], 16)
                    if final:
                        for c in range(nblk):
                            sp.wait_ge(xn_done, c + 1)
                            sp.dma_start(out[0, c * P:(c + 1) * P, :], xn[c % 2]).then_inc(st_done[c % 2], 16)
                    if rows or final:
                        for i in range(2):
                            sp.wait_ge(st_done[i], 16 * (nblk // 2))

                @block.gpsimd
                def _(pool):
                    def gather(c):
                        if c >= AHEAD:
                            pool.wait_ge(x_done, c - AHEAD + 1)
                        for j in range(2):
                            pool.indirect_dma_start(
                                got[c % AHEAD][j], None, y_dram,
                                bass.IndirectOffsetOnAxis(ap=pos_u[:, j, c:c + 1], axis=0),
                            ).then_inc(ga_done[c % AHEAD][j], 16)

                    if feed == "combine":
                        for c in range(AHEAD):
                            gather(c)
                    for c in range(nblk):
                        pool.wait_ge(ms_done, c + 1)
                        nc.gpsimd.tensor_tensor(rstd[:, c:c + 1], msq[:, c:c + 1], mhalf[:, 0:1],
                                                ALU.pow).then_inc(rs_done, 1)
                        if feed == "combine" and c + AHEAD < nblk:
                            gather(c + AHEAD)

                @block.scalar
                def _(act):
                    for c in range(nblk):
                        if feed == "load":
                            act.wait_ge((s_x if src is xs else s_mem)[c], 16)
                        else:
                            act.wait_ge(x_done, c + 1)
                        if c:
                            act.wait_ge(ss_done, c)
                        nc.scalar.activation(tmp[:, :], src[:, c, :], ACT.Square,
                                             accum_out=ssum[:, c:c + 1]).then_inc(ss_done, 1)
                    if act_tail:
                        act_tail(act)

                @block.vector
                def _(dve):
                    if final or bias is not None:
                        dve.wait_ge(gfin, 16)

                    def evacuate(c):
                        for h in range(2):
                            dve.wait_ge(tr_done, 2 * c + h + 1)
                            g4 = gains[:, gain, 4 * h:4 * h + 4].unsqueeze(2).broadcast_to([P, 4, P])
                            nc.vector.tensor_tensor(
                                dst[:, 4 * h:4 * h + 4, c * P:(c + 1) * P],
                                C[:, 512 * h:512 * h + 512].rearrange("p (k n) -> p k n", k=4), g4,
                                ALU.mult).then_inc(ev_done, 1)

                    def produce(c):
                        if feed == "project":
                            for h in range(2):
                                xh = src[:, c, 512 * h:512 * h + 512]
                                if bias is not None:
                                    nc.vector.tensor_tensor(xh, xh, bbc[:, 512 * h:512 * h + 512],
                                                            ALU.add).then_inc(ad_done, 1)
                                    dve.wait_ge(ad_done, 2 * c + h + 1)
                                dve.wait_ge(pr_done, 2 * c + h + 1)
                                ins = nc.vector.tensor_tensor(xh, xh, (A, B)[c % 2][:, 512 * h:512 * h + 512], ALU.add)
                            ins.then_inc(x_done, 1)
                        if feed == "combine":
                            for j in range(2):
                                dve.wait_ge(ga_done[c % AHEAD][j], 16 * (c // AHEAD + 1))
                                if j:
                                    dve.wait_ge(ad_done, c + 1)
                                ins = nc.vector.scalar_tensor_tensor(
                                    src[:, c, :], got[c % AHEAD][j], wgt[:, j, c:c + 1], src[:, c, :],
                                    ALU.mult, ALU.add)
                                ins.then_inc(x_done if j else ad_done, 1)

                    def mean_square(c):
                        dve.wait_ge(ss_done, c + 1)
                        nc.vector.tensor_scalar(msq[:, c:c + 1], ssum[:, c:c + 1], 1.0 / D, EPS,
                                                ALU.mult, ALU.add).then_inc(ms_done, 1)

                    def normed(c):
                        dve.wait_ge(rs_done, c + 1)
                        if c >= 2:
                            if not final:
                                dve.wait_ge(tr_done, 2 * (c - 1))
                            if rows or final:
                                dve.wait_ge(st_done[c % 2], 16 * (c // 2))
                        if final:
                            nc.vector.scalar_tensor_tensor(xn[c % 2], src[:, c, :], rstd[:, c:c + 1], gbc,
                                                           ALU.mult, ALU.mult).then_inc(xn_done, 1)
                        else:
                            nc.vector.tensor_scalar(xn[c % 2], src[:, c, :], rstd[:, c:c + 1], None,
                                                    ALU.mult).then_inc(xn_done, 1)

                    if feed == "project":
                        for c in range(nblk):
                            produce(c)
                            if c and not final:
                                evacuate(c - 1)
                            mean_square(c)
                            normed(c)
                    else:
                        for c in range(nblk + 1):
                            if c < nblk:
                                produce(c)
                            if c:
                                normed(c - 1)
                            if c >= 2 and not final:
                                evacuate(c - 2)
                            if c < nblk:
                                mean_square(c)
                    if not final:
                        evacuate(nblk - 1)

                @block.tensor
                def _(pe):
                    def transposes(c):
                        pe.wait_ge(xn_done, c + 1)
                        for h in range(2):
                            if c:
                                pe.wait_ge(ev_done, 2 * (c - 1) + h + 1)
                            for b in range(4):
                                k = 4 * h + b
                                ins = nc.tensor.transpose(C[:, k * P:(k + 1) * P],
                                                          xn[c % 2][:, k * P:(k + 1) * P], ident[:])
                            ins.then_inc(tr_done, 1)

                    if feed == "project":
                        pe.wait_ge(*w_ready)
                    for c in range(nblk):
                        if feed == "project":
                            if c >= 2:
                                pe.wait_ge(x_done, c - 1)
                            for h in range(2):
                                for k in range(kin):
                                    ins = nc.tensor.matmul((A, B)[c % 2][:, 512 * h:512 * h + 512],
                                                           yT[:, k, c * P:(c + 1) * P],
                                                           w_out[:, k, 512 * h:512 * h + 512],
                                                           start=(k == 0), stop=(k == kin - 1))
                                ins.then_inc(pr_done, 1)
                            if c and not final:
                                transposes(c - 1)
                        elif not final:
                            transposes(c)
                        if pe_side:
                            pe_side(pe, c)
                    if feed == "project" and not final:
                        transposes(nblk - 1)

        mkv_done = sem("memkv_product", keep=True)

        def memory_kv(pe, block):
            c = block - 2
            if c == 0:
                pe.wait_ge(s_kv, 16)
            if 0 <= c < XH:
                for k in range(KD):
                    ins = nc.tensor.matmul((A, B)[c // 2][:, 512 * (c % 2):512 * (c % 2) + MEM],
                                           w_out[:, k, c * P:(c + 1) * P], memT[:, k, :],
                                           start=(k == 0), stop=(k == KD - 1))
                ins.then_inc(mkv_done, 1)
            elif XH <= c < XH + MB:
                m = c - XH
                for k in range(KD):
                    ins = nc.tensor.matmul((pO, pU)[m][:, :], memT[:, k, m * P:(m + 1) * P],
                                           w_out[:, k, 512:1024], start=(k == 0), stop=(k == KD - 1))
                ins.then_inc(mkv_done, 1)

        def keep_memory_kv(act):
            for h in range(XH):
                act.wait_ge(mkv_done, h + 1)
                nc.scalar.activation(memK[:, h, :], (A, B)[h // 2][:, 512 * (h % 2):512 * (h % 2) + MEM], ACT.Copy)
            for m in range(MB):
                act.wait_ge(mkv_done, XH + m + 1)
                nc.scalar.activation(memV[:, m, :], (pO, pU)[m][:, :], ACT.Copy)

        W_Q, W_K, W_V, W_C, W_U, W_B = range(6)
        hyb_col = (1536, 2048, 2560, CONV_CH, 2 * CONV_CH, 0)
        hyb_w_loaded = [sem(f"hyb_w{b}_loaded", keep=True) for b in range(6)]

        def load_first_hybrid(sp):
            for b in range(6):
                sp.dma_start(slot[b], hyb_w_in[0].rearrange("(k p) n -> p k n", p=P)[:, :, hyb_col[b]:hyb_col[b] + P]
                             ).then_inc(hyb_w_loaded[b], 16)

        def hybrid():
            w_in = hyb_w_in[0].rearrange("(k p) n -> p k n", p=P)
            w_loaded = hyb_w_loaded
            product = [loop_sem(f"hyb_product{b}", 1) for b in range(3)]
            raw_done = loop_sem("hyb_raw", 2)
            swapped = loop_sem("hyb_swapped", 2)
            rope_step = loop_sem("hyb_rope_step", 6)
            v_copied = loop_sem("hyb_v_copied", 1)
            chunk = loop_sem("hyb_conv_chunk", 12)
            c_copied = loop_sem("hyb_c_copied", 4)
            cu_done = loop_sem("hyb_cu_done", 4)
            tapped = loop_sem("hyb_conv_tap", 12)
            gated = loop_sem("hyb_gated", 4)
            scored = loop_sem("hyb_scores", 16)
            maxed = loop_sem("hyb_max", 16)
            exped = loop_sem("hyb_exp", 16)
            ratio_step = loop_sem("hyb_ratio_step", 16)
            combined = loop_sem("hyb_combined", 8)
            turned0 = loop_sem("hyb_probT_low", 8)
            turned1 = loop_sem("hyb_probT_high", 4)
            copied0 = loop_sem("hyb_probT_low_copied", 8)
            copied1 = loop_sem("hyb_probT_high_copied", 4)
            weighed = loop_sem("hyb_pv", 8)
            o_copied = loop_sem("hyb_o_copied", 8)
            sub_step = loop_sem("hyb_subln_step", 4)
            sub_rstd = loop_sem("hyb_subln_rstd", 1)
            o_turned = loop_sem("hyb_oT_psum", 2)
            o_stored = loop_sem("hyb_oT_copied", 2)
            passed = sem("hyb_passed")
            CH = 256
            conv = raw[:, :]
            gu = w_out[:, KD - 1, :]
            Kz = [qk[:, 1, :], qk[:, 2, :]]
            ofull = tmp[:, :].rearrange("p (n e) -> p n e", n=NB)
            osq = prob[:, 0:1024].rearrange("p (n e) -> p n e", n=NB)
            vv = val[:, :].rearrange("p (n e) -> p n e", n=NB)
            FIRST, BEHIND = 2, (1, 1, 1, 1, 1, 1, 1, 2)
            assert FIRST + 1 + sum(BEHIND) == 12

            def chunk_at(n):
                return FIRST + 1 + sum(BEHIND[:n])

            with nc.Block() as block:
                @block.sync
                def _(sp):
                    give_credits(sp)
                    with sp.Fori(1, 4) as j:
                        for b in range(6):
                            if b in (W_C, W_U, W_B):
                                sp.wait_ge({W_C: c_copied, W_U: cu_done, W_B: gated}[b], j * 4 + 4)
                            else:
                                sp.wait_ge(product[b], j + 1)
                            sp.sem_inc(passed, 1)
                            sp.dma_start(slot[b], w_in[:, :, bass.ds(j * P + hyb_col[b], P)]
                                         ).then_inc(w_loaded[b], 16)
                    wo = hyb_w_out[0].rearrange("(k p) n -> p k n", p=P)
                    sp.dma_start(w_out[:, 0:KD - 1, :], wo[:, 0:KD - 1, :]).then_inc(s_wo[0], 16)
                    sp.wait_ge(gated, 4 * 5)
                    sp.dma_start(w_out[:, KD - 1, :], wo[:, KD - 1, :]).then_inc(s_wo[0], 16)

                @block.tensor
                def _(pe):
                    def project(j, b, pair):
                        pe.wait_ge(w_loaded[b], j * 16)
                        for n in range(2):
                            for k in range(KD):
                                ins = nc.tensor.matmul(pair[:, 512 * n:512 * n + 512], slot[b][:, k, :],
                                                       hT[:, k, 512 * n:512 * n + 512],
                                                       start=(k == 0), stop=(k == KD - 1))
                        ins.then_inc(product[b], 1)

                    def project_chunk(j, i):
                        q, kind = i // 3, i % 3
                        b = (W_C, W_U, W_B)[kind]
                        pe.wait_ge(w_loaded[b], j * 16)
                        pe.wait_ge((gated, c_copied, cu_done)[kind], j * 4 + q + (1 if kind else 0))
                        for k in range(KD):
                            ins = nc.tensor.matmul(pU[:, 0:CH], slot[b][:, k, :], hT[:, k, q * CH:(q + 1) * CH],
                                                   start=(k == 0), stop=(k == KD - 1))
                        ins.then_inc(chunk, 1)

                    def swap_halves():
                        for n in range(2):
                            ins = nc.tensor.matmul(C[:, 512 * n:512 * n + 512], rot[:],
                                                   raw[:, 512 * n:512 * n + 512], start=True, stop=True)
                        ins.then_inc(swapped, 1)

                    def scores(j, n):
                        w = (n + 1) * P
                        for m in range(2):
                            pair = (A, B)[m]
                            pe.wait_ge(exped, j * 16 + 2 * (n - 1) + m + 1)
                            for f in range(0, w, 512):
                                f1 = min(w, f + 512)
                                nc.tensor.matmul(pair[:, f:f1], qk[:, 0, n * P:(n + 1) * P],
                                                 Kz[m][:, f:f1], start=True, stop=f1 != w)
                            nc.tensor.matmul(pair[:, w - P:w], ident_b[:], mask_b[:, 1, :],
                                             start=False, stop=True).then_inc(scored, 1)

                    def turn(j, n):
                        pe.wait_ge(combined, j * 8 + n + 1)
                        pe.wait_ge(copied0, j * 8 + n)
                        if n > 3:
                            pe.wait_ge(copied1, j * 4 + n - 4)
                        for b in range(n + 1):
                            ins = nc.tensor.transpose(C[:, b * P:(b + 1) * P], prob[:, b * P:(b + 1) * P], ident[:])
                            if b == min(n, 3):
                                ins.then_inc(turned0, 1)
                        if n > 3:
                            ins.then_inc(turned1, 1)

                    def weigh(j, n):
                        pe.wait_ge(copied0, j * 8 + n + 1)
                        pe.wait_ge(o_copied, j * 8 + n)
                        for b in range(n + 1):
                            if b == 4:
                                pe.wait_ge(copied1, j * 4 + n - 3)
                            ins = nc.tensor.matmul(pO[:, 0:P], probT[:, b * P:(b + 1) * P], vv[:, b, :],
                                                   start=(b == 0), stop=(b == n))
                        ins.then_inc(weighed, 1)

                    with pe.Fori(1, 5) as j:
                        pe.wait_ge(exped, j * 16)
                        project(j, W_Q, A)
                        project(j, W_K, B)
                        pe.wait_ge(o_stored, j * 2)
                        pe.wait_ge(raw_done, j * 2 + 1)
                        swap_halves()
                        pe.wait_ge(w_loaded[W_V], j * 16)
                        for n in range(NB):
                            for k in range(KD):
                                ins = nc.tensor.matmul(A[:, n * P:(n + 1) * P], hT[:, k, n * P:(n + 1) * P],
                                                       slot[W_V][:, k, :], start=(k == 0), stop=(k == KD - 1))
                        ins.then_inc(product[W_V], 1)
                        pe.wait_ge(rope_step, j * 6 + 2)
                        pe.wait_ge(raw_done, j * 2 + 2)
                        swap_halves()
                        for i in range(FIRST):
                            project_chunk(j, i)
                        pe.wait_ge(rope_step, j * 6 + 6)
                        pe.wait_ge(v_copied, j + 1)
                        scores(j, 0)
                        project_chunk(j, FIRST)
                        for n in range(NB):
                            turn(j, n)
                            if n + 1 < NB:
                                scores(j, n + 1)
                            weigh(j, n)
                            for i in range(BEHIND[n]):
                                project_chunk(j, chunk_at(n) + i)
                        pe.wait_ge(sub_step, j * 4 + 4)
                        pe.wait_ge(copied1, j * 4 + 4)
                        pe.wait_ge(copied0, j * 8 + 8)
                        for b in range(NB):
                            ins = nc.tensor.transpose(C[:, b * P:(b + 1) * P], ofull[:, b, :], ident[:])
                            if b % 4 == 3:
                                ins.then_inc(o_turned, 1)

                @block.scalar
                def _(act):
                    def c_chunk(j, i):
                        if i % 3 == 0:
                            q = i // 3
                            act.wait_ge(chunk, j * 12 + i + 1)
                            act.wait_ge(rope_step, j * 6 + 4)
                            act.wait_ge(swapped, j * 2 + 2)
                            nc.scalar.activation(conv[:, q * CH:(q + 1) * CH], pU[:, 0:CH],
                                                 ACT.Copy).then_inc(c_copied, 1)

                    def exps(j, n):
                        w = (n + 1) * P
                        for m in range(2):
                            act.wait_ge(maxed, j * 16 + 2 * n + m + 1)
                            if m == 0:
                                act.wait_ge(turned0, j * 8 + n)
                                act.wait_ge(combined, j * 8 + n)
                                if n > 4:
                                    act.wait_ge(turned1, j * 4 + n - 4)
                            nc.scalar.activation(prob[:, 1024 * m:1024 * m + w], (A, B)[m][:, 0:w],
                                                 ACT.Exp, bias=nmax[:, 0, m:m + 1],
                                                 accum_out=psum_[:, 0, m:m + 1]).then_inc(exped, 1)

                    with act.Fori(1, 5) as j:
                        act.wait_ge(product[W_Q], j + 1)
                        act.wait_ge(gated, j * 4)
                        nc.scalar.activation(raw[:, :], A, ACT.Copy, scale=0.125).then_inc(raw_done, 1)
                        act.wait_ge(product[W_K], j + 1)
                        act.wait_ge(rope_step, j * 6 + 1)
                        act.wait_ge(swapped, j * 2 + 1)
                        nc.scalar.activation(raw[:, :], B, ACT.Copy).then_inc(raw_done, 1)
                        act.wait_ge(product[W_V], j + 1)
                        nc.scalar.activation(val[:, :], A, ACT.Copy).then_inc(v_copied, 1)
                        for i in range(FIRST):
                            c_chunk(j, i)
                        act.wait_ge(sub_step, j * 4)
                        act.wait_ge(turned1, j * 4)
                        exps(j, 0)
                        c_chunk(j, FIRST)
                        for n in range(NB):
                            act.wait_ge(turned0, j * 8 + n + 1)
                            act.wait_ge(weighed, j * 8 + n)
                            w0 = min((n + 1) * P, 512)
                            nc.scalar.activation(probT[:, 0:w0], C[:, 0:w0], ACT.Copy).then_inc(copied0, 1)
                            if n + 1 < NB:
                                exps(j, n + 1)
                            for i in range(BEHIND[n]):
                                c_chunk(j, chunk_at(n) + i)
                        for h in range(2):
                            act.wait_ge(o_turned, j * 2 + h + 1)
                            nc.scalar.activation(
                                yT[:, bass.ds(j + 3, 1), 512 * h:512 * h + 512].rearrange("p a n -> p (a n)"),
                                C[:, 512 * h:512 * h + 512], ACT.Copy, scale=subln[:, 0:1]).then_inc(o_stored, 1)

                @block.gpsimd
                def _(pool):
                    with pool.Fori(1, 5) as j:
                        pool.wait_ge(sub_step, j * 4 + 3)
                        nc.gpsimd.tensor_tensor(rstd[:, :], msq[:, :], mhalf[:, :], ALU.pow).then_inc(sub_rstd, 1)

                @block.vector
                def _(dve):
                    def ub_chunk(j, i):
                        q, kind = i // 3, i % 3
                        c0, c1 = q * CH, (q + 1) * CH
                        if kind == 1:
                            dve.wait_ge(chunk, j * 12 + i + 1)
                            dve.wait_ge(c_copied, j * 4 + q + 1)
                            dve.wait_ge(gated, j * 4 + q)
                            nc.vector.tensor_tensor(gu[:, c0:c1], conv[:, c0:c1], pU[:, 0:CH],
                                                    ALU.mult).then_inc(cu_done, 1)
                            dve.wait_ge(cu_done, j * 4 + q + 1)
                            nc.vector.tensor_scalar(conv[:, c0:c1], gu[:, c0:c1], conv_w[:, 2, bass.ds(j - 1, 1)],
                                                    None, ALU.mult).then_inc(tapped, 1)
                            for t in (1, 2):
                                lo = max(c0, t)
                                dve.wait_ge(tapped, j * 12 + 3 * q + t)
                                nc.vector.scalar_tensor_tensor(conv[:, lo:c1], gu[:, lo - t:c1 - t],
                                                               conv_w[:, 2 - t, bass.ds(j - 1, 1)],
                                                               conv[:, lo:c1], ALU.mult, ALU.add
                                                               ).then_inc(tapped, 1)
                        if kind == 2:
                            dve.wait_ge(chunk, j * 12 + i + 1)
                            dve.wait_ge(tapped, j * 12 + 3 * q + 3)
                            nc.vector.tensor_tensor(
                                yT[:, bass.ds(j - 1, 1), c0:c1].rearrange("p a n -> p (a n)"),
                                conv[:, c0:c1], pU[:, 0:CH], ALU.mult).then_inc(gated, 1)

                    def maxima(j, n):
                        for m in range(2):
                            dve.wait_ge(scored, j * 16 + 2 * n + m + 1)
                            dve.wait_ge(exped, j * 16 + 2 * n + m - 1)
                            nc.vector.tensor_reduce(nmax[:, 0, m:m + 1], (A, B)[m][:, 0:(n + 1) * P], AX, ALU.max,
                                                    negate=True).then_inc(maxed, 1)

                    def combine(j, n):
                        w = (n + 1) * P
                        dve.wait_ge(exped, j * 16 + 2 * n + 2)
                        dve.wait_ge(o_copied, j * 8 + n)
                        nc.vector.reciprocal(rsum[:, 0, 0:2], psum_[:, 0, 0:2]).then_inc(ratio_step, 1)
                        dve.wait_ge(ratio_step, j * 16 + 2 * n + 1)
                        nc.vector.tensor_scalar(ratio[:, 0:1], psum_[:, 0, 0:1], rsum[:, 0, 1:2],
                                                neg_lam[:, 0:1], ALU.mult, ALU.mult).then_inc(ratio_step, 1)
                        dve.wait_ge(ratio_step, j * 16 + 2 * n + 2)
                        nc.vector.scalar_tensor_tensor(prob[:, 0:w], prob[:, 1024:1024 + w], ratio[:, 0:1],
                                                       prob[:, 0:w], ALU.mult, ALU.add).then_inc(combined, 1)

                    nc.vector.memset(Kz[0][64:128, :], 0.0)
                    nc.vector.memset(Kz[1][0:64, :], 0.0)
                    dve.wait_ge(s_rope, 16)
                    with dve.Fori(1, 5) as j:
                        for t, parts in enumerate([[(qk[:, 0, :], 0, P)], [(Kz[0], 0, 64), (Kz[1], 64, 128)]]):
                            dve.wait_ge(raw_done, j * 2 + t + 1)
                            dve.wait_ge(scored, j * 16)
                            for dst, lo, hi in parts:
                                ins = nc.vector.tensor_tensor(dst[lo:hi, :], raw[lo:hi, :], rope[lo:hi, 0, :], ALU.mult)
                            ins.then_inc(rope_step, 1)
                            dve.wait_ge(rope_step, j * 6 + 3 * t)
                            dve.wait_ge(o_turned, j * 2)
                            dve.wait_ge(swapped, j * 2 + t + 1)
                            nc.vector.tensor_tensor(tmp[:, :], C, rope[:, 1, :], ALU.mult).then_inc(rope_step, 1)
                            dve.wait_ge(rope_step, j * 6 + 3 * t + 2)
                            for dst, lo, hi in parts:
                                ins = nc.vector.tensor_tensor(dst[lo:hi, :], dst[lo:hi, :], tmp[lo:hi, :], ALU.add)
                            ins.then_inc(rope_step, 1)
                        for i in range(FIRST):
                            ub_chunk(j, i)
                        dve.wait_ge(rope_step, j * 6 + 6)
                        maxima(j, 0)
                        combine(j, 0)
                        ub_chunk(j, FIRST)
                        for n in range(NB):
                            w = (n + 1) * P
                            if n > 3:
                                dve.wait_ge(turned1, j * 4 + n - 3)
                                dve.wait_ge(weighed, j * 8 + n)
                                nc.vector.tensor_copy(probT[:, 512:w], C[:, 512:w]).then_inc(copied1, 1)
                            if n + 1 < NB:
                                maxima(j, n + 1)
                            dve.wait_ge(weighed, j * 8 + n + 1)
                            nc.vector.tensor_scalar(ofull[:, n, :], pO[:, 0:P], rsum[:, 0, 0:1], None,
                                                    ALU.mult).then_inc(o_copied, 1)
                            if n + 1 < NB:
                                combine(j, n + 1)
                                for i in range(BEHIND[n]):
                                    ub_chunk(j, chunk_at(n) + i)
                        dve.wait_ge(o_copied, j * 8 + 8)
                        dve.wait_ge(turned0, j * 8 + 8)
                        nc.vector.tensor_tensor(osq, ofull, ofull, ALU.mult).then_inc(sub_step, 1)
                        for i in range(BEHIND[NB - 1] - 1):
                            ub_chunk(j, chunk_at(NB - 1) + i)
                        dve.wait_ge(sub_step, j * 4 + 1)
                        nc.vector.tensor_reduce(ssum[:, :], osq, AX, ALU.add).then_inc(sub_step, 1)
                        dve.wait_ge(sub_step, j * 4 + 2)
                        nc.vector.tensor_scalar(msq[:, :], ssum[:, :], 1.0 / P, EPS, ALU.mult,
                                                ALU.add).then_inc(sub_step, 1)
                        dve.wait_ge(sub_rstd, j + 1)
                        nc.vector.tensor_tensor(ofull, ofull, rstd[:, :].unsqueeze(2).broadcast_to([P, NB, P]),
                                                ALU.mult).then_inc(sub_step, 1)
                        ub_chunk(j, 11)

        NBLK, K_, V_ = 6, 4, 5
        win_w_loaded = [sem(f"win_w{b}_loaded", keep=True) for b in range(NBLK)]

        def load_window(sp, j, b):
            w_src = swa_w_qkv[0].rearrange("(k p) n -> p k n", p=P)
            if b in (K_, V_):
                c0 = (j - 1) * P + 1024 + 256 * (b - K_)
                sp.dma_start(slot[b % 3], w_src[:, :, c0:c0 + P]).then_inc(win_w_loaded[b], 16)
            else:
                for h in range(2):
                    c0 = (j - 1) * 512 + 256 * h + 64 * b
                    sp.dma_start(slot[b % 3][:, :, 64 * h:64 * h + 64],
                                 w_src[:, :, c0:c0 + 64]).then_inc(win_w_loaded[b], 16)

        def load_first_window(sp):
            for b in range(3):
                load_window(sp, 1, b)

        def window_attention():
            NS = 2 * NB
            w_loaded = win_w_loaded
            product = [loop_sem(f"win_product{b}", 1) for b in range(NBLK)]
            vb_loaded = sem("win_v_bias_loaded")
            raw_done = loop_sem("win_raw", 5)
            swapped = loop_sem("win_swapped", 5)
            rope_step = loop_sem("win_rope_step", 15)
            v_added = loop_sem("win_v_added", 1)
            scored = loop_sem("win_scores", NS)
            max_step = loop_sem("win_max_step", NS)
            maxed = loop_sem("win_max", NS)
            sunk = loop_sem("win_sink_difference", NS)
            exped = loop_sem("win_exp", NS)
            sunk_e = loop_sem("win_sink_exp", NS)
            summed = loop_sem("win_sum", NS)
            inverted = loop_sem("win_reciprocal", NS)
            turned0 = loop_sem("win_probT_psum_low", NS)
            turned1 = loop_sem("win_probT_psum_high", NS)
            copied0 = loop_sem("win_probT_low_copied", NS)
            copied1 = loop_sem("win_probT_high_copied", NS)
            weighed = loop_sem("win_pv", NS)
            scaled = loop_sem("win_o_scaled", NS)
            o_turned = loop_sem("win_oT_psum", NS)
            o_stored = loop_sem("win_oT_stored", NS)
            flat = [W[:, 1024 * b:1024 * (b + 1)] for b in range(6)]
            Q = [qk[:, 0, :], qk[:, 1, :], qk[:, 2, :], flat[3]]
            Kz = [flat[4], flat[5]]
            vv = val[:, :].rearrange("p (n e) -> p n e", n=NB)
            vbias = prob[:, 1024:1152]
            osb = [tmp[:, 0:256], tmp[:, 256:512]]
            PR = [prob[:, 1024 * i:1024 * (i + 1)].rearrange("p (r w) -> p r w", r=4) for i in range(2)]
            SC = [t.rearrange("p (r w) -> p r w", r=4) for t in (A, B)]
            cT = C.rearrange("p (r w) -> p r w", r=4)
            pT = probT[:, :].rearrange("p (r w) -> p r w", r=4)

            def width(s):
                return P if s < 2 else 256

            def at(j, s):
                return j * NS + s + 1

            with nc.Block() as block:
                @block.sync
                def _(sp):
                    give_credits(sp)
                    for j, b in [(j, b) for j in (1, 2) for b in range(NBLK)][3:]:
                        sp.wait_ge(product[(b + 3) % 6], j + 1 if b >= 3 else j)
                        load_window(sp, j, b)
                        if b == V_:
                            sp.wait_ge(turned1, j * NS)
                            sp.dma_start(vbias, vectors[:, (j - 1) * P + V_VB:j * P + V_VB]
                                         ).then_inc(vb_loaded, 16)
                    load_out_matrix(swa_w_out[0], 2)(sp)

                @block.tensor
                def _(pe):
                    def project(j, b):
                        pe.wait_ge(w_loaded[b], j * (16 if b == K_ else 32))
                        for n in range(2):
                            for k in range(KD):
                                ins = nc.tensor.matmul((A, B)[b % 2][:, 512 * n:512 * n + 512], slot[b % 3][:, k, :],
                                                       hT[:, k, 512 * n:512 * n + 512],
                                                       start=(k == 0), stop=(k == KD - 1))
                        ins.then_inc(product[b], 1)

                    def swap_halves(j, t):
                        pe.wait_ge(raw_done, j * 5 + t + 1)
                        pe.wait_ge(rope_step, j * 15 + 3 * t - 1)
                        for n in range(2):
                            ins = nc.tensor.matmul(C[:, 512 * n:512 * n + 512], rot[:],
                                                   raw[:, 512 * n:512 * n + 512], start=True, stop=True)
                        ins.then_inc(swapped, 1)

                    def scores(j, s):
                        n, g, w = s // 2, s % 2, width(s)
                        pe.wait_ge(exped, at(j, s - 2))
                        k0 = (n - 1) * P if n else 0
                        for r in range(4):
                            nc.tensor.matmul(SC[s % 2][:, r, 0:w], Q[r][:, n * P:(n + 1) * P],
                                             Kz[g][:, k0:k0 + w], start=True, stop=False)
                            ins = nc.tensor.matmul(SC[s % 2][:, r, 0:w], ident_b[:],
                                                   mask_b[:, :, :].rearrange("p a b -> p (a b)")[:, 256 - w:256],
                                                   start=False, stop=True)
                        ins.then_inc(scored, 1)

                    def turn(j, s):
                        pe.wait_ge(exped, at(j, s))
                        for r in range(4):
                            if r == 0:
                                pe.wait_ge(copied0, at(j, s - 1))
                            if r == 2:
                                pe.wait_ge(copied1, at(j, s - 1))
                            for b in range(width(s) // P):
                                ins = nc.tensor.transpose(cT[:, r, b * P:(b + 1) * P],
                                                          PR[s % 2][:, r, b * P:(b + 1) * P], ident[:])
                            if r % 2:
                                ins.then_inc((turned0, turned1)[r // 2], 1)

                    def weigh(j, s):
                        n, g, nb = s // 2, s % 2, width(s) // P
                        pe.wait_ge(scaled, at(j, s - 1))
                        for r in range(4):
                            if r % 2 == 0:
                                pe.wait_ge((copied0, copied1)[r // 2], at(j, s))
                            for b in range(nb):
                                ins = nc.tensor.matmul(pO[:, r * 64:(r + 1) * 64], pT[:, r, b * P:(b + 1) * P],
                                                       vv[:, n - nb + 1 + b, 64 * g:64 * g + 64],
                                                       start=(b == 0), stop=(b == nb - 1))
                        ins.then_inc(weighed, 1)

                    def turn_out(j, s):
                        pe.wait_ge(scaled, at(j, s))
                        pe.wait_ge(o_stored, at(j, s - 1))
                        for b in range(2):
                            ins = nc.tensor.transpose(pU[:, b * P:(b + 1) * P],
                                                      osb[s % 2][:, b * P:(b + 1) * P], ident[:])
                        ins.then_inc(o_turned, 1)

                    with pe.Fori(1, 3) as j:
                        pe.wait_ge(exped, j * NS)
                        pe.wait_ge(copied1, j * NS)
                        pe.wait_ge(copied0, j * NS)
                        project(j, 0)
                        project(j, 1)
                        for b in range(2, V_):
                            swap_halves(j, b - 2)
                            project(j, b)
                        swap_halves(j, 3)
                        pe.wait_ge(w_loaded[V_], j * 16)
                        pe.wait_ge(raw_done, j * 5 + 4)
                        for n in range(NB):
                            if n == NB // 2:
                                swap_halves(j, K_)
                            for k in range(KD):
                                ins = nc.tensor.matmul(B[:, n * P:(n + 1) * P], hT[:, k, n * P:(n + 1) * P],
                                                       slot[V_ % 3][:, k, :], start=(k == 0), stop=(k == KD - 1))
                        ins.then_inc(product[V_], 1)
                        pe.wait_ge(rope_step, j * 15 + 15)
                        scores(j, 0)
                        pe.wait_ge(v_added, j + 1)
                        scores(j, 1)
                        for s in range(NS):
                            turn(j, s)
                            if s + 2 < NS:
                                scores(j, s + 2)
                            if s:
                                turn_out(j, s - 1)
                            weigh(j, s)
                        turn_out(j, NS - 1)

                @block.scalar
                def _(act):
                    def exps(j, s):
                        w, i = width(s), s % 2
                        act.wait_ge(maxed, at(j, s))
                        act.wait_ge((turned0, turned1)[1], at(j, s - 2))
                        act.wait_ge(inverted, at(j, s - 2))
                        for r in range(4):
                            ins = nc.scalar.activation(PR[i][:, r, 0:w], SC[i][:, r, 0:w], ACT.Exp,
                                                       bias=nmax[:, i, r:r + 1], accum_out=psum_[:, i, r:r + 1])
                        ins.then_inc(exped, 1)
                        act.wait_ge(sunk, at(j, s))
                        nc.scalar.activation(sinkx[:, 2 + i, :], sinkx[:, i, :], ACT.Exp).then_inc(sunk_e, 1)

                    def store(j, s):
                        act.wait_ge(o_turned, at(j, s))
                        g, n = s % 2, s // 2
                        nc.scalar.activation(yT[:, bass.ds(4 * (j - 1) + 2 * g, 2), n * P:(n + 1) * P],
                                             pU[:, 0:256].rearrange("p (b n) -> p b n", b=2),
                                             ACT.Copy).then_inc(o_stored, 1)

                    with act.Fori(1, 3) as j:
                        for t in range(5):
                            act.wait_ge(product[t], j + 1)
                            act.wait_ge(rope_step, j * 15 + 3 * t - 2)
                            act.wait_ge(swapped, j * 5 + t)
                            bias = k_bias[:, bass.ds(j - 1, 1)] if t == K_ else q_bias[:, bass.ds(4 * (j - 1) + t, 1)]
                            nc.scalar.activation(raw[:, :], (A, B)[t % 2], ACT.Identity, bias=bias,
                                                 scale=1.0 if t == K_ else 0.125).then_inc(raw_done, 1)
                        act.wait_ge(v_added, j + 1)
                        exps(j, 0)
                        exps(j, 1)
                        for s in range(NS):
                            w = width(s)
                            act.wait_ge(turned0, at(j, s))
                            act.wait_ge(weighed, at(j, s - 1))
                            nc.scalar.activation(pT[:, 0:2, 0:w], cT[:, 0:2, 0:w], ACT.Copy).then_inc(copied0, 1)
                            if s:
                                store(j, s - 1)
                            if s + 2 < NS:
                                exps(j, s + 2)
                        store(j, NS - 1)

                @block.vector
                def _(dve):
                    def maxima(j, s):
                        w, i, g = width(s), s % 2, s % 2
                        dve.wait_ge(scored, at(j, s))
                        dve.wait_ge(exped, at(j, s - 2))
                        nc.vector.tensor_reduce(nmax[:, i, :], SC[i][:, :, 0:w], AX, ALU.max,
                                                negate=True).then_inc(max_step, 1)
                        dve.wait_ge(max_step, at(j, s))
                        nc.vector.tensor_tensor(nmax[:, i, :], nmax[:, i, :],
                                                sinks[:, 1, bass.ds(8 * (j - 1) + 4 * g, 4)],
                                                ALU.min).then_inc(maxed, 1)
                        dve.wait_ge(maxed, at(j, s))
                        dve.wait_ge(sunk_e, at(j, s - 2))
                        nc.vector.tensor_tensor(sinkx[:, i, :], nmax[:, i, :],
                                                sinks[:, 0, bass.ds(8 * (j - 1) + 4 * g, 4)],
                                                ALU.add).then_inc(sunk, 1)

                    nc.vector.memset(Kz[0][64:128, :], 0.0)
                    nc.vector.memset(Kz[1][0:64, :], 0.0)
                    with dve.Fori(1, 3) as j:
                        for t in range(5):
                            parts = [(Kz[0], 0, 64), (Kz[1], 64, 128)] if t == K_ else [(Q[t], 0, P)]
                            dve.wait_ge(raw_done, j * 5 + t + 1)
                            dve.wait_ge(scored, j * NS)
                            for dst, lo, hi in parts:
                                ins = nc.vector.tensor_tensor(dst[lo:hi, :], raw[lo:hi, :], rope[lo:hi, 0, :], ALU.mult)
                            ins.then_inc(rope_step, 1)
                            dve.wait_ge(swapped, j * 5 + t + 1)
                            dve.wait_ge(rope_step, j * 15 + 3 * t)
                            dve.wait_ge(o_turned, j * NS)
                            nc.vector.tensor_tensor(tmp[:, :], C, rope[:, 1, :], ALU.mult).then_inc(rope_step, 1)
                            dve.wait_ge(rope_step, j * 15 + 3 * t + 2)
                            for dst, lo, hi in parts:
                                ins = nc.vector.tensor_tensor(dst[lo:hi, :], dst[lo:hi, :], tmp[lo:hi, :], ALU.add)
                            ins.then_inc(rope_step, 1)
                        dve.wait_ge(product[V_], j + 1)
                        dve.wait_ge(vb_loaded, j * 16)
                        dve.wait_ge(weighed, j * NS)
                        nc.vector.tensor_tensor(vv, B.rearrange("p (n e) -> p n e", n=NB),
                                                vbias.unsqueeze(1).broadcast_to([P, NB, P]),
                                                ALU.add).then_inc(v_added, 1)
                        maxima(j, 0)
                        maxima(j, 1)
                        for s in range(NS):
                            w, i = width(s), s % 2
                            dve.wait_ge(exped, at(j, s))
                            dve.wait_ge(sunk_e, at(j, s))
                            nc.vector.tensor_tensor(psum_[:, i, :], psum_[:, i, :], sinkx[:, 2 + i, :],
                                                    ALU.add).then_inc(summed, 1)
                            dve.wait_ge(summed, at(j, s))
                            nc.vector.reciprocal(rsum[:, i, :], psum_[:, i, :]).then_inc(inverted, 1)
                            dve.wait_ge(turned1, at(j, s))
                            dve.wait_ge(weighed, at(j, s - 1))
                            nc.vector.tensor_copy(pT[:, 2:4, 0:w], cT[:, 2:4, 0:w]).then_inc(copied1, 1)
                            if s + 2 < NS:
                                maxima(j, s + 2)
                            dve.wait_ge(weighed, at(j, s))
                            dve.wait_ge(inverted, at(j, s))
                            dve.wait_ge(o_turned, at(j, s - 2))
                            nc.vector.tensor_tensor(osb[i].rearrange("p (r e) -> p r e", r=4),
                                                    pO[:, 0:256].rearrange("p (r e) -> p r e", r=4),
                                                    rsum[:, i, :].unsqueeze(2).broadcast_to([P, 4, 64]),
                                                    ALU.mult).then_inc(scaled, 1)

        cross_w_loaded = [sem(f"cross{l}_w_loaded", keep=True) for l in range(2)]

        def load_cross(sp, l):
            w_q = xattn_w_q[l].rearrange("(k p) n -> p k n", p=P)
            for h in range(XH):
                sp.dma_start(slot[h], w_q[:, :, h * P:(h + 1) * P]).then_inc(cross_w_loaded[l], 16)

        def cross_attention(l):
            name, NS = f"cross{l}", 2 * XH
            chunk = sem(name + "_q_chunk")
            q_ready = sem(name + "_q_ready")
            scored = sem(name + "_scores")
            maxed = sem(name + "_max")
            exped = sem(name + "_exp")
            inverted = sem(name + "_reciprocal")
            turned0 = sem(name + "_probT_psum_low")
            turned1 = sem(name + "_probT_psum_high")
            copied0 = sem(name + "_probT_low_copied")
            copied1 = sem(name + "_probT_high_copied")
            weighed = sem(name + "_pv")
            scaled = sem(name + "_o_scaled")
            o_turned = sem(name + "_oT_psum")
            o_stored = sem(name + "_oT_stored")
            qflat = qk[:, :, :].rearrange("p a n -> p (a n)")
            Q = [qflat[:, 512 * i:512 * (i + 1)] for i in range(4)]
            zeroed, cleared = sem(name + "_zero_rows_ready"), sem(name + "_rows_cleared")
            zero_rows = qk[:, 2, :]
            osb = [tmp[:, 0:512], tmp[:, 512:1024]]
            PR = [prob[:, 1024 * i:1024 * (i + 1)].rearrange("p (r w) -> p r w", r=4) for i in range(2)]
            SC = [t.rearrange("p (r w) -> p r w", r=4) for t in (A, B)]

            def wait(eng, s, n):
                if n > 0:
                    eng.wait_ge(s, n)

            with nc.Block() as block:
                @block.sync
                def _(sp):
                    load_out_matrix(xattn_w_o[l], 1 + 2 * l)(sp)
                    if l == 0:
                        sp.wait_ge(zeroed, 1)
                        for t in range(NE, NT_MAX):
                            sp.dma_start(y_dram[t * TS:(t + 1) * TS, :], zero_rows[0:TS, :]).then_inc(cleared, 16)
                        sp.wait_ge(cleared, 16 * XT)

                @block.gpsimd
                def _(pool):
                    if l == 0:
                        nc.gpsimd.memset(zero_rows, 0.0).then_inc(zeroed, 1)

                @block.tensor
                def _(pe):
                    def project_chunk(s):
                        wait(pe, o_stored, s - 3)
                        wait(pe, q_ready, s)
                        for k in range(KD):
                            ins = nc.tensor.matmul(pU[:, :], slot[s // 2][:, k, :],
                                                   hT[:, k, 512 * (s % 2):512 * (s % 2) + 512],
                                                   start=(k == 0), stop=(k == KD - 1))
                        ins.then_inc(chunk, 1)

                    def scores(s):
                        pe.wait_ge(q_ready, s + 1)
                        wait(pe, exped, s - 1)
                        for r in range(4):
                            ins = nc.tensor.matmul(SC[s % 2][:, r, :], Q[s % 4][:, r * P:(r + 1) * P],
                                                   memK[:, s // 2, :], start=True, stop=True)
                        ins.then_inc(scored, 1)

                    def turn(s):
                        pe.wait_ge(exped, s + 1)
                        for r in range(4):
                            if r % 2 == 0:
                                wait(pe, (copied0, copied1)[r // 2], s)
                            for b in range(MB):
                                ins = nc.tensor.transpose(C[:, (2 * r + b) * P:(2 * r + b + 1) * P],
                                                          PR[s % 2][:, r, b * P:(b + 1) * P], ident[:])
                            if r % 2:
                                ins.then_inc((turned0, turned1)[r // 2], 1)

                    def weigh(s):
                        wait(pe, scaled, s)
                        for r in range(4):
                            if r % 2 == 0:
                                pe.wait_ge((copied0, copied1)[r // 2], s + 1)
                            for b in range(MB):
                                ins = nc.tensor.matmul(pO[:, r * P:(r + 1) * P],
                                                       probT[:, (2 * r + b) * P:(2 * r + b + 1) * P],
                                                       memV[:, b, P * (s // 2):P * (s // 2) + P],
                                                       start=(b == 0), stop=(b == MB - 1))
                        ins.then_inc(weighed, 1)

                    def turn_out(s):
                        pe.wait_ge(scaled, s + 1)
                        wait(pe, o_stored, s)
                        wait(pe, q_ready, min(s + 4, NS))
                        for b in range(4):
                            ins = nc.tensor.transpose(pU[:, b * P:(b + 1) * P], osb[s % 2][:, b * P:(b + 1) * P],
                                                      ident[:])
                        ins.then_inc(o_turned, 1)

                    pe.wait_ge(cross_w_loaded[l], 64)
                    project_chunk(0)
                    project_chunk(1)
                    scores(0)
                    project_chunk(2)
                    scores(1)
                    for s in range(NS):
                        turn(s)
                        if s + 2 < NS:
                            scores(s + 2)
                        if s:
                            turn_out(s - 1)
                        weigh(s)
                        if s + 3 < NS:
                            project_chunk(s + 3)
                    turn_out(NS - 1)

                @block.scalar
                def _(act):
                    def keep_queries(s):
                        act.wait_ge(chunk, s + 1)
                        wait(act, scored, s - 3)
                        nc.scalar.activation(Q[s % 4], pU[:, :], ACT.Copy, scale=float(P) ** -0.5).then_inc(q_ready, 1)

                    def exps(s):
                        act.wait_ge(maxed, s + 1)
                        wait(act, turned1, s - 1)
                        wait(act, inverted, s - 1)
                        for r in range(4):
                            ins = nc.scalar.activation(PR[s % 2][:, r, :], SC[s % 2][:, r, :], ACT.Exp,
                                                       bias=nmax[:, s % 2, r:r + 1],
                                                       accum_out=psum_[:, s % 2, r:r + 1])
                        ins.then_inc(exped, 1)

                    def store(s):
                        act.wait_ge(o_turned, s + 1)
                        nc.scalar.activation(yT[:, s // 2, 512 * (s % 2):512 * (s % 2) + 512], pU[:, :],
                                             ACT.Copy).then_inc(o_stored, 1)

                    keep_queries(0)
                    keep_queries(1)
                    exps(0)
                    keep_queries(2)
                    exps(1)
                    for s in range(NS):
                        act.wait_ge(turned0, s + 1)
                        wait(act, weighed, s)
                        nc.scalar.activation(probT[:, 0:512], C[:, 0:512], ACT.Copy).then_inc(copied0, 1)
                        if s:
                            store(s - 1)
                        if s + 2 < NS:
                            exps(s + 2)
                        if s + 3 < NS:
                            keep_queries(s + 3)
                    store(NS - 1)

                @block.vector
                def _(dve):
                    def maxima(s):
                        dve.wait_ge(scored, s + 1)
                        wait(dve, exped, s - 1)
                        nc.vector.tensor_reduce(nmax[:, s % 2, :], SC[s % 2], AX, ALU.max,
                                                negate=True).then_inc(maxed, 1)

                    maxima(0)
                    maxima(1)
                    for s in range(NS):
                        dve.wait_ge(exped, s + 1)
                        nc.vector.reciprocal(rsum[:, s % 2, :], psum_[:, s % 2, :]).then_inc(inverted, 1)
                        dve.wait_ge(turned1, s + 1)
                        wait(dve, weighed, s)
                        nc.vector.tensor_copy(probT[:, 512:1024], C[:, 512:1024]).then_inc(copied1, 1)
                        if s + 2 < NS:
                            maxima(s + 2)
                        dve.wait_ge(weighed, s + 1)
                        dve.wait_ge(inverted, s + 1)
                        wait(dve, o_turned, s - 1)
                        nc.vector.tensor_tensor(osb[s % 2].rearrange("p (r e) -> p r e", r=4),
                                                pO[:, :].rearrange("p (r e) -> p r e", r=4),
                                                rsum[:, s % 2, :].unsqueeze(2).broadcast_to([P, 4, P]),
                                                ALU.mult).then_inc(scaled, 1)

        NL = NG + NE
        wr = W[:, 12288:12288 + KD * NL].rearrange("p (k n) -> p k n", k=KD)
        rb = W[:, 12288 + KD * NL:12288 + KD * NL + NG + NE]
        router_loaded = [sem(f"route{l}_loaded", keep=True) for l in range(2)]

        def load_router(sp, l):
            ld = router_loaded[l]
            sp.dma_start(wr[:, :, 0:NG], moe_w_group[l].rearrange("(k p) n -> p k n", p=P)).then_inc(ld, 16)
            sp.dma_start(wr[:, :, NG:NG + NE],
                         moe_w_router[l].rearrange("(k p) n -> p k n", p=P)).then_inc(ld, 16)
            sp.dma_start(rb[:, 0:NG], moe_b_group[l].partition_broadcast(P)).then_inc(ld, 16)
            sp.dma_start(rb[:, NG:NG + NE], moe_b_router[l].partition_broadcast(P)).then_inc(ld, 16)

        def router(l, w_gu, w_dn):
            n_ = f"route{l}"
            ld = router_loaded[l]
            lt, lk = sem(n_ + "_logitsT"), sem(n_ + "_logitsT_copied")
            lg = sem(n_ + "_logits")
            st = sem(n_ + "_step")
            ge1, ge2 = sem(n_ + "_group_exp"), sem(n_ + "_pair_exp")
            oh = sem(n_ + "_onehots")
            rk = sem(n_ + "_ranks")
            sl = sem(n_ + "_slot_onehots")
            sp_ = sem(n_ + "_slot_list")
            NP = 2 * NB
            at = [0]

            def room(*shape):
                n = math.prod(shape)
                v = yflat[:, at[0]:at[0] + n]
                at[0] += n
                if len(shape) == 2:
                    return v.rearrange("p (a b) -> p a b", a=shape[0])
                if len(shape) == 3:
                    return v.rearrange("p (a b c) -> p a b c", a=shape[0], b=shape[1])
                return v

            logT = prob[:, 0:S]
            lgt = room(NB, NG + NE)
            gmax, gsum, gmin = room(NB), room(NB), room(NB)
            gexp, geq, gcand, goh = (room(NB, NG) for _ in range(4))
            emask = room(NB, NE)
            top = room(2, NB)
            low = room(2, NB)
            eeq, ecand = room(NB, NE), room(NB, NE)
            oneh = room(2, NB, NE)
            both = room(NB, NE)
            pe2, w1 = room(NB), room(NB)
            cnt, nx, xe, base2 = room(NE), room(NE), room(NE), room(NE)
            over = room(NE, JT)
            rank = room(NB, NE)
            where, far = room(NB, NE), room(NB, NE)
            pos = room(2, NB)
            xcmp = room(XT, NE)
            xid = room(XT)
            half = room(XT // 2)
            wide = room(NP, NTT + 1)
            tile_oh = room(NP, NTT)
            tsum, rem = room(NP), room(NP)
            starts = room(NTT + 1)
            slot_oh = room(NP, TS)
            both_b = probT[:, 0:128].bitcast(BF16)
            assert at[0] <= KD * S
            R = pO
            with nc.Block() as block:
                @block.sync
                def _(sp):
                    load_expert(sp, l, 0, 0, w_gu, w_dn, lambda: None, lambda: None)

                @block.tensor
                def _(pe):
                    pe.wait_ge(ld, 64)
                    for k in range(KD):
                        for h in range(2):
                            ins = nc.tensor.matmul(A[64 * h:64 * h + NL, 512 * h:512 * h + 512], wr[:, k, :],
                                                   hT[:, k, 512 * h:512 * h + 512], start=(k == 0), stop=(k == KD - 1))
                    ins.then_inc(lt, 2)
                    for c in range(NB):
                        if c % 4 == 0:
                            pe.wait_ge(lk, c // 4 + 1)
                        ins = nc.tensor.transpose(R[:, c * NL:(c + 1) * NL], logT[0:NL, c * P:(c + 1) * P],
                                                  ident[0:NL, 0:NL])
                    ins.then_inc(lg, 1)
                    pe.wait_ge(oh, 1)
                    for c in range(NB + 1):
                        for b in range(min(c + 1, NB)):
                            ins = nc.tensor.matmul(pU[:, c * NE:(c + 1) * NE],
                                                   (tri_b if b == c else ones_b)[:],
                                                   both_b[:, b * NE:(b + 1) * NE],
                                                   start=(b == 0), stop=(b == min(c, NB - 1)))
                    ins.then_inc(rk, 1)
                    pe.wait_ge(sl, 1)
                    for i in range(NP):
                        ins = nc.tensor.matmul(A[0:TS, 0:NTT], slot_oh[:, i, :], tile_oh[:, i, :],
                                               start=(i == 0), stop=(i == NP - 1))
                    ins.then_inc(sp_, 1)

                @block.scalar
                def _(act):
                    for h in range(2):
                        act.wait_ge(lt, h + 1)
                        nc.scalar.activation(logT[0:NL, 512 * h:512 * h + 512], A[64 * h:64 * h + NL, 512 * h:512 * h + 512],
                                             ACT.Copy).then_inc(lk, 1)
                    act.wait_ge(ge1, 1)
                    nc.scalar.activation(gexp, gexp, ACT.Exp).then_inc(ge1, 1)
                    act.wait_ge(ge2, 1)
                    nc.scalar.activation(pe2, pe2, ACT.Exp).then_inc(ge2, 1)

                @block.vector
                def _(dve):
                    done = [0]

                    def then(ins):
                        done[0] += 1
                        ins.then_inc(st, 1)
                        dve.wait_ge(st, done[0])

                    def bc(ap, n):
                        return ap.unsqueeze(2).broadcast_to([P, ap.shape[1], n])

                    def iota_bc(n, m):
                        return iota[:, 0:m].unsqueeze(1).broadcast_to([P, n, m])

                    dve.wait_ge(lg, 1)
                    dve.wait_ge(ld, 64)
                    then(nc.vector.tensor_tensor(lgt, R[:, 0:NB * NL].rearrange("p (c n) -> p c n", c=NB),
                                                 rb.unsqueeze(1).broadcast_to([P, NB, 36]), ALU.add))
                    then(nc.vector.tensor_reduce(gmax, lgt[:, :, 0:NG], AX, ALU.max))
                    nc.vector.tensor_tensor(gexp, lgt[:, :, 0:NG], bc(gmax, NG), ALU.subtract).then_inc(ge1, 1)

                    def first_of_max(values, best, eq, cand, least, onehot, n):
                        then(nc.vector.tensor_tensor(eq, values, bc(best, n), ALU.is_equal))
                        then(nc.vector.scalar_tensor_tensor(cand, eq, -1000.0, iota_bc(NB, n), ALU.mult, ALU.add))
                        then(nc.vector.tensor_reduce(least, cand, AX, ALU.min))
                        then(nc.vector.tensor_tensor(onehot, cand, bc(least, n), ALU.is_equal))

                    first_of_max(lgt[:, :, 0:NG], gmax, geq, gcand, gmin, goh, NG)
                    ohx = goh.rearrange("p c g -> p (c g)").unsqueeze(2).broadcast_to([P, NB * NG, EPG])
                    eq8 = eeq.rearrange("p c (g e) -> p (c g) e", g=NG)
                    then(nc.vector.tensor_scalar(eq8, ohx, -NEG, NEG, ALU.mult, ALU.add))
                    nc.vector.tensor_copy(emask, lgt[:, :, NG:NG + NE]).then_inc(st, 1)
                    done[0] += 1
                    dve.wait_ge(st, done[0])
                    em8 = emask.rearrange("p c (g e) -> p (c g) e", g=NG)
                    then(nc.vector.tensor_tensor(em8, em8, ohx, ALU.mult))
                    then(nc.vector.tensor_tensor(emask, emask, eeq, ALU.add))
                    for i in range(2):
                        then(nc.vector.tensor_reduce(top[:, i, :], emask, AX, ALU.max))
                        first_of_max(emask, top[:, i, :], eeq, ecand, low[:, i, :], oneh[:, i], NE)
                        if i == 0:
                            then(nc.vector.scalar_tensor_tensor(emask, oneh[:, 0], 3.0 * NEG, emask,
                                                                ALU.mult, ALU.add))
                    then(nc.vector.tensor_tensor(both, oneh[:, 0], oneh[:, 1], ALU.add))
                    nc.vector.tensor_copy(both_b, both.rearrange("p c e -> p (c e)")).then_inc(oh, 1)
                    nc.vector.tensor_tensor(pe2, top[:, 1, :], top[:, 0, :], ALU.subtract).then_inc(ge2, 1)
                    dve.wait_ge(ge1, 2)
                    then(nc.vector.tensor_reduce(gsum, gexp, AX, ALU.add))
                    dve.wait_ge(ge2, 2)
                    then(nc.vector.tensor_scalar(w1, pe2, 1.0, None, ALU.add))
                    then(nc.vector.tensor_tensor(w1, w1, gsum, ALU.mult))
                    then(nc.vector.reciprocal(wgt[:, 0, :], w1))
                    then(nc.vector.tensor_tensor(wgt[:, 1, :], wgt[:, 0, :], pe2, ALU.mult))
                    dve.wait_ge(rk, 1)
                    nc.vector.tensor_copy(rank, pU[:, 0:NB * NE].rearrange("p (c e) -> p c e", c=NB))
                    then(nc.vector.tensor_copy(cnt, pU[:, NB * NE:(NB + 1) * NE]))
                    for t in range(JT):
                        ins = nc.vector.tensor_scalar(over[:, :, t], cnt, float((t + 1) * TS), None, ALU.is_gt)
                    then(ins)
                    then(nc.vector.tensor_reduce(nx, over, AX, ALU.add))
                    then(nc.vector.tensor_tensor_scan(xe, ones_b[:, 0:NE], nx, 0.0, ALU.mult, ALU.add))
                    then(nc.vector.tensor_tensor(base2, xe, nx, ALU.subtract))
                    then(nc.vector.tensor_scalar(base2, base2, float(NE - 1), float(TS), ALU.add, ALU.mult))
                    then(nc.vector.scalar_tensor_tensor(base2, iota[:, 0:NE], -float(TS), base2, ALU.mult, ALU.add))
                    then(nc.vector.tensor_scalar(half, iota[:, 0:XT // 2], 2.0, None, ALU.mult))
                    then(nc.vector.tensor_scalar(half, half, xe[:, NE - 1:NE], None, ALU.is_lt))
                    then(nc.vector.tensor_reduce(cnt[:, 0:1], half, AX, ALU.add))
                    then(nc.vector.tensor_scalar(nround[:], cnt[:, 0:1], float(NE // 2), None, ALU.add))
                    nc.vector.tensor_copy(tile_e[:, 0:NE], iota[:, 0:NE])
                    then(nc.vector.tensor_tensor(
                        xcmp, xe.unsqueeze(1).broadcast_to([P, XT, NE]),
                        iota[:, 0:XT].unsqueeze(2).broadcast_to([P, XT, NE]), ALU.is_le))
                    then(nc.vector.tensor_reduce(xid, xcmp, AX, ALU.add))
                    nc.vector.memset(tile_e[:, NT_MAX:NTT], 0)
                    then(nc.vector.tensor_scalar(tile_e[:, NE:NE + XT], xid, float(NE - 1), None, ALU.min))
                    then(nc.vector.tensor_scalar(far, rank, float(TS), None, ALU.is_ge))
                    then(nc.vector.tensor_tensor(far, far, base2.unsqueeze(1).broadcast_to([P, NB, NE]), ALU.mult))
                    then(nc.vector.tensor_tensor(where, rank, far, ALU.add))
                    then(nc.vector.scalar_tensor_tensor(where, iota_bc(NB, NE), float(TS), where,
                                                        ALU.mult, ALU.add))
                    for i in range(2):
                        then(nc.vector.tensor_tensor(far, where, oneh[:, i], ALU.mult))
                        then(nc.vector.tensor_reduce(pos[:, i, :], far, AX, ALU.add))
                    nc.vector.tensor_copy(pos_u[:, :, :], pos)
                    posf = pos.rearrange("p i c -> p (i c)")
                    then(nc.vector.tensor_scalar(starts, iota[:, 0:NTT + 1], float(TS), None, ALU.mult))
                    then(nc.vector.tensor_tensor(wide, bc(posf, NTT + 1),
                                                 starts.unsqueeze(1).broadcast_to([P, NP, NTT + 1]), ALU.is_ge))
                    then(nc.vector.tensor_reduce(tsum, wide, AX, ALU.add))
                    then(nc.vector.tensor_scalar(tsum, tsum, -1.0, -float(TS), ALU.add, ALU.mult))
                    then(nc.vector.tensor_tensor(rem, posf, tsum, ALU.add))
                    then(nc.vector.tensor_tensor(tile_oh, wide[:, :, 0:NTT], wide[:, :, 1:NTT + 1], ALU.subtract))
                    for i in range(2):
                        ti = tile_oh[:, i * NB:(i + 1) * NB, :]
                        ins = nc.vector.tensor_tensor(ti, ti, bc(tok_id[:, :], NTT), ALU.mult)
                    then(ins)
                    nc.vector.tensor_tensor(slot_oh, iota_bc(NP, TS), bc(rem, TS), ALU.is_equal).then_inc(sl, 1)
                    dve.wait_ge(sp_, 1)
                    nc.vector.tensor_copy(slots[0:TS, :], A[0:TS, 0:NTT]).then_inc(sl, 1)
                    dve.wait_ge(sl, 2)

        gu_set = [W[:, 0:8192].rearrange("p (k n) -> p k n", k=KD), hT]
        dn_set = [W[:, 8192:12288].rearrange("p (k n) -> p k n", k=4),
                  yflat[:, 4096:8192].rearrange("p (k n) -> p k n", k=4)]

        def load_expert(sp, l, e, s, s_gu, s_dn, before_gu, before_dn):
            wgu = moe_w_gate_up[l].rearrange("e (k p) f -> e p k f", p=P)
            wdn = moe_w_down[l].rearrange("e (k p) n -> e p k n", p=P)
            before_gu()
            for k in range(0, KD, 2):
                sp.dma_start(gu_set[s][:, k:k + 2, :],
                             wgu[bass.ds(e, 1), :, k:k + 2, :].rearrange("a p k f -> (a p) k f")
                             ).then_inc(s_gu[s], 16)
            before_dn()
            for k in range(0, 4, 2):
                sp.dma_start(dn_set[s][:, k:k + 2, :],
                             wdn[bass.ds(e, 1), :, k:k + 2, :].rearrange("a p k n -> (a p) k n")
                             ).then_inc(s_dn[s], 16)

        def experts(l, w_gu, w_dn):
            n_ = f"moe{l}"
            idx_ready = loop_sem(n_ + "_index", 2)
            gathered = [sem(n_ + f"_gathered{i}") for i in range(2)]
            x_turned = loop_sem(n_ + "_xT_psum", 4)
            x_ready = loop_sem(n_ + "_xT_ready", 4)
            gu_sum = loop_sem(n_ + "_gate_up", 8)
            silu_done = loop_sem(n_ + "_silu", 8)
            hid_done = loop_sem(n_ + "_hidden", 8)
            y_sum = loop_sem(n_ + "_y", 4)
            y0, y1 = loop_sem(n_ + "_y_low_copied", 2), loop_sem(n_ + "_y_high_copied", 2)
            stored = [loop_sem(n_ + f"_stored{i}", 16) for i in range(2)]
            passed = sem(n_ + "_passed")
            xg = [yflat[:, 0:1024], prob[:, 0:1024]]
            ysb = [yflat[:, 3072:4096], prob[:, 1024:2048]]
            xT = yflat[:, 1024:2048].rearrange("p (k n) -> p k n", k=KD)
            gate = yflat[:, 2048:2560].rearrange("p (f n) -> p f n", f=4)
            hid = yflat[:, 2560:3072].rearrange("p (f n) -> p f n", f=4)
            GU = [A[:, 0:512], A[:, 512:1024], B[:, 0:512], B[:, 512:1024]]
            Y = [C[:, 0:512], C[:, 512:1024]]
            T = [pO[:, :], pU[:, :]]

            def rounds(eng):
                return eng.value_load(nround[0:1, 0:1], min_val=NE // 2, max_val=NT_MAX // 2)

            with nc.Block() as block:
                @block.sync
                def _(sp):
                    give_credits(sp)

                    def load(v, s):
                        e = sp.value_load(tile_e[0:1, bass.ds(v - 2, 1)], min_val=0, max_val=NE - 1)
                        load_expert(sp, l, e, s, w_gu, w_dn,
                                    lambda: sp.wait_ge(gu_sum, (v - 1) * 4), lambda: sp.wait_ge(y_sum, (v - 1) * 2))

                    n = rounds(sp)
                    with sp.Fori(1, n) as r:
                        load(r * 2 + 1, 1)
                        load(r * 2 + 2, 0)
                    load(n * 2 + 1, 1)

                @block.gpsimd
                def _(pool):
                    def gather(at, i, register):
                        nc.gpsimd.tensor_copy(icol[0:TS, i:i + 1], slots[0:TS, bass.ds(at, 1)]).then_inc(idx_ready, 1)
                        pool.wait_ge(idx_ready, at + 3)
                        if register:
                            pool.sem_inc(passed, 1)
                        pool.indirect_dma_start(xg[i][0:TS, :], None, h_dram,
                                                bass.IndirectOffsetOnAxis(ap=icol[0:TS, i:i + 1], axis=0)
                                                ).then_inc(gathered[i], 16)

                    gather(0, 0, False)
                    gather(1, 1, False)
                    n = rounds(pool)
                    with pool.Fori(1, n + 1) as r:
                        for u in range(2):
                            v = r * 2 + u
                            pool.wait_ge(x_turned, (v + 1) * 2)
                            gather(v, u, True)
                    for u in range(2):
                        pool.wait_ge(gathered[u], n * 16 + 16)
                        pool.sem_inc(passed, 1)

                @block.tensor
                def _(pe):
                    def turn(i, count):
                        pe.wait_ge(gathered[i], count)
                        for h in range(2):
                            for b in range(4):
                                k = 4 * h + b
                                ins = nc.tensor.transpose(T[h][:, b * P:b * P + TS], xg[i][0:TS, k * P:(k + 1) * P],
                                                          ident[0:TS, 0:TS])
                            ins.then_inc(x_turned, 1)

                    turn(0, 16)
                    with pe.Fori(1, rounds(pe) + 1) as r:
                        for u in range(2):
                            v = r * 2 + u
                            pe.wait_ge(x_ready, (v + 1) * 2)
                            pe.wait_ge(hid_done, v * 4)
                            pe.wait_ge(w_gu[u], r * 64)
                            for f in range(4):
                                for i in range(2):
                                    for k in range(KD):
                                        c0 = i * EH + f * P
                                        ins = nc.tensor.matmul(GU[f][:, i * P:i * P + TS],
                                                               gu_set[u][:, k, c0:c0 + P], xT[:, k, 0:TS],
                                                               start=(k == 0), stop=(k == KD - 1))
                                ins.then_inc(gu_sum, 1)
                            turn(1 - u, (r + u) * 16)
                            pe.wait_ge(w_dn[u], r * 32)
                            pe.wait_ge(hid_done, v * 4 + 4)
                            for c in range(2):
                                pe.wait_ge((y0, y1)[c], v)
                                for f in range(4):
                                    ins = nc.tensor.matmul(Y[c][0:TS, :], hid[:, f, 0:TS],
                                                           dn_set[u][:, f, 512 * c:512 * c + 512],
                                                           start=(f == 0), stop=(f == 3))
                                ins.then_inc(y_sum, 1)

                @block.scalar
                def _(act):
                    n = rounds(act)
                    with act.Fori(1, n + 1) as r:
                        for u in range(2):
                            v = r * 2 + u
                            act.wait_ge(hid_done, v * 4)
                            for f in range(4):
                                act.wait_ge(gu_sum, v * 4 + f + 1)
                                nc.scalar.activation(gate[:, f, 0:TS], GU[f][:, 0:TS],
                                                     ACT.Silu).then_inc(silu_done, 1)
                            act.wait_ge(y_sum, v * 2 + 1)
                            act.wait_ge(stored[u], r * 16)
                            nc.scalar.activation(ysb[u][0:TS, 0:512], Y[0][0:TS, :], ACT.Copy).then_inc(y0, 1)
                            act.wait_ge(y0, v + 1)
                            act.wait_ge(y1, v + 1)
                            act.dma_start(y_dram[bass.ds((v - 2) * TS, TS), :], ysb[u][0:TS, :]
                                          ).then_inc(stored[u], 16)
                    for u in range(2):
                        act.wait_ge(stored[u], n * 16 + 16)
                        act.sem_inc(passed, 1)

                @block.vector
                def _(dve):
                    def keep(done):
                        for h in range(2):
                            dve.wait_ge(x_turned, done + h + 1)
                            g4 = gains[:, 3 + 3 * l, 4 * h:4 * h + 4].unsqueeze(2).broadcast_to([P, 4, TS])
                            nc.vector.tensor_tensor(
                                xT[:, 4 * h:4 * h + 4, 0:TS],
                                T[h].rearrange("p (k n) -> p k n", k=4)[:, :, 0:TS], g4,
                                ALU.mult).then_inc(x_ready, 1)

                    keep(4)
                    with dve.Fori(1, rounds(dve) + 1) as r:
                        for u in range(2):
                            v = r * 2 + u
                            dve.wait_ge(y_sum, v * 2)
                            for f in range(4):
                                dve.wait_ge(silu_done, v * 4 + f + 1)
                                nc.vector.tensor_tensor(hid[:, f, 0:TS], gate[:, f, 0:TS], GU[f][:, P:P + TS],
                                                        ALU.mult).then_inc(hid_done, 1)
                            dve.wait_ge(gu_sum, v * 4 + 4)
                            keep(v * 2 + 2)
                            dve.wait_ge(y_sum, v * 2 + 2)
                            dve.wait_ge(stored[u], r * 16)
                            nc.vector.tensor_copy(ysb[u][0:TS, 512:1024], Y[1][0:TS, :]).then_inc(y1, 1)

        def load_out_matrix(w, i):
            def go(sp):
                k = w.shape[0] // P
                sp.dma_start(w_out[:, 0:k, :], w.rearrange("(k p) n -> p k n", p=P)).then_inc(s_wo[i], 16)
            return go

        setup()
        end_phase()

        stream("memory", MB, memx, 0, "load", dst=memT)
        end_phase()

        def during_first_norm(sp):
            load_first_hybrid(sp)
            sp.dma_start(rope[:, :, :], rope_tables).then_inc(s_rope, 16)

        stream("in0", NB, xs, 1, "load", preload=during_first_norm, pe_side=memory_kv, act_tail=keep_memory_kv)
        end_phase()
        hybrid()
        end_phase()
        stream("mix0", NB, xs, 2, "project", kin=KD, w_ready=(s_wo[0], 32), preload=lambda sp: load_cross(sp, 0))
        end_phase()
        for l in range(2):
            if l == 1:
                window_attention()
                end_phase()
                stream("mix1", NB, xs, 5, "project", kin=KD, w_ready=(s_wo[2], 16), bias=swa_b_out[0],
                       preload=lambda sp: load_cross(sp, 1))
                end_phase()
            cross_attention(l)
            end_phase()
            stream(f"att{l}", NB, xs, 3 + 3 * l, "project", kin=4, w_ready=(s_wo[1 + 2 * l], 16), rows=True,
                   preload=lambda sp: load_router(sp, l))
            end_phase()
            expert_w = [[sem(f"moe{l}_{w}_loaded{i}", keep=True) for i in range(2)] for w in ("gate_up", "down")]
            router(l, *expert_w)
            end_phase()
            experts(l, *expert_w)
            end_phase()
            if l == 0:
                stream("moe0_in", NB, xs, 4, "combine", preload=load_first_window)
            else:
                stream("moe1_in", NB, xs, 6, "combine", final=True)
            end_phase()


_INS = ["x", "mem", "mem_norm", "mem_w_kv", "norm_mix", "norm_xattn", "norm_ffn", "hyb_w_in",
        "hyb_conv_w", "diff_lambda", "diff_subln", "hyb_w_out", "swa_w_qkv", "swa_b_qkv", "swa_sinks",
        "swa_w_out", "swa_b_out", "xattn_w_q", "xattn_w_o", "moe_w_group", "moe_b_group",
        "moe_w_router", "moe_b_router", "moe_w_gate_up", "moe_w_down", "final_norm"]


def shape_constants():
    import numpy as np
    f = np.float32
    inv = f(500000.0) ** (-np.arange(0, 16, 2, dtype=f) / f(16))
    ang = (np.arange(S, dtype=f)[:, None] * inv.astype(f)[None, :]).astype(f)
    cos, sin = np.cos(ang).T.astype(f), np.sin(ang).T.astype(f)
    rope = np.zeros((P, 2, S), f)
    rope[:, 0] = 1.0
    swap = np.zeros((P, P), f)
    for h in (0, 64):
        rope[h:h + 8, 0] = rope[h + 8:h + 16, 0] = cos
        rope[h:h + 8, 1], rope[h + 8:h + 16, 1] = -sin, sin
        for i in range(8):
            swap[h + i, h + 8 + i] = swap[h + 8 + i, h + i] = 1.0
    r = np.arange(P)
    c = np.zeros((P, C_ALL), f)
    c[:, C_ID:C_ID + P] = np.eye(P)
    c[:, C_R:C_R + P] = swap
    c[:, C_TRI:C_TRI + P] = r[:, None] < r[None, :]
    c[:, C_CAUSAL:C_CAUSAL + P] = np.where(r[None, :] > r[:, None], NEG, 0.0)
    c[:, C_PREV:C_PREV + P] = np.where(r[None, :] <= r[:, None], NEG, 0.0)
    c[:, C_IOTA:C_IOTA + P] = r[None, :]
    c[:, C_TOK:C_TOK + NB] = r[:, None] + P * np.arange(NB)[None, :]
    return rope, c


def small_vectors(a):
    import numpy as np
    by_p = [np.reshape(g, (KD, P)).T for g in (a["mem_norm"], a["norm_mix"][0], a["norm_xattn"][0],
                                               a["norm_ffn"][0], a["norm_mix"][1], a["norm_xattn"][1],
                                               a["norm_ffn"][1])]
    by_p.append(np.reshape(a["hyb_conv_w"][0], (3 * 4, P)).T)
    by_p.append(np.reshape(a["diff_subln"], (1, P)).T)
    b = a["swa_b_qkv"][0]
    by_p.append(np.transpose(np.reshape(b[0:1024], (2, 2, 4, 64)), (1, 3, 0, 2)).reshape(P, 8))
    by_p.append(np.reshape(b[1024:1280], (2, P)).T)
    rows = [np.reshape(a["diff_lambda"][0], (1, 256)), np.reshape(a["swa_sinks"][0], (1, 16)),
            np.reshape(b[1280:1536], (1, 256))]
    return np.ascontiguousarray(np.concatenate(by_p + [np.repeat(r, P, axis=0) for r in rows], axis=1))


def kernel(**inputs):
    import numpy as _np
    import concourse.bacc as _bacc
    from concourse.bass_utils import run_bass_kernel_spmd as _run

    nc = _bacc.Bacc("TRN2", target_bir_lowering=False, num_devices=1)
    arrays, args = {}, []
    given = [(name, _np.ascontiguousarray(inputs[name])) for name in _INS]
    given += list(zip(("rope_tables", "constants"), shape_constants()))
    given.append(("vectors", small_vectors(dict(given))))
    for name, a in given:
        arrays[f"in_{name}_dram"] = a
        args.append(nc.dram_tensor(f"in_{name}_dram", a.shape, mybir.dt.from_np(a.dtype),
                                   kind="ExternalInput").ap())
    args.append(nc.dram_tensor("out_dram", (1, S, D), F32, kind="ExternalOutput").ap())
    build(nc, *args)
    r = _run(nc, [arrays], core_ids=[0])
    return r.results[0]["out_dram"]
```
